# Optimizing a Trainium2 kernel written in Bass

```python
import math
import jax
import jax.numpy as jnp
from jax import lax
import numpy as np

D_MODEL = 1024
BATCH = 1
SEQ = 1024
DEPTH = 1

D_MIX = D_MODEL
HY_WIDTH = D_MIX // 4
LRU_WIDTH = D_MIX // 4
MLA_HEADS = 8
MLA_V_DIM = (D_MIX - HY_WIDTH - LRU_WIDTH) // MLA_HEADS
MLA_NOPE_DIM = MLA_V_DIM
MLA_ROPE_DIM = MLA_V_DIM // 2
MLA_KV_LORA = 4 * MLA_V_DIM
MLA_Q_LORA = 12 * MLA_V_DIM
ROPE_THETA = 10000.0
Q_BLOCK = 128
HY_ORDER = 2
HY_SHORT_CONV = 3
HY_POS_EMB = 33
HY_FILTER_FFN = 64
HY_FAST_DECAY = 0.3
HY_SLOW_DECAY = 1.5
HY_DECAY_TARGET = 1e-2
LRU_BLOCKS = 4
LRU_BLOCK_WIDTH = LRU_WIDTH // LRU_BLOCKS
LRU_CONV = 4
LRU_C = 8.0
N_EXPERTS = 16
EC_CAPACITY_FACTOR = 2
EXPERT_FF = D_MODEL
EPS = 1e-5
IN_SIZES = [(HY_ORDER + 1) * HY_WIDTH, LRU_WIDTH, LRU_WIDTH, MLA_Q_LORA, MLA_KV_LORA, MLA_ROPE_DIM]
N_IN = sum(IN_SIZES)
IN_SPLITS = [int(v) for v in np.cumsum(IN_SIZES)[:-1]]

kernel_name = "hybrid_hyena_rglru_mla_ecmoe_encoder"

F32 = jnp.float32

def _layer_norm(x, g, b):
    xf = x.astype(F32)
    xc = xf - jnp.mean(xf, axis=-1, keepdims=True)
    var = jnp.mean(xc * xc, axis=-1, keepdims=True)
    return (xc * lax.rsqrt(var + EPS) * g.astype(F32) + b.astype(F32)).astype(x.dtype)

def _rms_norm(x, g):
    xf = x.astype(F32)
    y = xf * lax.rsqrt(jnp.mean(xf * xf, axis=-1, keepdims=True) + EPS)
    return (y * g.astype(F32)).astype(x.dtype)

def _depthwise_conv(x, w, b, pad_left, pad_right):
    c = x.shape[-1]
    y = lax.conv_general_dilated(x, w[:, None, :].astype(x.dtype), window_strides=(1,),
                                 padding=[(pad_left, pad_right)],
                                 dimension_numbers=("NWC", "WIO", "NWC"),
                                 feature_group_count=c)
    return y + b.astype(x.dtype)

def _hyena_filters(length, w1, b1, f1, w2, b2, f2, w3):
    t = jnp.linspace(0.0, 1.0, length, dtype=F32)[:, None]
    bands = (HY_POS_EMB - 1) // 2
    t_idx = jnp.arange(length, dtype=F32)[:, None]
    freqs = jnp.linspace(1e-4, bands - 1, bands, dtype=F32)[None, :]
    ang = 2.0 * math.pi * t_idx * freqs / length
    z = jnp.concatenate([t, jnp.cos(ang), -jnp.sin(ang)], axis=-1)
    h = jnp.sin(f1.astype(F32) * (z @ w1.astype(F32) + b1.astype(F32)))
    h = jnp.sin(f2.astype(F32) * (h @ w2.astype(F32) + b2.astype(F32)))
    h = (h @ w3.astype(F32)).reshape(length, 2, HY_ORDER, HY_WIDTH)
    max_decay = math.log(HY_DECAY_TARGET) / HY_FAST_DECAY
    min_decay = math.log(HY_DECAY_TARGET) / HY_SLOW_DECAY
    deltas = jnp.abs(jnp.linspace(min_decay, max_decay, HY_WIDTH, dtype=F32))
    window = jnp.exp(-t * deltas[None, :])
    return h * window[:, None, None, :]

def _bidir_fftconv(u, h_fwd, h_bwd):
    length, c = h_fwd.shape
    k = jnp.concatenate([h_fwd, jnp.zeros((1, c), F32), h_bwd[1:][::-1]], axis=0)
    kf = jnp.fft.rfft(k, axis=0)
    uf = jnp.fft.rfft(u, n=2 * length, axis=1)
    return jnp.fft.irfft(uf * kf[None], n=2 * length, axis=1)[:, :length]

def _hyena_mixer(u, conv_w, conv_b, w1, b1, f1, w2, b2, f2, w3, skip):
    u = _depthwise_conv(u, conv_w, conv_b, HY_SHORT_CONV // 2, HY_SHORT_CONV // 2)
    x1, x2, v = jnp.split(u.astype(F32), HY_ORDER + 1, axis=-1)
    h = _hyena_filters(u.shape[1], w1, b1, f1, w2, b2, f2, w3)
    z = v
    for o, gate in enumerate((x1, x2)):
        z = gate * (_bidir_fftconv(z, h[:, 0, o], h[:, 1, o]) + skip[o].astype(F32) * z)
    return z.astype(u.dtype)

def _linear_combine(left, right):
    a_l, b_l = left
    a_r, b_r = right
    return a_l * a_r, a_r * b_l + b_r

def _rglru_mixer(xr, xg, conv_w, conv_b, wa, ba, wx, bx, lam):
    xr = _depthwise_conv(xr, conv_w, conv_b, LRU_CONV // 2, LRU_CONV - 1 - LRU_CONV // 2)
    bsz, seq, _ = xr.shape
    xf = xr.astype(F32)
    xb = xf.reshape(bsz, seq, LRU_BLOCKS, LRU_BLOCK_WIDTH)
    gate_a = jax.nn.sigmoid(jnp.einsum("bsnj,dnjk->dbsnk", xb, wa.astype(F32)).reshape(2, bsz, seq, LRU_WIDTH)
                            + ba.astype(F32)[:, None, None, :])
    gate_x = jax.nn.sigmoid(jnp.einsum("bsnj,dnjk->dbsnk", xb, wx.astype(F32)).reshape(2, bsz, seq, LRU_WIDTH)
                            + bx.astype(F32)[:, None, None, :])
    log_a = -LRU_C * gate_a * jax.nn.softplus(-lam.astype(F32))[:, None, None, :]
    a = jnp.exp(log_a)
    u = jnp.sqrt(-jnp.expm1(2.0 * log_a)) * gate_x * xf[None]
    _, h_fwd = lax.associative_scan(_linear_combine, (a[0], u[0]), axis=1)
    _, h_bwd = lax.associative_scan(_linear_combine, (a[1], u[1]), axis=1, reverse=True)
    return ((h_fwd + h_bwd) * jax.nn.gelu(xg.astype(F32))).astype(xr.dtype)

def _rope_tables(seq):
    inv = ROPE_THETA ** (-jnp.arange(0, MLA_ROPE_DIM, 2, dtype=F32) / MLA_ROPE_DIM)
    ang = jnp.arange(seq, dtype=F32)[:, None] * inv[None, :]
    return jnp.cos(ang), jnp.sin(ang)

def _apply_rope(x, cos, sin):
    xf = x.astype(F32)
    x1, x2 = jnp.split(xf, 2, axis=-1)
    return jnp.concatenate([x1 * cos - x2 * sin, x1 * sin + x2 * cos], axis=-1).astype(x.dtype)

def _mla_mixer(cq, ckv, k_rope, q_norm_g, w_uq, kv_norm_g, w_ukv, cos, sin):
    bsz, seq, _ = cq.shape
    q = (_rms_norm(cq, q_norm_g) @ w_uq).reshape(bsz, seq, MLA_HEADS, MLA_NOPE_DIM + MLA_ROPE_DIM)
    q_nope = q[..., :MLA_NOPE_DIM]
    q_rope = _apply_rope(q[..., MLA_NOPE_DIM:], cos[:, None, :], sin[:, None, :])
    kv = (_rms_norm(ckv, kv_norm_g) @ w_ukv).reshape(bsz, seq, MLA_HEADS, MLA_NOPE_DIM + MLA_V_DIM)
    k_nope = kv[..., :MLA_NOPE_DIM]
    v = kv[..., MLA_NOPE_DIM:]
    k_rope = _apply_rope(k_rope, cos, sin)
    nblk = seq // Q_BLOCK
    scale = (MLA_NOPE_DIM + MLA_ROPE_DIM) ** -0.5

    def to_blocks(t):
        return t.reshape(bsz, nblk, Q_BLOCK, MLA_HEADS, t.shape[-1]).transpose(1, 0, 2, 3, 4)

    def attend(blk):
        qn, qr = blk
        s = jnp.einsum("bqhd,bkhd->bhqk", qn, k_nope) + jnp.einsum("bqhr,bkr->bhqk", qr, k_rope)
        p = jax.nn.softmax(s.astype(F32) * scale, axis=-1).astype(v.dtype)
        return jnp.einsum("bhqk,bkhd->bqhd", p, v)

    o = lax.map(attend, (to_blocks(q_nope), to_blocks(q_rope)))
    return o.transpose(1, 0, 2, 3, 4).reshape(bsz, seq, MLA_HEADS * MLA_V_DIM)

def _expert_choice_moe(x, router_w, w_gate, w_up, w_down):
    bsz, seq, d = x.shape
    cap = max(1, EC_CAPACITY_FACTOR * seq // N_EXPERTS)
    affinity = jax.nn.softmax(jnp.einsum("bsd,de->bse", x, router_w).astype(F32), axis=-1)
    gate, idx = lax.top_k(jnp.swapaxes(affinity, 1, 2), cap)
    xe = jax.vmap(lambda xb, ib: xb[ib])(x, idx)
    hid = jax.nn.silu(jnp.einsum("becd,edf->becf", xe, w_gate)) * jnp.einsum("becd,edf->becf", xe, w_up)
    ye = jnp.einsum("becf,efd->becd", hid, w_down) * gate[..., None].astype(x.dtype)
    return jax.vmap(lambda ib, yb: jnp.zeros((seq, d), yb.dtype).at[ib.reshape(-1)].add(yb.reshape(-1, d)))(idx, ye)

def setup_inputs(seed: int = 0) -> dict:
    key = jax.random.key(seed)
    ks = iter(jax.random.split(key, 40))
    L = DEPTH
    beta = (8.0 * DEPTH) ** -0.25

    def nrm(shape, scale):
        return scale * jax.random.normal(next(ks), shape, F32)

    x = nrm((BATCH, SEQ, D_MODEL), 1.0)
    ln_in_g = 1.0 + nrm((D_MODEL,), 0.02)
    ln_in_b = nrm((D_MODEL,), 0.02)
    w_in = nrm((L, D_MODEL, N_IN), D_MODEL ** -0.5)
    hy_conv_w = nrm((L, HY_SHORT_CONV, (HY_ORDER + 1) * HY_WIDTH), HY_SHORT_CONV ** -0.5)
    hy_conv_b = nrm((L, (HY_ORDER + 1) * HY_WIDTH), 0.02)
    hy_ffn_w1 = nrm((L, HY_POS_EMB, HY_FILTER_FFN), HY_POS_EMB ** -0.5)
    hy_ffn_b1 = nrm((L, HY_FILTER_FFN), 0.02)
    hy_sin_f1 = 1.0 + nrm((L, HY_FILTER_FFN), 0.05)
    hy_ffn_w2 = nrm((L, HY_FILTER_FFN, HY_FILTER_FFN), HY_FILTER_FFN ** -0.5)
    hy_ffn_b2 = nrm((L, HY_FILTER_FFN), 0.02)
    hy_sin_f2 = 1.0 + nrm((L, HY_FILTER_FFN), 0.05)
    hy_ffn_w3 = nrm((L, HY_FILTER_FFN, 2 * HY_ORDER * HY_WIDTH), HY_FILTER_FFN ** -0.5)
    hy_skip = nrm((L, HY_ORDER, HY_WIDTH), 1.0)
    lru_conv_w = nrm((L, LRU_CONV, LRU_WIDTH), LRU_CONV ** -0.5)
    lru_conv_b = nrm((L, LRU_WIDTH), 0.02)
    lru_wa = nrm((L, 2, LRU_BLOCKS, LRU_BLOCK_WIDTH, LRU_BLOCK_WIDTH), LRU_BLOCK_WIDTH ** -0.5)
    lru_ba = nrm((L, 2, LRU_WIDTH), 0.02)
    lru_wx = nrm((L, 2, LRU_BLOCKS, LRU_BLOCK_WIDTH, LRU_BLOCK_WIDTH), LRU_BLOCK_WIDTH ** -0.5)
    lru_bx = nrm((L, 2, LRU_WIDTH), 0.02)
    a_c = jax.random.uniform(next(ks), (L, 2, LRU_WIDTH), F32, minval=0.9, maxval=0.999)
    a0 = a_c ** (1.0 / LRU_C)
    lru_lambda = jnp.log(a0) - jnp.log1p(-a0)
    mla_q_norm_g = 1.0 + nrm((L, MLA_Q_LORA), 0.02)
    mla_w_uq = nrm((L, MLA_Q_LORA, MLA_HEADS * (MLA_NOPE_DIM + MLA_ROPE_DIM)), MLA_Q_LORA ** -0.5)
    mla_kv_norm_g = 1.0 + nrm((L, MLA_KV_LORA), 0.02)
    mla_w_ukv = nrm((L, MLA_KV_LORA, MLA_HEADS * (MLA_NOPE_DIM + MLA_V_DIM)), MLA_KV_LORA ** -0.5)
    group_norm_g = 1.0 + nrm((L, D_MIX), 0.02)
    w_out = nrm((L, D_MIX, D_MODEL), beta * D_MIX ** -0.5)
    ln_mix_g = 1.0 + nrm((L, D_MODEL), 0.02)
    ln_mix_b = nrm((L, D_MODEL), 0.02)
    router_w = nrm((L, D_MODEL, N_EXPERTS), D_MODEL ** -0.5)
    exp_w_gate = nrm((L, N_EXPERTS, D_MODEL, EXPERT_FF), D_MODEL ** -0.5)
    exp_w_up = nrm((L, N_EXPERTS, D_MODEL, EXPERT_FF), D_MODEL ** -0.5)
    exp_w_down = nrm((L, N_EXPERTS, EXPERT_FF, D_MODEL), beta * EXPERT_FF ** -0.5)
    ln_ffn_g = 1.0 + nrm((L, D_MODEL), 0.02)
    ln_ffn_b = nrm((L, D_MODEL), 0.02)
    return {"x": x, "ln_in_g": ln_in_g, "ln_in_b": ln_in_b, "w_in": w_in,
            "hy_conv_w": hy_conv_w, "hy_conv_b": hy_conv_b, "hy_ffn_w1": hy_ffn_w1, "hy_ffn_b1": hy_ffn_b1,
            "hy_sin_f1": hy_sin_f1, "hy_ffn_w2": hy_ffn_w2, "hy_ffn_b2": hy_ffn_b2, "hy_sin_f2": hy_sin_f2,
            "hy_ffn_w3": hy_ffn_w3, "hy_skip": hy_skip, "lru_conv_w": lru_conv_w, "lru_conv_b": lru_conv_b,
            "lru_wa": lru_wa, "lru_ba": lru_ba, "lru_wx": lru_wx, "lru_bx": lru_bx, "lru_lambda": lru_lambda,
            "mla_q_norm_g": mla_q_norm_g, "mla_w_uq": mla_w_uq, "mla_kv_norm_g": mla_kv_norm_g,
            "mla_w_ukv": mla_w_ukv, "group_norm_g": group_norm_g, "w_out": w_out,
            "ln_mix_g": ln_mix_g, "ln_mix_b": ln_mix_b, "router_w": router_w, "exp_w_gate": exp_w_gate,
            "exp_w_up": exp_w_up, "exp_w_down": exp_w_down, "ln_ffn_g": ln_ffn_g, "ln_ffn_b": ln_ffn_b}

def reference(x, ln_in_g, ln_in_b, w_in, hy_conv_w, hy_conv_b, hy_ffn_w1, hy_ffn_b1, hy_sin_f1,
              hy_ffn_w2, hy_ffn_b2, hy_sin_f2, hy_ffn_w3, hy_skip, lru_conv_w, lru_conv_b, lru_wa, lru_ba,
              lru_wx, lru_bx, lru_lambda, mla_q_norm_g, mla_w_uq, mla_kv_norm_g, mla_w_ukv, group_norm_g,
              w_out, ln_mix_g, ln_mix_b, router_w, exp_w_gate, exp_w_up, exp_w_down, ln_ffn_g, ln_ffn_b):
    alpha = (2.0 * DEPTH) ** 0.25
    cos, sin = _rope_tables(x.shape[1])
    x = _layer_norm(x, ln_in_g, ln_in_b)
    g0, g1 = HY_WIDTH, HY_WIDTH + LRU_WIDTH
    for l in range(DEPTH):
        proj = x @ w_in[l]
        p_hy, p_lr, p_lg, p_cq, p_ckv, p_kr = jnp.split(proj, IN_SPLITS, axis=-1)
        y_hy = _hyena_mixer(p_hy, hy_conv_w[l], hy_conv_b[l], hy_ffn_w1[l], hy_ffn_b1[l], hy_sin_f1[l],
                            hy_ffn_w2[l], hy_ffn_b2[l], hy_sin_f2[l], hy_ffn_w3[l], hy_skip[l])
        y_lr = _rglru_mixer(p_lr, p_lg, lru_conv_w[l], lru_conv_b[l], lru_wa[l], lru_ba[l],
                            lru_wx[l], lru_bx[l], lru_lambda[l])
        y_at = _mla_mixer(p_cq, p_ckv, p_kr, mla_q_norm_g[l], mla_w_uq[l], mla_kv_norm_g[l],
                          mla_w_ukv[l], cos, sin)
        gn = group_norm_g[l]
        y = jnp.concatenate([_rms_norm(y_hy, gn[:g0]), _rms_norm(y_lr, gn[g0:g1]),
                             _rms_norm(y_at, gn[g1:])], axis=-1)
        x = _layer_norm(alpha * x + y @ w_out[l], ln_mix_g[l], ln_mix_b[l])
        moe = _expert_choice_moe(x, router_w[l], exp_w_gate[l], exp_w_up[l], exp_w_down[l])
        x = _layer_norm(alpha * x + moe, ln_ffn_g[l], ln_ffn_b[l])
    return x


_drawn_inputs = setup_inputs


def setup_inputs(seed=0):
    import zlib

    import numpy as np

    out = dict(_drawn_inputs(seed))
    spreads = {}
    factors = {'hy_ffn_b1': 4.362,
     'hy_sin_f1': 4.071,
     'hy_ffn_b2': 3.486,
     'hy_sin_f2': 3.673,
     'lru_ba': 8.0,
     'lru_bx': 8.0,
     'mla_q_norm_g': 7.756,
     'mla_kv_norm_g': 4.658,
     'group_norm_g': 5.578,
     'ln_mix_g': 2.9,
     'ln_mix_b': 2.7,
     'ln_ffn_g': 2.833,
     'ln_ffn_b': 2.852}
    for name, (base, spread) in spreads.items():
        noise = np.random.default_rng([zlib.crc32(name.encode()), seed]).standard_normal(out[name].shape)
        drawn = base * np.exp(spread * noise) if base else spread * noise
        out[name] = jnp.asarray(drawn.astype(out[name].dtype))
    for name, factor in factors.items():
        out[name] = (out[name] * factor).astype(out[name].dtype)
    return out
```

```python
import numpy as np
import concourse.bass as bass
from concourse import mybir
from contextlib import ExitStack

F32 = mybir.dt.float32
U32 = mybir.dt.uint32
ALU = mybir.AluOpType
ACT = mybir.ActivationFunctionType
AX = mybir.AxisListType

P = 128
D = 1024
T = 1024
KT = D // P
TT = T // P
HALF = 512
HYW = D // 4
LRW = D // 4
NH, DV, DR = 8, 64, 32
DQ = DV + DR
QL, KVL = 12 * DV, 4 * DV
FFN, POS = 64, 33
NE, CAP = 16, 2 * T // 16
NIN = 3 * HYW + 2 * LRW + QL + KVL + DR
EPS = 1e-5
ALPHA = 2.0 ** 0.25
SCALE = float(DQ) ** -0.5
LRU_C = 8.0
MAGIC = 1.5 * 2.0 ** 23
TWO_PI_HI = 6.28125
TWO_PI_LO = 2.0 * np.pi - 6.28125
PI_IN = 3.1415925

C_HYW, C_HYB, C_LRW, C_LRB = 0, 18, 24, 32
C_BA, C_BX, C_LAM, C_QG, C_KVG = 34, 38, 42, 46, 52
C_GN, C_LG, C_LB, N_PAR = 54, 62, 70, 78


def shape_constants():
    f32 = np.float32
    tab = np.zeros((P, 352), f32)
    tab[:, 0:128] = np.eye(P)
    tab[:, 128:256] = 1.0
    for i in range(DR // 2):
        tab[DV + DR // 2 + i, 256 + DV + i] = 1.0
        tab[DV + i, 256 + DV + DR // 2 + i] = 1.0
    order = np.concatenate([np.arange(0, T, 2), np.arange(1, T, 2)])
    t = np.linspace(0.0, 1.0, T, dtype=f32)[:, None]
    bands = (POS - 1) // 2
    freqs = np.linspace(1e-4, bands - 1, bands, dtype=f32)[None, :]
    ang = (f32(2.0 * np.pi) * np.arange(T, dtype=f32)[:, None] * freqs / f32(T)).astype(f32)
    a64 = ang.astype(np.float64)
    z = np.concatenate([t, np.cos(a64), -np.sin(a64)], axis=-1).astype(f32)
    lo, hi = np.log(1e-2) / 1.5, np.log(1e-2) / 0.3
    deltas = np.abs(np.linspace(lo, hi, HYW, dtype=f32))
    window = np.exp((-t * deltas[None, :]).astype(np.float64)).astype(f32)
    j = np.arange(HALF)
    w = np.pi * (2 * j + 1) / (2.0 * T)
    fall = np.concatenate([w, np.pi - w])
    n = order[:, None]
    tau = (np.arange(HALF) + 0.5)[:, None]
    inv = 1.0 / T
    rope = 10000.0 ** (-np.arange(0, DR, 2, dtype=f32) / f32(DR))
    rang = (np.arange(T, dtype=f32)[:, None] * rope.astype(f32)[None, :]).astype(np.float64).T
    out = {
        "c_tab": tab, "c_pos": z[order].T, "c_win": window[order],
        "c_fc": np.cos(n * w), "c_fs": np.sin(n * w),
        "c_dc": np.cos(tau * fall), "c_ds": np.sin(tau * fall),
        "c_ic": (np.cos(tau * fall) * inv).T, "c_is": (np.sin(tau * fall) * inv).T,
        "c_cos": np.concatenate([np.cos(rang), np.cos(rang)]),
        "c_sin": np.concatenate([-np.sin(rang), np.sin(rang)]),
    }
    return {k: np.ascontiguousarray(v, dtype=f32) for k, v in out.items()}


def encoder(nc, A, out):
    ctx = ExitStack()
    with ctx:
        def sem(name):
            return ctx.enter_context(nc.semaphore(name))

        WORDS = 53200
        arena = ctx.enter_context(nc.sbuf_tensor("arena", [P, WORDS], F32))
        psum = ctx.enter_context(nc.psum_tensor("psum", [P, 8 * HALF], F32))

        def mem(at, *dims, p0=0, p1=P):
            n = int(np.prod(dims))
            assert at + n <= WORDS
            v = arena[p0:p1, at:at + n]
            if len(dims) == 2:
                v = v.rearrange("p (a b) -> p a b", a=dims[0])
            elif len(dims) == 3:
                v = v.rearrange("p (a b c) -> p a b c", a=dims[0], b=dims[1])
            elif len(dims) == 4:
                v = v.rearrange("p (a b c d) -> p a b c d", a=dims[0], b=dims[1], c=dims[2])
            return v

        def bank(b, n=1, p0=0, p1=P):
            return psum[p0:p1, HALF * b:HALF * (b + n)]

        def dram(name, shape):
            return nc.dram_tensor(name, shape, F32, kind="Internal").ap()

        xhat_dram = dram("xhat_scratch", [T, D])
        x1_dram = dram("x1_scratch", [T, D])
        acc_dram = dram("acc_scratch", [T, D])

        ident, ones, rot = mem(0, 128), mem(128, 128), mem(256, 96, p1=DQ)
        par = mem(352, 80)
        w1, w2 = mem(432, FFN, p1=POS), mem(496, FFN, p1=FFN)
        fpar = mem(560, 4, p1=FFN)
        eps, idle = mem(564, 1), mem(596, 2)
        sp8 = mem(566, 4)
        nsp8 = mem(570, 4)
        spt = mem(574, 5, 4)
        st = mem(600, 2, 12)
        mv = mem(624, 2, 2)
        sd = mem(628, 2)
        rstd = mem(630, 2)
        hss = mem(632, 8)
        hsd = mem(640, 8)
        hrs = mem(648, 8)
        mx, nm, rsum, rinv = mem(656, 2), mem(658, 2), mem(660, 4), mem(664, 2)
        ass, asd, ars = mem(666, 8), mem(674, 8), mem(682, 8)
        rmx, rsm, rri = mem(690, 2), mem(692, 2), mem(694, 2)
        aff = mem(696, 2, NE)
        idxf_t, gate_t = mem(728, NE), mem(744, NE)
        idx_t = mem(760, NE).bitcast(U32)
        idx_e = mem(776, 2).bitcast(U32)
        gate_e = mem(778, 2)
        prow = mem(784, 128, p1=N_PAR)
        frow = mem(912, FFN, p1=4)

        kf = mem(976, 2, 8, 2, HYW)
        xT = mem(9168, KT, T)
        fc, fs = mem(17360, 8, HALF), mem(21456, 8, HALF)
        hf = mem(25552, 8, 2, HALF)
        pos_t, w3 = mem(39888, T, p1=POS), mem(40912, 1024, p1=FFN)
        h1, h2 = mem(41936, T, p1=FFN), mem(42960, T, p1=FFN)
        win = mem(43984, 8, HYW)
        xr_in = mem(46032, 3, D)
        hw = mem(49104, 2, 1024)
        fodd = mem(51152, 2, HALF)
        warg, turns = mem(52176, T, p1=FFN), mem(24528, T, p1=FFN)
        win_w = mem(33744, 3, KT, 256)
        u_hy = mem(39888, 6, T)
        g_hy = mem(46032, 3, 4, 2, HYW)
        dc, ds_ = mem(17360, 4, T), mem(21456, 4, T)
        ic, is_ = mem(25552, 8, HALF), mem(29648, 8, HALF)
        pm = mem(39888, 2, 4, HYW)
        zbuf = mem(41936, 4, 2, HYW)
        yf = mem(43984, 2, HALF)
        t1, t2 = mem(45008, HALF), mem(45520, HALF)
        odd = t1[:, 0:HYW]
        skipb = mem(52176, 2, HYW)
        tsk = mem(37840, 4, 2, HYW)
        xr, gelu = mem(976, 2, T), mem(3024, 2, T)
        rb, rb_lru = mem(5072, T), mem(8144, T)
        cos_t, sin_t = mem(6096, T), mem(7120, T)
        hs = mem(17360, 2, T)
        la, lx, lt = mem(19408, 2, T), mem(21456, 2, T), mem(23504, 2, T)
        ld = mem(25552, T)
        lruw = mem(52176, 8, 128)
        wuq = mem(26576, 6, NH * DQ)
        wukv = mem(31184, 2, 1024)
        cq, ckv = mem(39888, 6, T), mem(46032, 2, T)
        kr = mem(48080, T, p1=DQ)
        sq = mem(49104, T)
        yT_hy = mem(50128, 2, T)
        yT_lru = hs
        v_at, o_at = mem(9168, TT, NH * DV), mem(13264, TT, NH * DV)
        qh, kh = mem(33744, 2, T), mem(35792, 2, T)
        rtmp, rtmp2 = mem(37840, T), mem(25552, T)
        p_at, pT = mem(19408, 2, T), mem(21456, 2, T)
        yT_at = mem(23504, 4, T)
        wout = mem(976, KT, D)
        gin, bin_ = mem(9168, D), mem(10192, D)
        gmix, bmix = mem(11216, D), mem(12240, D)
        xres, x1t = mem(19408, 2, D), mem(21456, 2, D)
        x1T = [mem(27600, D), mem(52176, D)]
        rw = mem(16848, KT, NE)
        accb = mem(13264, 2, D)
        affT = mem(15312, T, p1=NE)

        WC = 12
        wring = mem(28624, WC, 4, HALF)
        xe, xeT = mem(976, 2, D), mem(3024, KT, CAP)
        sil, hid, hidT, ye = mem(5072, 2, HALF), mem(6096, D), mem(7120, KT, CAP), mem(8144, 2, D)
        vals, idxs, idxf = mem(10192, CAP, p1=NE), mem(10320, CAP, p1=NE).bitcast(U32), mem(10448, CAP, p1=NE)
        gff, bff = mem(11216, D), mem(12240, D)
        fin = mem(13264, 3, D)
        fst, fmv, fsd, frs = mem(16336, 2, 12), mem(16360, 2, 2), mem(16364, 2), mem(16366, 2)


        s_par, s_wint, s_fmat = sem("params_ld"), sem("window_ld"), sem("filter_mats_ld")
        s_x = [sem(f"x_ld{i}") for i in range(3)]
        s_eps, s_parT, s_parc = sem("eps_set"), sem("params_turned"), sem("params_copied")
        s_fmm, s_arg, s_sin, s_f3 = sem("ffn_psum"), sem("sine_arg"), sem("sine_done"), sem("filter_psum")
        s_hw, s_hab = sem("filter_windowed"), sem("filter_folded")
        s_st, s_sd, s_xn, s_xst, s_xp, s_xT = sem("in_stats"), sem("in_root"), sem("in_normed"), sem("xhat_stored"), sem("x_turned"), sem("xT_done")
        s_dft, s_fodd, s_kf = sem("filter_sums_psum"), sem("filter_odd_copied"), sem("spectra_done")
        s_w = [sem(f"w_in_ld{i}") for i in range(3)]
        s_pj, s_pja, s_pjv = sem("proj_psum"), sem("proj_read_act"), sem("proj_read_dve")
        s_ut, s_uta, s_utv = sem("hyena_turned"), sem("hyena_copied_act"), sem("hyena_copied_dve")
        s_dmat = sem("dft_ld")
        s_fold, s_uf, s_yf, s_yfu = sem("folded"), sem("spectrum_psum"), sem("product_done"), sem("product_used")
        s_inv, s_od, s_z = sem("inverse_psum"), sem("odd_copied"), sem("z_done")
        s_hsd, s_hyn, s_hyT, s_hyc = sem("hyena_root"), sem("hyena_normed"), sem("hyena_back_psum"), sem("hyena_out")
        s_zero, s_lw, s_spa, s_spv = sem("zeroed"), sem("lru_w_ld"), sem("softplus_exp"), sem("softplus_done")
        s_gmm, s_gact, s_lact, s_lv, s_hsg = sem("gates_psum"), sem("gates_read"), sem("lru_act"), sem("lru_dve"), sem("lru_gated")
        s_sq, s_ssq, s_rsd, s_rb = sem("squares"), sem("squares_summed"), sem("rms_root"), sem("rms_applied")
        s_mw, s_rope, s_krm, s_kro = sem("mla_w_ld"), sem("rope_ld"), sem("kr_partner_psum"), sem("kr_roped")
        s_vmm, s_va, s_vv = sem("v_psum"), sem("v_copied_act"), sem("v_copied_dve")
        s_hp, s_hpa, s_hpv = sem("head_proj_psum"), sem("head_proj_act"), sem("head_proj_dve")
        s_qk, s_nm, s_exp, s_tr = sem("scores_psum"), sem("neg_max"), sem("exp_done"), sem("probs_turned")
        s_pta, s_ptv, s_pv, s_ov = sem("probsT_act"), sem("probsT_dve"), sem("pv_psum"), sem("o_done")
        s_osd, s_on, s_oT, s_oc = sem("o_root"), sem("o_normed"), sem("o_turned"), sem("yT_at_done")
        s_wo, s_gb, s_rw, s_gff = sem("w_out_ld"), sem("gains_ld"), sem("router_w_ld"), sem("ffn_gains_ld")
        s_xh = [sem(f"xhat_ld{i}") for i in range(2)]
        s_res, s_mix, s_mixu, s_mst, s_msd, s_mn, s_x1 = sem("residual"), sem("mix_psum"), sem("mix_read"), sem("mix_stats"), sem("mix_root"), sem("mix_normed"), sem("x1_done")
        s_x1st, s_acst, s_acc = [sem(f"x1_stored{i}") for i in range(2)], [sem(f"acc_stored{i}") for i in range(2)], sem("acc_scaled")
        s_x1p, s_x1ta, s_x1tv, s_lg = sem("x1_turned"), sem("x1T_act"), sem("x1T_dve"), sem("logits")
        s_rm, s_re, s_aff, s_afT, s_afc = sem("router_max"), sem("router_exp"), sem("affinity"), sem("affinity_turned"), sem("affinityT")
        s_topk, s_idxp, s_idxc = sem("topk_done"), sem("idx_turned"), sem("idx_ready")
        s_wc, s_wcu = [sem(f"expert_w_ld{c}") for c in range(WC)], sem("expert_w_used")
        s_ie, s_xe = sem("expert_idx"), [sem(f"xe_gathered{i}") for i in range(2)]
        s_xep, s_xea, s_xev = sem("xe_turned"), sem("xeT_act"), sem("xeT_dve")
        s_sil, s_hid = sem("silu_done"), sem("hidden_done")
        s_ht, s_hta, s_htv = sem("hid_turned"), sem("hidT_act"), sem("hidT_dve")
        s_yea, s_yev, s_sc = sem("ye_act"), sem("ye_dve"), sem("scattered")
        s_fx, s_out = [sem(f"final_ld{i}") for i in range(3)], [sem(f"out_stored{i}") for i in range(3)]
        s_fst, s_fsd, s_fn, s_fo = sem("final_stats"), sem("final_root"), sem("final_normed"), sem("final_done")
        s_dve, s_act, s_pool = sem("dve_chain"), sem("act_chain"), sem("pool_chain")

        def links(eng, chain):
            count = [0]

            def link(ins):
                count[0] += 1
                ins.then_inc(chain, 1)
                eng.wait_ge(chain, count[0])
            return link

        def tokens(ap):
            return ap.rearrange("(t p) d -> p t d", p=P)

        def rows(ap):
            return ap.rearrange("(k p) n -> p k n", p=P)

        def flat(ap3):
            return ap3.rearrange("p a b -> p (a b)")

        def reverse(m, a, b):
            return u_hy[:, m, T - 1 - a:T - 1 - b:-1]

        w_in = rows(A["w_in"][0])
        x_tok, xh_tok, x1_tok, acc_tok = tokens(A["x"][0]), tokens(xhat_dram), tokens(x1_dram), tokens(acc_dram)
        out_tok = tokens(out[0])

        LR0, CQ0, KV0, KR0 = 3 * HYW, 3 * HYW + 2 * LRW, 3 * HYW + 2 * LRW + QL, 3 * HYW + 2 * LRW + QL + KVL
        PROJ = ([(P * m, P) for m in range(10)] + [(KV0 + P * m, P) for m in range(2)] + [(KR0, DR)]
                + [(CQ0 + P * m, P) for m in range(6)])
        N_HY, I_LR, I_LG, I_KV, I_KR, I_CQ = 6, 6, 8, 10, 12, 13
        CHUNKS = [(256 * c, 256) for c in range(5)] + [(KV0, 256), (KR0, DR)] + [(CQ0 + 256 * c, 256) for c in range(3)]
        LAST = [1, 3, 5, 7, 9, 11, 12, 14, 16, 18]

        def chunk_of(i):
            return min(c for c in range(len(CHUNKS)) if LAST[c] >= i)

        def proj_bank(i):
            return 2 * (i % 2) if i < N_HY else 6 if i < I_LG else 4 + 2 * (i % 2)

        def proj_before(i):
            return max([j for j in range(i) if proj_bank(j) == proj_bank(i)], default=None)

        def dve_reads(i):
            return sum(j not in (I_LG, I_LG + 1, I_KR) for j in range(i + 1))

        def act_read(i):
            if i in (I_KV, I_KV + 1):
                return s_sq, i - I_KV + 1
            return (s_sq, i - I_CQ + 3) if i >= I_CQ else (s_pja, min(i, I_KV) + 1)

        block = ctx.enter_context(nc.Block())

        @block.sync
        def _(sp):
            sp.dma_start(mem(0, 352), A["c_tab"]).then_inc(s_par, 16)
            for at, src in ((C_HYW, A["hy_conv_w"][0].rearrange("k (m p) -> (k m) p", p=P)),
                            (C_HYB, A["hy_conv_b"][0].rearrange("(m p) -> m p", p=P)),
                            (C_LRW, A["lru_conv_w"][0].rearrange("k (m p) -> (k m) p", p=P)),
                            (C_LRB, A["lru_conv_b"][0].rearrange("(m p) -> m p", p=P)),
                            (C_BA, A["lru_ba"][0].rearrange("k (m p) -> (k m) p", p=P)),
                            (C_BX, A["lru_bx"][0].rearrange("k (m p) -> (k m) p", p=P)),
                            (C_LAM, A["lru_lambda"][0].rearrange("k (m p) -> (k m) p", p=P)),
                            (C_QG, A["mla_q_norm_g"][0].rearrange("(m p) -> m p", p=P)),
                            (C_KVG, A["mla_kv_norm_g"][0].rearrange("(m p) -> m p", p=P)),
                            (C_GN, A["group_norm_g"][0].rearrange("(m p) -> m p", p=P)),
                            (C_LG, A["ln_in_g"].rearrange("(m p) -> m p", p=P)),
                            (C_LB, A["ln_in_b"].rearrange("(m p) -> m p", p=P))):
                sp.dma_start(prow[at:at + src.shape[0], :], src).then_inc(s_par, 16)
            for i, name in enumerate(("hy_ffn_b1", "hy_sin_f1", "hy_ffn_b2", "hy_sin_f2")):
                sp.dma_start(frow[i:i + 1, :], A[name]).then_inc(s_par, 16)
            sp.dma_start(pos_t, A["c_pos"]).then_inc(s_par, 16)
            sp.dma_start(w1, A["hy_ffn_w1"][0]).then_inc(s_par, 16)
            sp.dma_start(w2, A["hy_ffn_w2"][0]).then_inc(s_par, 16)
            sp.dma_start(w3, A["hy_ffn_w3"][0]).then_inc(s_par, 16)
            for i in range(3):
                sp.dma_start(xr_in[:, i, :], x_tok[:, i, :]).then_inc(s_x[i], 16)
            sp.dma_start(win, rows(A["c_win"])).then_inc(s_wint, 16)
            for i in range(TT):
                sp.wait_ge(s_xn, i + 1)
                sp.dma_start(xh_tok[:, i, :], xr_in[:, i % 3, :]).then_inc(s_xst, 16)
                if i + 3 < TT:
                    sp.wait_ge(s_xst, 16 * (i + 1))
                    sp.wait_ge(s_xp, i + 1)
                    sp.dma_start(xr_in[:, i % 3, :], x_tok[:, i + 3, :]).then_inc(s_x[i % 3], 16)
                if i == 1:
                    sp.dma_start(fc, rows(A["c_fc"])).then_inc(s_fmat, 16)
                    sp.dma_start(fs, rows(A["c_fs"])).then_inc(s_fmat, 16)

            def load_w(c):
                c0, w = CHUNKS[c]
                if c >= 3:
                    sp.wait_ge(s_pj, LAST[c - 3] + 1)
                sp.dma_start(win_w[:, c % 3, :, 0:w], w_in[:, :, c0:c0 + w]).then_inc(s_w[c % 3], 16)

            for c in range(3):
                load_w(c)
            sp.wait_ge(s_dft, 4)
            for dst, name in ((dc, "c_dc"), (ds_, "c_ds"), (ic, "c_ic"), (is_, "c_is")):
                sp.dma_start(dst, rows(A[name])).then_inc(s_dmat, 16)
            sp.wait_ge(s_sin, 4)
            sp.dma_start(skipb, A["hy_skip"][0].partition_broadcast(P)).then_inc(s_dmat, 16)
            load_w(3)
            load_w(4)
            sp.wait_ge(s_inv, 8)
            sp.dma_start(wuq, rows(A["mla_w_uq"][0])).then_inc(s_mw, 16)
            sp.dma_start(wukv, rows(A["mla_w_ukv"][0])).then_inc(s_mw, 16)
            sp.wait_ge(s_z, 8)
            sp.dma_start(cos_t[DV:DQ, :], A["c_cos"]).then_inc(s_rope, 16)
            sp.dma_start(sin_t[DV:DQ, :], A["c_sin"]).then_inc(s_rope, 16)
            load_w(5)
            sp.wait_ge(s_zero, 1)
            for d in range(2):
                for g, name in enumerate(("lru_wa", "lru_wx")):
                    for c in range(2):
                        for b in range(2):
                            sp.dma_start(lruw[64 * b:64 * b + 64, 4 * d + 2 * g + c, 64 * b:64 * b + 64],
                                         A[name][0, d, 2 * c + b]).then_inc(s_lw, 16)
            for c in range(6, len(CHUNKS)):
                load_w(c)
            sp.wait_ge(s_hpv, 2 * NH)
            sp.wait_ge(s_hpa, 4 * NH)
            sp.dma_start(wout, rows(A["w_out"][0])).then_inc(s_wo, 16)
            sp.wait_ge(s_pv, NH * TT)
            for dst, src in ((gin, A["ln_in_g"]), (bin_, A["ln_in_b"]), (gmix, A["ln_mix_g"][0]), (bmix, A["ln_mix_b"][0])):
                sp.dma_start(dst, src.partition_broadcast(P)).then_inc(s_gb, 16)
            for i in range(2):
                sp.dma_start(xres[:, i, :], xh_tok[:, i, :]).then_inc(s_xh[i], 16)
            sp.wait_ge(s_oT, TT)
            sp.dma_start(rw, rows(A["router_w"][0])).then_inc(s_rw, 16)

            def load_chunk(e, c):
                if c < 8:
                    half, kind, k = c // 4, ("exp_w_gate", "exp_w_up")[c % 2], c % 4 // 2
                else:
                    half, kind, k = (c - 8) // 2, "exp_w_down", c % 2
                w = A[kind][0]
                w = w[e] if isinstance(e, int) else w[bass.ds(e, 1)].rearrange("a k n -> (a k) n")
                src = w[HALF * k:HALF * k + HALF, HALF * half:HALF * half + HALF]
                sp.dma_start(wring[:, c], rows(src)).then_inc(s_wc[c], 16)

            for c in range(10):
                load_chunk(0, c)
            for i in range(TT):
                sp.wait_ge(s_x1, i + 1)
                sp.dma_start(x1_tok[:, i, :], x1t[:, i % 2, :]).then_inc(s_x1st[i % 2], 16)
                if i + 2 < TT:
                    sp.wait_ge(s_mixu, i + 1)
                    sp.dma_start(xres[:, i % 2, :], xh_tok[:, i + 2, :]).then_inc(s_xh[i % 2], 16)
            sp.wait_ge(s_lg, TT)
            for c in (10, 11):
                load_chunk(0, c)
            for dst, name in ((gff, "ln_ffn_g"), (bff, "ln_ffn_b")):
                sp.dma_start(dst, A[name][0].partition_broadcast(P)).then_inc(s_gff, 16)
            with sp.Fori(1, NE) as e:
                for c in range(WC):
                    sp.wait_ge(s_wcu, WC * e + (c + 1 - WC))
                    load_chunk(e, c)
            sp.wait_ge(s_sc, 16 * NE)
            for i in range(TT + 2):
                if i < TT:
                    if i >= 3:
                        sp.wait_ge(s_out[i % 3], 16 * (i // 3))
                    sp.dma_start(fin[:, i % 3, :], acc_tok[:, i, :]).then_inc(s_fx[i % 3], 16)
                if i >= 2:
                    sp.wait_ge(s_fo, i - 1)
                    sp.dma_start(out_tok[:, i - 2, :], fin[:, (i - 2) % 3, :]).then_inc(s_out[(i - 2) % 3], 16)
            for i in range(3):
                sp.wait_ge(s_out[i], 16 * len(range(i, TT, 3)))

        @block.gpsimd
        def _(pool):
            link = links(pool, s_pool)
            pool.memset(eps, EPS).then_inc(s_eps, 1)
            for nt in range(8):
                pool.wait_ge(s_hw, nt + 1)
                fwd, bwd = hw[:, nt % 2, 0:HALF], hw[:, nt % 2, HALF:]
                if nt == 0:
                    link(pool.memset(bwd[0:1, :], 0.0))
                pool.tensor_tensor(hf[:, nt, 0, :], fwd, bwd, ALU.add)
                pool.tensor_tensor(hf[:, nt, 1, :], fwd, bwd, ALU.subtract).then_inc(s_hab, 1)
            pool.wait_ge(s_z, 8)
            pool.memset(lruw, 0.0).then_inc(s_zero, 1)
            pool.memset(kr[0:DV, :], 0.0).then_inc(s_zero, 1)
            pool.wait_ge(s_gb, 64)
            for i in range(TT + 1):
                if i < TT:
                    res = xres[:, i % 2, :]
                    pool.wait_ge(s_xh[i % 2], 16 * (i // 2 + 1))
                    link(pool.tensor_tensor(res, res, gin, ALU.mult))
                    pool.tensor_tensor(res, res, bin_, ALU.add).then_inc(s_res, 1)
                if i >= 1:
                    x1i = x1t[:, (i - 1) % 2, :]
                    pool.wait_ge(s_mn, i)
                    link(pool.tensor_tensor(x1i, x1i, gmix, ALU.mult))
                    pool.tensor_tensor(x1i, x1i, bmix, ALU.add).then_inc(s_x1, 1)

            def gather(e, slot):
                copied, col = 2 * e + 2, slice(e, e + 1) if isinstance(e, int) else bass.ds(e, 1)
                pool.tensor_copy(idx_e[:, slot:slot + 1], idx_t[:, col]).then_inc(s_ie, 1)
                pool.tensor_copy(gate_e[:, slot:slot + 1], gate_t[:, col]).then_inc(s_ie, 1)
                pool.wait_ge(s_ie, copied)
                if not isinstance(e, int):
                    pool.tensor_tensor(idle[:, 0:1], eps, eps, ALU.add)
                pool.indirect_dma_start(xe[:, slot, :], None, x1_dram,
                                        bass.IndirectOffsetOnAxis(ap=idx_e[:, slot:slot + 1], axis=0)).then_inc(s_xe[slot], 16)

            def scatter(e, slot):
                pool.wait_ge(s_yea, e + 1)
                pool.wait_ge(s_yev, e + 1)
                if not isinstance(e, int):
                    pool.tensor_tensor(idle[:, 1:2], eps, eps, ALU.add)
                pool.indirect_dma_start(acc_dram, bass.IndirectOffsetOnAxis(ap=idx_e[:, slot:slot + 1], axis=0),
                                        ye[:, slot, :], None, compute_op=ALU.add).then_inc(s_sc, 16)

            for i in range(2):
                pool.wait_ge(s_x1st[i], 16 * TT // 2)
                pool.wait_ge(s_acst[i], 16 * TT // 2)
            pool.wait_ge(s_idxc, 1)
            gather(0, 0)
            gather(1, 1)
            scatter(0, 0)
            pool.wait_ge(s_sc, 16)
            gather(2, 0)
            scatter(1, 1)
            with pool.Fori(2, NE - 2, 2) as e:
                for n, slot in ((e, 0), (e + 1, 1)):
                    pool.wait_ge(s_sc, 16 * n)
                    pool.wait_ge(s_xep, 2 * n + 2)
                    gather(n + 1, 1 - slot)
                    scatter(n, slot)
            pool.wait_ge(s_sc, 16 * (NE - 2))
            gather(NE - 1, 1)
            scatter(NE - 2, 0)
            pool.wait_ge(s_sc, 16 * (NE - 1))
            scatter(NE - 1, 1)
            pool.wait_ge(s_gff, 32)
            for i in range(TT):
                pool.wait_ge(s_fn, i + 1)
                pool.tensor_tensor(fin[:, i % 3, :], fin[:, i % 3, :], bff, ALU.add).then_inc(s_fo, 1)

        @block.scalar
        def _(act):
            link = links(act, s_act)
            a = act.activation

            def sines(layer):
                for j in range(2):
                    act.wait_ge(s_arg, 2 * layer + j + 1)
                    h = slice(HALF * j, HALF * j + HALF)
                    a((h1, h2)[layer][:, h], warg[:, h], ACT.Sin).then_inc(s_sin, 1)

            def in_root(i):
                act.wait_ge(s_st, i + 1)
                a(sd[:, i % 2:i % 2 + 1], mv[:, i % 2, 1:2], ACT.Sqrt, bias=eps).then_inc(s_sd, 1)

            def x_copy(i):
                act.wait_ge(s_xp, i + 1)
                src = bank(4 + 2 * (i % 2), 2)
                for k in range(KT):
                    ins = a(xT[:, k, P * i:P * i + P], src[:, P * k:P * k + P], ACT.Identity,
                            scale=par[:, C_LG + k:C_LG + k + 1], bias=par[:, C_LB + k:C_LB + k + 1])
                ins.then_inc(s_xT, 1)

            act.wait_ge(s_eps, 1)
            act.wait_ge(s_parc, 2)
            sines(0)
            in_root(0)
            sines(1)
            for i in range(TT):
                if i + 1 < TT:
                    in_root(i + 1)
                x_copy(i)

            for jt in range(4):
                act.wait_ge(s_dft, jt + 1)
                if jt:
                    act.wait_ge(s_kf, 4 * jt)
                a(fodd[:, 0, :], bank(4 * (jt % 2) + 1), ACT.Copy).then_inc(s_fodd, 1)
                a(fodd[:, 1, :], bank(4 * (jt % 2) + 3), ACT.Copy).then_inc(s_fodd, 1)

            def hy_copy(m):
                act.wait_ge(s_ut, 2 * m + 1)
                a(g_hy[:, m // 2, :, 0, P * (m % 2):P * (m % 2) + P],
                  bank(4).rearrange("p (i c) -> p i c", i=4), ACT.Copy).then_inc(s_uta, 1)

            act.wait_ge(s_xst, 16 * TT)
            for m in range(N_HY):
                act.wait_ge(s_pj, m + 1)
                y = bank(proj_bank(m), 2)
                for dst, src in ((u_hy[:, m, 0:HALF], y[:, HALF:]), (reverse(m, 0, HALF), y[:, 0:HALF])):
                    ins = a(dst, src, ACT.Identity, scale=par[:, C_HYW + 6 + m:C_HYW + 7 + m], bias=par[:, C_HYB + m:C_HYB + m + 1])
                ins.then_inc(s_pja, 1)
                if m:
                    hy_copy(m - 1)
            hy_copy(N_HY - 1)

            def odd_copies(o):
                for i in range(4):
                    act.wait_ge(s_inv, 4 * o + i + 1)
                    if i or o:
                        act.wait_ge(s_z, 4 * o + i)
                    a(odd, bank(i)[:, HYW:], ACT.Copy).then_inc(s_od, 1)

            def lr_centre(c):
                act.wait_ge(s_pj, I_LR + c + 1)
                a(xr[:, c, :], bank(6, 2), ACT.Identity, scale=par[:, C_LRW + 4 + c:C_LRW + 5 + c],
                  bias=par[:, C_LRB + c:C_LRB + c + 1]).then_inc(s_pja, 1)

            odd_copies(0)
            lr_centre(0)
            odd_copies(1)
            act.wait_ge(s_z, 8)
            for i in range(8):
                link(a(odd, zbuf[:, i // 2, i % 2, :], ACT.Square, accum_out=hss[:, i:i + 1]))
            a(hsd, hss, ACT.Sqrt, scale=1.0 / HYW, bias=eps).then_inc(s_hsd, 1)
            link(a(spt[:, 0, :], par[:, C_LAM:C_LAM + 4], ACT.Abs))
            a(spt[:, 1, :], spt[:, 0, :], ACT.Exp, scale=-1.0).then_inc(s_spa, 1)
            lr_centre(1)
            for c in range(2):
                act.wait_ge(s_pj, I_LG + c + 1)
                a(gelu[:, c, :], bank(proj_bank(I_LG + c), 2), ACT.Gelu_apprx_tanh).then_inc(s_pja, 1)
            for c in range(2):
                act.wait_ge(s_hyT, c + 1)
                gcol = par[:, C_GN + c:C_GN + c + 1]
                a(yT_hy[:, c, HALF:T], bank(2 * c), ACT.Copy, scale=gcol)
                a(yT_hy[:, c, HALF - 1::-1], bank(2 * c + 1), ACT.Copy, scale=gcol).then_inc(s_hyc, 1)

            def gates(q):
                la_, lx_, lt_ = la[:, q % 2, :], lx[:, q % 2, :], lt[:, q % 2, :]
                if q == 0:
                    act.wait_ge(s_spv, 1)
                if q >= 2:
                    act.wait_ge(s_lv, 2 * (q - 1))
                for j in range(2):
                    act.wait_ge(s_gmm, 2 * q + j + 1)
                    h = slice(HALF * j, HALF * j + HALF)
                    a(lx_[:, h], bank(1), ACT.Sigmoid, bias=par[:, C_BX + q:C_BX + q + 1])
                    a(lt_[:, h], bank(0), ACT.Sigmoid, bias=par[:, C_BA + q:C_BA + q + 1]).then_inc(s_gact, 1)
                act.wait_ge(s_gact, 2 * q + 2)
                a(la_, lt_, ACT.Exp, scale=nsp8[:, q:q + 1])
                a(lt_, lt_, ACT.Tanh, scale=sp8[:, q:q + 1]).then_inc(s_lact, 1)
                act.wait_ge(s_lv, 2 * q + 1)
                a(lt_, lt_, ACT.Sqrt, scale=2.0).then_inc(s_lact, 1)

            def squares(i, n):
                act.wait_ge(s_pj, i + 1)
                if n:
                    act.wait_ge(s_ssq, n)
                a(sq, bank(proj_bank(i), 2), ACT.Square).then_inc(s_sq, 1)

            def rms_root(dst, n, k):
                act.wait_ge(s_ssq, n)
                a(dst, bank(2, 2), ACT.Sqrt, scale=1.0 / k, bias=eps).then_inc(s_rsd, 1)

            squares(I_KV, 0)
            gates(0)
            squares(I_KV + 1, 1)
            gates(1)
            rms_root(rb, 2, KVL)
            act.wait_ge(s_pj, I_KR + 1)
            act.wait_ge(s_zero, 2)
            a(kr[DV:DQ, :], bank(proj_bank(I_KR), 2, DV, DQ), ACT.Copy).then_inc(s_pja, 1)
            gates(2)
            squares(I_CQ, 2)
            squares(I_CQ + 1, 3)
            gates(3)
            for c in range(2, 6):
                squares(I_CQ + c, 2 + c)
            act.wait_ge(s_rb, 1)
            rms_root(rb, 8, QL)
            for c in range(2):
                act.wait_ge(s_hsg, c + 1)
                act.wait_ge(s_ssq, 8 + c)
                a(sq, hs[:, c, :], ACT.Square).then_inc(s_sq, 1)
            rms_root(rb_lru, 10, LRW)

            for t in range(0, TT, 2):
                act.wait_ge(s_vmm, t + 1)
                a(v_at[:, t, :], bank(0), ACT.Copy).then_inc(s_va, 1)

            def head_copy(h, s):
                act.wait_ge(s_hp, 6 * h + s + 1)
                if h >= 2 and s == 0:
                    act.wait_ge(s_qk, TT * (h - 1))
                dst, p1 = (qh, DQ) if s < 2 else (kh, DV)
                a(dst[0:p1, h % 2, HALF * (s % 2):HALF * (s % 2) + HALF], bank(6, p1=p1), ACT.Copy).then_inc(s_hpa, 1)

            def probs_copy(n):
                act.wait_ge(s_tr, 2 * n + 1)
                if n >= 2:
                    act.wait_ge(s_pv, n - 1)
                a(pT[:, n % 2, 0:HALF], bank(4), ACT.Copy).then_inc(s_pta, 1)

            for s in (0, 1, 4, 5):
                head_copy(0, s)
            for n in range(NH * TT):
                h, qt = divmod(n, TT)
                act.wait_ge(s_nm, n + 1)
                if n >= 2:
                    act.wait_ge(s_tr, 2 * (n - 1))
                a(p_at[:, n % 2, :], bank(2 * (n % 2), 2), ACT.Exp, scale=SCALE, bias=nm[:, n % 2:n % 2 + 1],
                  accum_out=rsum[:, n % 4:n % 4 + 1]).then_inc(s_exp, 1)
                if n >= 1:
                    probs_copy(n - 1)
                if h + 1 < NH and qt in (1, 2, 5, 6):
                    head_copy(h + 1, qt - 1)
            probs_copy(NH * TT - 1)
            for t in range(TT):
                act.wait_ge(s_ov, NH * TT - TT + t + 1)
                link(a(sq[:, 0:HALF], o_at[:, t, :], ACT.Square, accum_out=ass[:, t:t + 1]))
                a(asd[:, t:t + 1], ass[:, t:t + 1], ACT.Sqrt, scale=1.0 / (NH * DV), bias=eps).then_inc(s_osd, 1)

            def router_exp(i):
                act.wait_ge(s_rm, i + 1)
                a(aff[:, i % 2, :], bank(6)[:, NE * (i % 2):NE * (i % 2) + NE], ACT.Exp, bias=rmx[:, i % 2:i % 2 + 1],
                  accum_out=rsm[:, i % 2:i % 2 + 1]).then_inc(s_re, 1)

            def aff_copy(i):
                act.wait_ge(s_afT, i + 1)
                a(affT[:, P * i:P * i + P], bank(7, p1=NE)[:, P * (i % 2):P * (i % 2) + P], ACT.Copy).then_inc(s_afc, 1)

            for i in range(TT + 2):
                if i < TT:
                    act.wait_ge(s_mst, i + 1)
                    a(sd[:, i % 2:i % 2 + 1], mv[:, i % 2, 1:2], ACT.Sqrt, bias=eps).then_inc(s_msd, 1)
                    act.wait_ge(s_x1, i + 1)
                    if i >= 2:
                        act.wait_ge(s_acst[i % 2], 16 * (i // 2))
                    else:
                        act.wait_ge(s_oT, TT)
                    a(accb[:, i % 2, :], x1t[:, i % 2, :], ACT.Copy, scale=ALPHA).then_inc(s_acc, 1)
                    act.wait_ge(s_acc, i + 1)
                    act.dma_start(acc_tok[:, i, :], accb[:, i % 2, :]).then_inc(s_acst[i % 2], 16)
                    act.wait_ge(s_x1p, 2 * i + 1)
                    if i >= 2:
                        act.wait_ge(s_lg, i - 1)
                    a(x1T[i % 2][:, 0:HALF], bank(4), ACT.Copy).then_inc(s_x1ta, 1)
                if 1 <= i <= TT:
                    router_exp(i - 1)
                if i >= 2:
                    aff_copy(i - 2)

            def xe_copy(e):
                act.wait_ge(s_xep, 2 * e + 1)
                a(flat(xeT)[:, 0:HALF], bank(4), ACT.Copy).then_inc(s_xea, 1)

            def expert(e, slot, first, last):
                for f in range(2):
                    act.wait_ge(s_wcu, WC * e + (4 * f + 4))
                    a(sil[:, f, :], bank(2 * f), ACT.Silu).then_inc(s_sil, 1)
                if not last:
                    xe_copy(e + 1)
                act.wait_ge(s_ht, 2 * e + 1)
                a(flat(hidT)[:, 0:HALF], bank(4), ACT.Copy).then_inc(s_hta, 1)
                act.wait_ge(s_wcu, WC * e + 10)
                if not first:
                    act.wait_ge(s_sc, 16 * e - 16)
                a(ye[:, slot, 0:HALF], bank(6), ACT.Copy, scale=gate_e[:, slot:slot + 1]).then_inc(s_yea, 1)

            act.wait_ge(s_idxc, 1)
            xe_copy(0)
            expert(0, 0, True, False)
            expert(1, 1, True, False)
            with act.Fori(2, NE - 2, 2) as e:
                expert(e, 0, False, False)
                expert(e + 1, 1, False, False)
            expert(NE - 2, 0, False, False)
            expert(NE - 1, 1, False, True)
            for i in range(TT):
                act.wait_ge(s_fst, i + 1)
                a(fsd[:, i % 2:i % 2 + 1], fmv[:, i % 2, 1:2], ACT.Sqrt, bias=eps).then_inc(s_fsd, 1)

        @block.tensor
        def _(pe):
            mm = pe.matmul
            pe.wait_ge(s_par, 16 * 21)
            pe.transpose(bank(0)[:, 0:N_PAR], prow, ident[0:N_PAR, 0:N_PAR]).then_inc(s_parT, 1)
            pe.transpose(bank(1, p1=FFN)[:, 0:4], frow, ident[0:4, 0:4]).then_inc(s_parT, 1)
            pe.wait_ge(s_parc, 2)
            for j in range(2):
                mm(bank(j, p1=FFN), w1, pos_t[:, HALF * j:HALF * j + HALF], start=True, stop=True).then_inc(s_fmm, 1)
            for j in range(2):
                pe.wait_ge(s_sin, j + 1)
                mm(bank(j, p1=FFN), w2, h1[:, HALF * j:HALF * j + HALF], start=True, stop=True).then_inc(s_fmm, 1)

            def x_turn(i):
                pe.wait_ge(s_xn, i + 1)
                if i >= 2:
                    pe.wait_ge(s_xT, i - 1)
                for k in range(KT):
                    ins = pe.transpose(bank(4 + 2 * (i % 2), 2)[:, P * k:P * k + P], xr_in[:, i % 3, P * k:P * k + P], ident)
                ins.then_inc(s_xp, 1)

            for nt in range(8):
                if nt == 0:
                    pe.wait_ge(s_sin, 4)
                else:
                    pe.wait_ge(s_hw, max(nt - 1, 1))
                for d in range(2):
                    ins = mm(bank(2 * (nt % 2) + d), h2[:, P * nt:P * nt + P], w3[:, HALF * d:HALF * d + HALF], start=True, stop=True)
                ins.then_inc(s_f3, 1)
                x_turn(nt)

            pe.wait_ge(s_fmat, 32)
            pe.wait_ge(s_hab, 8)
            pe.wait_ge(s_hw, 8)
            pe.wait_ge(s_xT, TT)
            for jt in range(4):
                if jt >= 2:
                    pe.wait_ge(s_kf, 4 * (jt - 1))
                for b, (mat, part) in enumerate(((fc, 0), (fc, 0), (fs, 1), (fs, 1))):
                    for n in range(4):
                        nt = 4 * (b % 2) + n
                        ins = mm(bank(4 * (jt % 2) + b), mat[:, nt, P * jt:P * jt + P], hf[:, nt, part, :], start=(n == 0), stop=(n == 3))
                ins.then_inc(s_dft, 1)

            def project(i):
                c = chunk_of(i)
                c0, w = PROJ[i]
                at = c0 - CHUNKS[c][0]
                p0 = DV if i == I_KR else 0
                pe.wait_ge(s_w[c % 3], 16 * (c // 3 + 1))
                before = proj_before(i)
                if before is not None:
                    pe.wait_ge(*act_read(before))
                    pe.wait_ge(s_pjv, dve_reads(before))
                for k in range(KT):
                    for j in range(2):
                        ins = mm(bank(proj_bank(i) + j, 1, p0, p0 + w), win_w[:, c % 3, k, at:at + w], xT[:, k, HALF * j:HALF * j + HALF],
                                 start=(k == 0), stop=(k == KT - 1))
                ins.then_inc(s_pj, 1)

            def hy_turn(m):
                pe.wait_ge(s_pjv, m + 1)
                for half in range(2):
                    if m:
                        pe.wait_ge((s_uta, s_utv)[half], m)
                    for i in range(4):
                        t0 = HALF * half + P * i
                        ins = pe.transpose(bank(4 + half)[:, P * i:P * i + P], u_hy[:, m, t0:t0 + P], ident)
                    ins.then_inc(s_ut, 1)

            pe.wait_ge(s_kf, 16)
            for m in range(N_HY):
                project(m)
                if m:
                    hy_turn(m - 1)
            hy_turn(N_HY - 1)

            def conv(o):
                if o == 0:
                    pe.wait_ge(s_dmat, 80)
                    pe.wait_ge(s_uta, N_HY)
                    pe.wait_ge(s_utv, N_HY)
                pe.wait_ge(s_fold, o + 1)
                for f in range(9):
                    if f < 8:
                        if f >= 2 or o:
                            pe.wait_ge(s_yf, 8 * o + f - 1 if f >= 2 else 8)
                        for part, mat in enumerate((dc, ds_)):
                            for i in range(4):
                                ins = mm(bank(4 + f % 2)[:, HYW * part:HYW * part + HYW], mat[:, i, P * f:P * f + P], pm[:, part, i, :],
                                         start=(i == 0), stop=(i == 3))
                        ins.then_inc(s_uf, 1)
                    if f:
                        g = f - 1
                        if g == 0 and o:
                            pe.wait_ge(s_z, 4)
                        pe.wait_ge(s_yf, 8 * o + g + 1)
                        for i in range(4):
                            mm(bank(i)[:, 0:HYW], ic[:, g, P * i:P * i + P], yf[:, g % 2, 0:HYW], start=(g == 0), stop=(g == 7), skip_group_check=True)
                            ins = mm(bank(i)[:, HYW:], is_[:, g, P * i:P * i + P], yf[:, g % 2, HYW:], start=False, stop=(g == 7), skip_group_check=True)
                            if g == 7:
                                ins.then_inc(s_inv, 1)
                        if g < 7:
                            ins.then_inc(s_yfu, 1)

            pe.wait_ge(s_pja, N_HY)
            conv(0)
            project(I_LR)
            conv(1)
            pe.wait_ge(s_yf, 16)
            for i in range(I_LR + 1, I_KV):
                project(i)
            pe.wait_ge(s_hyn, 1)
            for c in range(2):
                for half in range(2):
                    for i in range(4):
                        ins = pe.transpose(bank(2 * c + half)[:, P * i:P * i + P], zbuf[:, i, half, P * c:P * c + P], ident)
                ins.then_inc(s_hyT, 1)

            def gates(q):
                d, c = divmod(q, 2)
                if q == 0:
                    pe.wait_ge(s_lw, 16 * 16)
                    pe.wait_ge(s_hyc, 2)
                    pe.wait_ge(s_pjv, dve_reads(I_LR + 1))
                for j in range(2):
                    if 2 * q + j:
                        pe.wait_ge(s_gact, 2 * q + j)
                    for g in range(2):
                        ins = mm(bank(g), lruw[:, 4 * d + 2 * g + c, :], xr[:, c, HALF * j:HALF * j + HALF], start=True, stop=True)
                    ins.then_inc(s_gmm, 1)

            def sum_squares(n, first, last):
                if n == 2 or n == 8:
                    pe.wait_ge(s_rsd, 1 if n == 2 else 2)
                pe.wait_ge(s_sq, n + 1)
                for j in range(2):
                    ins = mm(bank(2 + j), ones, sq[:, HALF * j:HALF * j + HALF], start=first, stop=last)
                ins.then_inc(s_ssq, 1)

            project(I_KV)
            gates(0)
            project(I_KV + 1)
            sum_squares(0, True, False)
            gates(1)
            sum_squares(1, False, True)
            project(I_KR)
            gates(2)
            pe.wait_ge(*act_read(I_KR))
            pe.wait_ge(s_gact, 6)
            for j in range(2):
                ins = mm(bank(j, p1=DQ), rot, kr[:, HALF * j:HALF * j + HALF], start=True, stop=True)
            ins.then_inc(s_krm, 1)
            project(I_CQ)
            project(I_CQ + 1)
            sum_squares(2, True, False)
            pe.wait_ge(s_kro, 1)
            gates(3)
            for c in range(2, 6):
                project(I_CQ + c)
                sum_squares(1 + c, False, False)
            sum_squares(7, False, True)
            sum_squares(8, True, False)
            sum_squares(9, False, True)

            pe.wait_ge(s_mw, 32)
            pe.wait_ge(s_rb, 1)
            pe.wait_ge(s_gact, 8)
            wv = wukv.rearrange("p k (h n) -> p k h n", h=NH)
            for t in range(TT):
                if t >= 2:
                    pe.wait_ge((s_va, s_vv)[t % 2], t // 2)
                for k in range(2):
                    ins = mm(bank(t % 2), ckv[:, k, P * t:P * t + P], wv[:, k, :, DV:], start=(k == 0), stop=(k == 1))
                ins.then_inc(s_vmm, 1)

            def head_step(h, s):
                if s == 0:
                    if h:
                        pe.wait_ge(s_hpa, 4 * h)
                    else:
                        pe.wait_ge(s_rb, 2)
                        pe.wait_ge(*act_read(len(PROJ) - 1))
                elif s in (1, 2):
                    pe.wait_ge(s_hpa, 4 * h + s)
                elif s in (3, 4):
                    pe.wait_ge(s_hpv, 2 * h + s - 2)
                else:
                    pe.wait_ge(s_hpa, 4 * h + 3)
                h0 = HALF * (s % 2)
                if s < 2:
                    for k in range(6):
                        ins = mm(bank(6, p1=DQ), wuq[:, k, DQ * h:DQ * h + DQ], cq[:, k, h0:h0 + HALF], start=(k == 0), stop=(k == 5))
                elif s < 4:
                    ins = mm(bank(6, p1=DQ), rot, qh[0:DQ, h % 2, h0:h0 + HALF], start=True, stop=True)
                else:
                    for k in range(2):
                        ins = mm(bank(6, p1=DV), wv[:, k, h, 0:DV], ckv[:, k, h0:h0 + HALF], start=(k == 0), stop=(k == 1))
                ins.then_inc(s_hp, 1)

            def scores(n):
                h, qt = divmod(n, TT)
                if qt == 0:
                    pe.wait_ge(s_hpa, 4 * h + 4)
                    pe.wait_ge(s_hpv, 2 * h + 2)
                if n == 0:
                    pe.wait_ge(s_kro, 2)
                    pe.wait_ge(s_rsd, 3)
                    pe.wait_ge(s_va, TT // 2)
                    pe.wait_ge(s_vv, TT // 2)
                if n >= 2:
                    pe.wait_ge(s_exp, n - 1)
                for j in range(2):
                    ins = mm(bank(2 * (n % 2) + j), qh[0:DQ, h % 2, P * qt:P * qt + P], kh[0:DQ, h % 2, HALF * j:HALF * j + HALF], start=True, stop=True)
                ins.then_inc(s_qk, 1)

            def probs_turn(n):
                pe.wait_ge(s_exp, n + 1)
                for b in range(2):
                    if n:
                        pe.wait_ge((s_pta, s_ptv)[b], n)
                    for k in range(4):
                        ins = pe.transpose(bank(4 + b)[:, P * k:P * k + P], p_at[:, n % 2, HALF * b + P * k:HALF * b + P * k + P], ident)
                    ins.then_inc(s_tr, 1)

            def pv(n):
                h = n // TT
                pe.wait_ge(s_pta, n + 1)
                pe.wait_ge(s_ptv, n + 1)
                if n:
                    pe.wait_ge(s_ov, n)
                for k in range(KT):
                    ins = mm(bank(7)[:, DV * (n % 2):DV * (n % 2) + DV], pT[:, n % 2, P * k:P * k + P], v_at[:, k, DV * h:DV * h + DV],
                             start=(k == 0), stop=(k == KT - 1))
                ins.then_inc(s_pv, 1)

            for s in range(6):
                head_step(0, s)
            scores(0)
            N = NH * TT
            for n in range(N):
                h, qt = divmod(n, TT)
                if n + 1 < N:
                    scores(n + 1)
                probs_turn(n)
                if n:
                    pv(n - 1)
                if h + 1 < NH and qt < 6:
                    head_step(h + 1, qt)
            pv(N - 1)

            for t in range(TT):
                pe.wait_ge(s_on, t + 1)
                if t >= 2:
                    pe.wait_ge(s_oc, t - 1)
                for c in range(4):
                    ins = pe.transpose(bank(t % 2)[:, P * c:P * c + P], o_at[:, t, P * c:P * c + P], ident)
                ins.then_inc(s_oT, 1)

            def x1_turn(i):
                pe.wait_ge(s_x1, i + 1)
                for b in range(2):
                    if i:
                        pe.wait_ge((s_x1ta, s_x1tv)[b], i)
                    for k in range(4):
                        ins = pe.transpose(bank(4 + b)[:, P * k:P * k + P], x1t[:, i % 2, HALF * b + P * k:HALF * b + P * k + P], ident)
                    ins.then_inc(s_x1p, 1)

            def logits(i):
                pe.wait_ge(s_x1ta, i + 1)
                pe.wait_ge(s_x1tv, i + 1)
                if i == 0:
                    pe.wait_ge(s_rw, 16)
                if i:
                    pe.wait_ge(s_re, i)
                for k in range(KT):
                    ins = mm(bank(6)[:, NE * (i % 2):NE * (i % 2) + NE], x1T[i % 2][:, P * k:P * k + P], rw[:, k, :], start=(k == 0), stop=(k == KT - 1))
                ins.then_inc(s_lg, 1)

            def aff_turn(i):
                pe.wait_ge(s_aff, i + 1)
                if i:
                    pe.wait_ge(s_afc, i)
                pe.transpose(bank(7, p1=NE)[:, P * (i % 2):P * (i % 2) + P], aff[:, i % 2, :], ident).then_inc(s_afT, 1)

            pe.wait_ge(s_wo, 16)
            pe.wait_ge(s_oc, TT)
            pe.wait_ge(s_rb, 3)
            yT = [yT_hy[:, 0, :], yT_hy[:, 1, :], yT_lru[:, 0, :], yT_lru[:, 1, :]] + [yT_at[:, c, :] for c in range(4)]
            for i in range(TT + 3):
                if i < TT:
                    if i >= 2:
                        pe.wait_ge(s_mixu, i - 1)
                    for k in range(KT):
                        for j in range(2):
                            ins = mm(bank(2 * (i % 2) + j), yT[k][:, P * i:P * i + P], wout[:, k, HALF * j:HALF * j + HALF], start=(k == 0), stop=(k == KT - 1))
                    ins.then_inc(s_mix, 1)
                if 1 <= i <= TT:
                    x1_turn(i - 1)
                if 2 <= i <= TT + 1:
                    logits(i - 2)
                if i >= 3:
                    aff_turn(i - 3)
            pe.wait_ge(s_topk, 1)
            pe.transpose(bank(4)[:, 0:NE], idxf, ident[0:NE, 0:NE])
            pe.transpose(bank(4)[:, NE:2 * NE], vals, ident[0:NE, 0:NE]).then_inc(s_idxp, 1)

            def xe_turn(e, slot, first):
                pe.wait_ge(s_xe[slot], 16 if first else 8 * e + (16 if slot == 0 else 8))
                for b in range(2):
                    if not first:
                        pe.wait_ge((s_hta, s_htv)[b], e - 1)
                    for k in range(4):
                        ins = pe.transpose(bank(4 + b)[:, P * k:P * k + P], xe[:, slot, HALF * b + P * k:HALF * b + P * k + P], ident)
                    ins.then_inc(s_xep, 1)

            def expert(e, slot, first, last):
                pe.wait_ge(s_xea, e + 1)
                pe.wait_ge(s_xev, e + 1)
                for f in range(2):
                    if not first or slot:
                        pe.wait_ge(s_hid, 2 * e + f - 1)
                    for k in range(KT):
                        if k % 4 == 0:
                            for g in range(2):
                                pe.wait_ge(s_wc[4 * f + k // 2 + g], 16 * e + 16)
                        for g in range(2):
                            ins = mm(bank(2 * f + g), xeT[:, k, :], wring[:, 4 * f + k // 4 * 2 + g, k % 4, :], start=(k == 0), stop=(k == KT - 1))
                            if k % 4 == 3:
                                ins.then_inc(s_wcu, 1)
                if not last:
                    xe_turn(e + 1, 1 - slot, first and not slot)
                for b in range(2):
                    if not last:
                        pe.wait_ge((s_xea, s_xev)[b], e + 2)
                    pe.wait_ge(s_hid, 2 * e + b + 1)
                    for k in range(4):
                        ins = pe.transpose(bank(4 + b)[:, P * k:P * k + P], hid[:, HALF * b + P * k:HALF * b + P * k + P], ident)
                    ins.then_inc(s_ht, 1)
                for j in range(2):
                    if not first or slot:
                        pe.wait_ge((s_yea, s_yev)[j], e)
                    for k in range(KT):
                        if k % 4 == 0:
                            pe.wait_ge(s_wc[8 + 2 * j + k // 4], 16 * e + 16)
                            if j == 0:
                                pe.wait_ge((s_hta, s_htv)[k // 4], e + 1)
                        ins = mm(bank(6 + j), hidT[:, k, :], wring[:, 8 + 2 * j + k // 4, k % 4, :], start=(k == 0), stop=(k == KT - 1))
                        if k % 4 == 3:
                            ins.then_inc(s_wcu, 1)

            pe.wait_ge(s_idxc, 1)
            xe_turn(0, 0, True)
            expert(0, 0, True, False)
            expert(1, 1, True, False)
            with pe.Fori(2, NE - 2, 2) as e:
                expert(e, 0, False, False)
                expert(e + 1, 1, False, False)
            expert(NE - 2, 0, False, False)
            expert(NE - 1, 1, False, True)

        @block.vector
        def _(v):
            link = links(v, s_dve)
            stt, tt, ts = v.scalar_tensor_tensor, v.tensor_tensor, v.tensor_scalar

            v.wait_ge(s_parT, 2)
            v.tensor_copy(par[:, 0:N_PAR], bank(0)[:, 0:N_PAR]).then_inc(s_parc, 1)
            v.tensor_copy(fpar, bank(1, p1=FFN)[:, 0:4]).then_inc(s_parc, 1)
            v.wait_ge(s_parc, 2)

            def sine_args(layer):
                for j in range(2):
                    w, n = warg[:, HALF * j:HALF * j + HALF], turns[:, HALF * j:HALF * j + HALF]
                    v.wait_ge(s_fmm, 2 * layer + j + 1)
                    link(ts(w, bank(j, p1=FFN), fpar[:, 2 * layer:2 * layer + 1], fpar[:, 2 * layer + 1:2 * layer + 2], ALU.add, ALU.mult))
                    link(ts(n, w, 1.0 / (2.0 * np.pi), MAGIC, ALU.mult, ALU.add))
                    link(ts(n, n, MAGIC, None, ALU.subtract))
                    link(stt(w, n, -TWO_PI_HI, w, ALU.mult, ALU.add))
                    link(stt(w, n, -TWO_PI_LO, w, ALU.mult, ALU.add))
                    ts(w, w, PI_IN, -PI_IN, ALU.min, ALU.max).then_inc(s_arg, 1)

            def stats(x, st_, mv_):
                v.bn_stats(st_[:, 0:6], x[:, 0:HALF])
                link(v.bn_stats(st_[:, 6:12], x[:, HALF:D]))
                return v.bn_aggr(mv_, st_)

            def norm_rows(x, root, inv, mv_):
                link(v.reciprocal(inv, root))
                return ts(x, x, mv_[:, 0:1], inv, ALU.subtract, ALU.mult)

            def in_norm(i):
                v.wait_ge(s_x[i % 3], 16 * (i // 3 + 1))
                x, b = xr_in[:, i % 3, :], i % 2
                stats(x, st[:, b, :], mv[:, b, :]).then_inc(s_st, 1)
                v.wait_ge(s_sd, i + 1)
                norm_rows(x, sd[:, b:b + 1], rstd[:, b:b + 1], mv[:, b, :]).then_inc(s_xn, 1)

            sine_args(0)
            in_norm(0)
            sine_args(1)
            v.wait_ge(s_wint, 16)
            for nt in range(8):
                if nt + 1 < TT:
                    in_norm(nt + 1)
                v.wait_ge(s_f3, nt + 1)
                if nt >= 2:
                    v.wait_ge(s_hab, nt - 1)
                tt(hw[:, nt % 2, :].rearrange("p (a c) -> p a c", a=4), bank(2 * (nt % 2), 2).rearrange("p (a c) -> p a c", a=4),
                   win[:, nt, :].unsqueeze(1).to_broadcast([P, 4, HYW]), ALU.mult).then_inc(s_hw, 1)

            def by_order(ap):
                return ap.rearrange("p (o c) -> p o c", o=2)

            for jt in range(4):
                b0 = 4 * (jt % 2)
                v.wait_ge(s_fodd, 2 * jt + 2)
                for part in range(2):
                    even, oddp = by_order(bank(b0 + 2 * part)), by_order(fodd[:, part, :])
                    tt(kf[:, :, jt, part, :], even, oddp, ALU.add).then_inc(s_kf, 1)
                    if part == 0:
                        tt(kf[:, :, 4 + jt, part, :], even, oddp, ALU.subtract).then_inc(s_kf, 1)
                    else:
                        tt(kf[:, :, 4 + jt, part, :], oddp, even, ALU.subtract).then_inc(s_kf, 1)

            def hy_copy(m):
                v.wait_ge(s_ut, 2 * m + 2)
                v.tensor_copy(g_hy[:, m // 2, :, 1, P * (m % 2):P * (m % 2) + P], bank(5).rearrange("p (i c) -> p i c", i=4)).then_inc(s_utv, 1)

            v.wait_ge(s_xst, 16 * TT)
            for m in range(N_HY):
                v.wait_ge(s_pja, m + 1)
                u, y = u_hy[:, m, :], bank(proj_bank(m), 2)
                w0, w2 = par[:, C_HYW + m:C_HYW + m + 1], par[:, C_HYW + 12 + m:C_HYW + 13 + m]
                lo = reverse(m, 1, HALF)
                stt(u[:, 0:HALF], y[:, HALF - 1:T - 1], w0, u[:, 0:HALF], ALU.mult, ALU.add)
                link(stt(lo, y[:, 0:HALF - 1], w0, lo, ALU.mult, ALU.add))
                lo = reverse(m, 0, HALF)
                stt(u[:, 0:HALF - 1], y[:, HALF + 1:], w2, u[:, 0:HALF - 1], ALU.mult, ALU.add)
                stt(lo, y[:, 1:HALF + 1], w2, lo, ALU.mult, ALU.add).then_inc(s_pjv, 1)
                if m:
                    hy_copy(m - 1)
            hy_copy(N_HY - 1)

            def lr_taps(c):
                v.wait_ge(s_pja, I_LR + c + 1)
                x, y = xr[:, c, :], bank(6, 2)
                w = [par[:, C_LRW + 2 * k + c:C_LRW + 2 * k + c + 1] for k in range(4)]
                link(stt(x[:, 2:], y[:, 0:T - 2], w[0], x[:, 2:], ALU.mult, ALU.add))
                link(stt(x[:, 1:], y[:, 0:T - 1], w[1], x[:, 1:], ALU.mult, ALU.add))
                stt(x[:, 0:T - 1], y[:, 1:], w[3], x[:, 0:T - 1], ALU.mult, ALU.add).then_inc(s_pjv, 1)

            def conv(o, z):
                tt(pm[:, 0], z[:, :, 0, :], z[:, :, 1, :], ALU.add)
                tt(pm[:, 1], z[:, :, 0, :], z[:, :, 1, :], ALU.subtract).then_inc(s_fold, 1)
                tt(tsk.rearrange("p i h c -> p (i h) c"), z.rearrange("p i h c -> p (i h) c"),
                   skipb[:, o, :].unsqueeze(1).to_broadcast([P, 8, HYW]), ALU.mult)
                for f in range(8):
                    v.wait_ge(s_uf, 8 * o + f + 1)
                    kc, ks = kf[:, o, f, 0, :], kf[:, o, f, 1, :]
                    u = bank(4 + f % 2)
                    if f or o:
                        v.wait_ge(s_yf, 8 * o + f)
                    tt(by_order(t1), by_order(u), kc.unsqueeze(1).to_broadcast([P, 2, HYW]), ALU.mult)
                    tt(t2[:, 0:HYW], u[:, HYW:], ks, ALU.mult)
                    link(tt(t2[:, HYW:], u[:, 0:HYW], ks, ALU.mult))
                    if f >= 2:
                        v.wait_ge(s_yfu, 7 * o + f - 1)
                    elif o:
                        v.wait_ge(s_inv, 4)
                    y = yf[:, f % 2, :]
                    tt(y[:, 0:HYW], t1[:, 0:HYW], t2[:, 0:HYW], ALU.subtract)
                    tt(y[:, HYW:], t1[:, HYW:], t2[:, HYW:], ALU.add).then_inc(s_yf, 1)
                for i in range(4):
                    s = tsk[:, i]
                    v.wait_ge(s_od, 4 * o + i + 1)
                    link(tt(s, s, bank(i)[:, 0:HYW].unsqueeze(1).to_broadcast([P, 2, HYW]), ALU.add))
                    tt(s[:, 0, :], s[:, 0, :], odd, ALU.add)
                    link(tt(s[:, 1, :], s[:, 1, :], odd, ALU.subtract))
                    tt(zbuf[:, i], s, g_hy[:, o, i], ALU.mult).then_inc(s_z, 1)

            v.wait_ge(s_dmat, 80)
            v.wait_ge(s_pj, N_HY)
            v.wait_ge(s_uta, N_HY)
            v.wait_ge(s_utv, N_HY)
            conv(0, g_hy[:, 2])
            v.wait_ge(s_z, 4)
            conv(1, zbuf)
            lr_taps(0)
            v.wait_ge(s_z, 8)
            v.wait_ge(s_hsd, 1)
            link(v.reciprocal(hrs, hsd))
            for i in range(8):
                zz = zbuf[:, i // 2, i % 2, :]
                ins = ts(zz, zz, hrs[:, i:i + 1], None, ALU.mult)
            ins.then_inc(s_hyn, 1)
            v.wait_ge(s_spa, 1)
            e_, r_, s2, q_ = spt[:, 1, :], spt[:, 2, :], spt[:, 3, :], spt[:, 4, :]
            link(ts(r_, e_, 2.0, None, ALU.add))
            link(v.reciprocal(r_, r_))
            link(tt(r_, r_, e_, ALU.mult))
            link(tt(s2, r_, r_, ALU.mult))
            link(ts(q_, s2, 1.0 / 19, 1.0 / 17, ALU.mult, ALU.add))
            for k in (15, 13, 11, 9, 7, 5, 3, 1):
                link(tt(q_, q_, s2, ALU.mult))
                link(ts(q_, q_, 1.0 / k, None, ALU.add))
            link(tt(q_, q_, r_, ALU.mult))
            link(ts(r_, par[:, C_LAM:C_LAM + 4], -1.0, 0.0, ALU.mult, ALU.max))
            link(stt(q_, q_, 2.0, r_, ALU.mult, ALU.add))
            ts(sp8, q_, LRU_C, None, ALU.mult)
            ts(nsp8, q_, -LRU_C, None, ALU.mult).then_inc(s_spv, 1)
            lr_taps(1)

            def scan(q):
                d, c = divmod(q, 2)
                la_, lx_, lt_ = la[:, q % 2, :], lx[:, q % 2, :], lt[:, q % 2, :]
                v.wait_ge(s_lact, 2 * q + 1)
                link(ts(ld, lt_, 1.0, None, ALU.add))
                link(v.reciprocal(ld, ld))
                tt(lt_, lt_, ld, ALU.mult).then_inc(s_lv, 1)
                link(tt(lx_, lx_, xr[:, c, :], ALU.mult))
                v.wait_ge(s_lact, 2 * q + 2)
                link(tt(lx_, lx_, lt_, ALU.mult))
                if d == 0:
                    v.tensor_tensor_scan(hs[:, c, :], la_, lx_, 0.0, ALU.mult, ALU.add).then_inc(s_lv, 1)
                else:
                    link(v.tensor_tensor_scan(ld[:, ::-1], la_[:, ::-1], lx_[:, ::-1], 0.0, ALU.mult, ALU.add))
                    v.wait_ge(s_lv, 2 * c + 2)
                    tt(hs[:, c, :], hs[:, c, :], ld, ALU.add).then_inc(s_lv, 1)
                    v.wait_ge(s_lv, 2 * q + 2)
                    tt(hs[:, c, :], hs[:, c, :], gelu[:, c, :], ALU.mult).then_inc(s_hsg, 1)

            def latent(i, dst, gcol):
                v.wait_ge(*act_read(i))
                ts(dst, bank(proj_bank(i), 2), gcol, None, ALU.mult).then_inc(s_pjv, 1)

            latent(I_KV, ckv[:, 0, :], par[:, C_KVG:C_KVG + 1])
            scan(0)
            latent(I_KV + 1, ckv[:, 1, :], par[:, C_KVG + 1:C_KVG + 2])
            scan(1)
            v.wait_ge(s_rsd, 1)
            link(v.reciprocal(rb, rb))
            for c in range(2):
                ins = tt(ckv[:, c, :], ckv[:, c, :], rb, ALU.mult)
            ins.then_inc(s_rb, 1)
            v.wait_ge(s_rope, 32)
            v.wait_ge(s_krm, 1)
            tt(rtmp2[DV:DQ, :], bank(0, 2, DV, DQ), sin_t[DV:DQ, :], ALU.mult)
            link(tt(kr[DV:DQ, :], kr[DV:DQ, :], cos_t[DV:DQ, :], ALU.mult))
            tt(kr[DV:DQ, :], kr[DV:DQ, :], rtmp2[DV:DQ, :], ALU.add).then_inc(s_kro, 1)
            v.wait_ge(s_kro, 1)
            scan(2)
            for c in range(6):
                latent(I_CQ + c, cq[:, c, :], par[:, C_QG + c:C_QG + c + 1])
                if c == 1:
                    scan(3)
            v.wait_ge(s_rsd, 2)
            link(v.reciprocal(rb, rb))
            for c in range(6):
                ins = tt(cq[:, c, :], cq[:, c, :], rb, ALU.mult)
            ins.then_inc(s_rb, 1)
            v.wait_ge(s_rsd, 3)
            link(v.reciprocal(rb_lru, rb_lru))
            for c in range(2):
                ins = stt(yT_lru[:, c, :], hs[:, c, :], par[:, C_GN + 2 + c:C_GN + 3 + c], rb_lru, ALU.mult, ALU.mult)
            ins.then_inc(s_rb, 1)
            v.wait_ge(s_pj, len(PROJ))
            v.wait_ge(s_kro, 1)
            for b in range(2):
                ins = v.tensor_copy(kh[DV:DQ, b, :], kr[DV:DQ, :])
            ins.then_inc(s_kro, 1)
            for t in range(1, TT, 2):
                v.wait_ge(s_vmm, t + 1)
                v.tensor_copy(v_at[:, t, :], bank(1)).then_inc(s_vv, 1)

            def rope(h, s):
                hh = slice(HALF * s, HALF * s + HALF)
                q, tmp = qh[DV:DQ, h % 2, hh], rtmp[DV:DQ, hh]
                v.wait_ge(s_hp, 6 * h + 3 + s)
                tt(tmp, bank(6, 1, DV, DQ), sin_t[DV:DQ, hh], ALU.mult)
                link(tt(q, q, cos_t[DV:DQ, hh], ALU.mult))
                tt(q, q, tmp, ALU.add).then_inc(s_hpv, 1)

            def row_max(n):
                v.wait_ge(s_qk, n + 1)
                link(v.tensor_reduce(mx[:, n % 2:n % 2 + 1], bank(2 * (n % 2), 2), AX.X, ALU.max))
                ts(nm[:, n % 2:n % 2 + 1], mx[:, n % 2:n % 2 + 1], -SCALE, None, ALU.mult).then_inc(s_nm, 1)

            def probs_copy(n):
                v.wait_ge(s_tr, 2 * n + 2)
                if n >= 2:
                    v.wait_ge(s_pv, n - 1)
                v.tensor_copy(pT[:, n % 2, HALF:], bank(5)).then_inc(s_ptv, 1)

            def output(n):
                h, qt = divmod(n, TT)
                v.wait_ge(s_pv, n + 1)
                link(v.reciprocal(rinv[:, n % 2:n % 2 + 1], rsum[:, n % 4:n % 4 + 1]))
                ts(o_at[:, qt, DV * h:DV * h + DV], bank(7)[:, DV * (n % 2):DV * (n % 2) + DV], rinv[:, n % 2:n % 2 + 1], None, ALU.mult).then_inc(s_ov, 1)

            rope(0, 0)
            rope(0, 1)
            N = NH * TT
            for n in range(N):
                h, qt = divmod(n, TT)
                row_max(n)
                if n >= 1:
                    probs_copy(n - 1)
                if n >= 2:
                    output(n - 2)
                if h + 1 < NH and qt in (3, 4):
                    rope(h + 1, qt - 3)
            probs_copy(N - 1)
            output(N - 2)
            output(N - 1)
            for t in range(TT):
                v.wait_ge(s_osd, t + 1)
                link(v.reciprocal(ars[:, t:t + 1], asd[:, t:t + 1]))
                ts(o_at[:, t, :], o_at[:, t, :], ars[:, t:t + 1], None, ALU.mult).then_inc(s_on, 1)
                if t:
                    o_copy = t - 1
                    v.wait_ge(s_oT, o_copy + 1)
                    tt(yT_at[:, :, P * o_copy:P * o_copy + P], bank(o_copy % 2).rearrange("p (c t) -> p c t", c=4),
                       par[:, C_GN + 4:C_GN + 8].unsqueeze(2).to_broadcast([P, 4, P]), ALU.mult).then_inc(s_oc, 1)
            v.wait_ge(s_oT, TT)
            tt(yT_at[:, :, T - P:], bank((TT - 1) % 2).rearrange("p (c t) -> p c t", c=4),
               par[:, C_GN + 4:C_GN + 8].unsqueeze(2).to_broadcast([P, 4, P]), ALU.mult).then_inc(s_oc, 1)

            def router(i):
                b, b1 = i % 2, i % 2 + 1
                lgt = bank(6)[:, NE * b:NE * b + NE]
                v.wait_ge(s_lg, i + 1)
                if i >= 2:
                    v.wait_ge(s_afT, i - 1)
                v.tensor_reduce(rmx[:, b:b1], lgt, AX.X, ALU.max, negate=True).then_inc(s_rm, 1)
                v.wait_ge(s_re, i + 1)
                link(v.reciprocal(rri[:, b:b1], rsm[:, b:b1]))
                ts(aff[:, b, :], aff[:, b, :], rri[:, b:b1], None, ALU.mult).then_inc(s_aff, 1)

            for i in range(TT + 1):
                if i < TT:
                    b = i % 2
                    x = x1t[:, b, :]
                    v.wait_ge(s_mix, i + 1)
                    v.wait_ge(s_res, i + 1)
                    if i >= 2:
                        v.wait_ge(s_x1st[b], 16 * (i // 2))
                        v.wait_ge(s_acc, i - 1)
                        v.wait_ge(s_x1p, 2 * (i - 1))
                    stt(x, xres[:, b, :], ALPHA, bank(2 * b, 2), ALU.mult, ALU.add).then_inc(s_mixu, 1)
                    v.wait_ge(s_mixu, i + 1)
                    stats(x, st[:, b, :], mv[:, b, :]).then_inc(s_mst, 1)
                    v.wait_ge(s_msd, i + 1)
                    norm_rows(x, sd[:, b:b + 1], rstd[:, b:b + 1], mv[:, b, :]).then_inc(s_mn, 1)
                    v.wait_ge(s_x1p, 2 * i + 2)
                    if i >= 2:
                        v.wait_ge(s_lg, i - 1)
                    v.tensor_copy(x1T[b][:, HALF:], bank(5)).then_inc(s_x1tv, 1)
                if i >= 1:
                    router(i - 1)

            v.wait_ge(s_afc, TT)
            v.wait_ge(s_x1, TT)
            for r in range(CAP // 8):
                best = vals[:, 8 * r:8 * r + 8]
                link(v.max(best, affT))
                link(v.max_index(idxs[:, 8 * r:8 * r + 8], best, affT))
                link(v.match_replace(affT, best, affT, -1.0))
            v.tensor_copy(idxf, idxs).then_inc(s_topk, 1)
            v.wait_ge(s_idxp, 1)
            v.tensor_copy(idx_t, bank(4)[:, 0:NE])
            v.tensor_copy(gate_t, bank(4)[:, NE:2 * NE]).then_inc(s_idxc, 1)

            def xe_copy(e):
                v.wait_ge(s_xep, 2 * e + 2)
                v.tensor_copy(flat(xeT)[:, HALF:], bank(5)).then_inc(s_xev, 1)

            def expert(e, slot, first, last):
                for f in range(2):
                    v.wait_ge(s_sil, 2 * e + f + 1)
                    tt(hid[:, HALF * f:HALF * f + HALF], sil[:, f, :], bank(2 * f + 1), ALU.mult).then_inc(s_hid, 1)
                if not last:
                    xe_copy(e + 1)
                v.wait_ge(s_ht, 2 * e + 2)
                v.tensor_copy(flat(hidT)[:, HALF:], bank(5)).then_inc(s_htv, 1)
                v.wait_ge(s_wcu, WC * e + WC)
                if not first:
                    v.wait_ge(s_sc, 16 * e - 16)
                ts(ye[:, slot, HALF:], bank(7), gate_e[:, slot:slot + 1], None, ALU.mult).then_inc(s_yev, 1)

            xe_copy(0)
            expert(0, 0, True, False)
            expert(1, 1, True, False)
            with v.Fori(2, NE - 2, 2) as e:
                expert(e, 0, False, False)
                expert(e + 1, 1, False, False)
            expert(NE - 2, 0, False, False)
            expert(NE - 1, 1, False, True)

            v.wait_ge(s_gff, 32)
            for i in range(TT):
                x, b = fin[:, i % 3, :], i % 2
                v.wait_ge(s_fx[i % 3], 16 * (i // 3 + 1))
                stats(x, fst[:, b, :], fmv[:, b, :]).then_inc(s_fst, 1)
                v.wait_ge(s_fsd, i + 1)
                link(norm_rows(x, fsd[:, b:b + 1], frs[:, b:b + 1], fmv[:, b, :]))
                tt(x, x, gff, ALU.mult).then_inc(s_fn, 1)


_INS = ["x", "ln_in_g", "ln_in_b", "w_in", "hy_conv_w", "hy_conv_b", "hy_ffn_w1", "hy_ffn_b1", "hy_sin_f1",
        "hy_ffn_w2", "hy_ffn_b2", "hy_sin_f2", "hy_ffn_w3", "hy_skip", "lru_conv_w", "lru_conv_b", "lru_wa", "lru_ba",
        "lru_wx", "lru_bx", "lru_lambda", "mla_q_norm_g", "mla_w_uq", "mla_kv_norm_g", "mla_w_ukv", "group_norm_g",
        "w_out", "ln_mix_g", "ln_mix_b", "router_w", "exp_w_gate", "exp_w_up", "exp_w_down", "ln_ffn_g", "ln_ffn_b"]


def kernel(**inputs):
    import numpy as _np
    import concourse.bacc as _bacc
    from concourse import mybir as _mybir
    from concourse.bass_utils import run_bass_kernel_spmd as _run

    nc = _bacc.Bacc("TRN2", target_bir_lowering=False, num_devices=1)
    given = {name: _np.ascontiguousarray(inputs[name]) for name in _INS}
    given.update(shape_constants())
    arrays = {f"in_{name}": a for name, a in given.items()}
    aps = {name: nc.dram_tensor(f"in_{name}", a.shape, _mybir.dt.from_np(a.dtype), kind="ExternalInput").ap()
           for name, a in given.items()}
    out = nc.dram_tensor("out_0", (1, T, D), F32, kind="ExternalOutput").ap()
    encoder(nc, aps, out)
    r = _run(nc, [arrays], core_ids=[0])
    return r.results[0]["out_0"]
```

```python
import numpy as np
import concourse.bass as bass
from concourse import mybir
from contextlib import ExitStack

F32 = mybir.dt.float32
F32R = mybir.dt.float32r
U32 = mybir.dt.uint32
ALU = mybir.AluOpType
ACT = mybir.ActivationFunctionType
AX = mybir.AxisListType

P = 128
D = 1024
T = 1024
KT = D // P
TT = T // P
HALF = 512
HYW = D // 4
LRW = D // 4
NH, DV, DR = 8, 64, 32
DQ = DV + DR
QL, KVL = 12 * DV, 4 * DV
FFN, POS = 64, 33
NE, CAP = 16, 2 * T // 16
NE2 = 32 + NE
NIN = 3 * HYW + 2 * LRW + QL + KVL + DR
EPS = 1e-5
ALPHA = 2.0 ** 0.25
SCALE = float(DQ) ** -0.5
LRU_C = 8.0
MAGIC = 1.5 * 2.0 ** 23
TWO_PI_HI = 6.28125
TWO_PI_LO = 2.0 * np.pi - 6.28125
PI_IN = 3.1415925

C_HYW, C_HYB, C_LRW, C_LRB = 0, 18, 24, 32
C_BA, C_BX, C_LAM, C_QG, C_KVG = 34, 38, 42, 46, 52
C_GN, C_LG, C_LB, N_PAR = 54, 62, 70, 78


def shape_constants():
    f32 = np.float32
    tab = np.zeros((P, 352), f32)
    tab[:, 0:128] = np.eye(P)
    tab[:, 128:256] = 1.0
    for i in range(DR // 2):
        tab[DV + DR // 2 + i, 256 + DV + i] = 1.0
        tab[DV + i, 256 + DV + DR // 2 + i] = 1.0
    order = np.concatenate([np.arange(0, T, 2), np.arange(1, T, 2)])
    t = np.linspace(0.0, 1.0, T, dtype=f32)[:, None]
    bands = (POS - 1) // 2
    freqs = np.linspace(1e-4, bands - 1, bands, dtype=f32)[None, :]
    ang = (f32(2.0 * np.pi) * np.arange(T, dtype=f32)[:, None] * freqs / f32(T)).astype(f32)
    a64 = ang.astype(np.float64)
    z = np.concatenate([t, np.cos(a64), -np.sin(a64)], axis=-1).astype(f32)
    lo, hi = np.log(1e-2) / 1.5, np.log(1e-2) / 0.3
    deltas = np.abs(np.linspace(lo, hi, HYW, dtype=f32))
    window = np.exp((-t * deltas[None, :]).astype(np.float64)).astype(f32)
    j = np.arange(HALF)
    w = np.pi * (2 * j + 1) / (2.0 * T)
    fall = np.concatenate([w, np.pi - w])
    n = order[:, None]
    tau = (np.arange(HALF) + 0.5)[:, None]
    inv = 1.0 / T
    rope = 10000.0 ** (-np.arange(0, DR, 2, dtype=f32) / f32(DR))
    rang = (np.arange(T, dtype=f32)[:, None] * rope.astype(f32)[None, :]).astype(np.float64).T
    out = {
        "c_tab": tab, "c_pos": z[order].T, "c_win": window[order],
        "c_fc": np.cos(n * w), "c_fs": np.sin(n * w),
        "c_dc": np.cos(tau * fall), "c_ds": np.sin(tau * fall),
        "c_ic": (np.cos(tau * fall) * inv).T, "c_is": (np.sin(tau * fall) * inv).T,
        "c_cos": np.concatenate([np.cos(rang), np.cos(rang)]),
        "c_sin": np.concatenate([-np.sin(rang), np.sin(rang)]),
    }
    return {k: np.ascontiguousarray(v, dtype=f32) for k, v in out.items()}


def encoder(nc, A, out):
    ctx = ExitStack()
    with ctx:
        def sem(name):
            return ctx.enter_context(nc.semaphore(name))

        WORDS, ARENA_AT = 53200, 16512
        arena = nc.alloc_sbuf_tensor_at("arena", [P, WORDS], F32, offset=ARENA_AT)
        psum = ctx.enter_context(nc.psum_tensor("psum", [P, 8 * HALF], F32))

        def mem(at, *dims, p0=0, p1=P):
            n = int(np.prod(dims))
            assert at + n <= WORDS
            return shaped(arena[p0:p1, at:at + n], dims)

        def shaped(v, dims):
            if len(dims) == 2:
                v = v.rearrange("p (a b) -> p a b", a=dims[0])
            elif len(dims) == 3:
                v = v.rearrange("p (a b c) -> p a b c", a=dims[0], b=dims[1])
            elif len(dims) == 4:
                v = v.rearrange("p (a b c d) -> p a b c d", a=dims[0], b=dims[1], c=dims[2])
            return v

        def parts(at, *dims, p1=P):
            n = int(np.prod(dims))
            both = nc.alloc_sbuf_tensor_at(f"split_at_{at}_{dims[-1]}", [P, 2 * n], F32R, offset=ARENA_AT + 4 * at)
            return shaped(both[0:p1, 0:n], dims), shaped(both[0:p1, n:2 * n], dims), shaped(both[0:p1, 0:n].bitcast(F32), dims)

        def bank(b, n=1, p0=0, p1=P):
            return psum[p0:p1, HALF * b:HALF * (b + n)]

        def dram(name, shape):
            return nc.dram_tensor(name, shape, F32, kind="Internal").ap()

        xhat_dram = dram("xhat_scratch", [T, D])
        x1_dram = dram("x1_scratch", [T, D])
        acc_dram = dram("acc_scratch", [T, D])

        ident, ones, rot = mem(0, 128), mem(128, 128), mem(256, 96, p1=DQ)
        par = mem(352, 80)
        w1, w2 = mem(432, FFN, p1=POS), mem(496, FFN, p1=FFN)
        fpar = mem(560, 4, p1=FFN)
        eps, idle = mem(564, 1), mem(596, 2)
        sp8 = mem(566, 4)
        nsp8 = mem(570, 4)
        spt = mem(574, 5, 4)
        st = mem(600, 2, 12)
        mv = mem(624, 2, 2)
        sd = mem(628, 2)
        rstd = mem(630, 2)
        hss = mem(632, 8)
        hsd = mem(640, 8)
        hrs = mem(648, 8)
        mx, nm, rsum, rinv = mem(656, 2), mem(658, 2), mem(660, 4), mem(664, 2)
        ass, asd, ars = mem(666, 8), mem(674, 8), mem(682, 8)
        rmx, rsm, rri = mem(690, 2), mem(692, 2), mem(694, 2)
        aff = mem(784, 4, NE2)
        idxf_t, gate_t = mem(728, NE), mem(744, NE)
        idx_t = mem(760, NE).bitcast(U32)
        idx_e = mem(776, 2).bitcast(U32)
        gate_e = mem(778, 2)
        prow = mem(784, 128, p1=N_PAR)
        frow = mem(912, FFN, p1=4)

        kf = mem(976, 2, 8, 2, HYW)
        xT = mem(9168, KT, T)
        fc, fs = mem(17360, 8, HALF), mem(21456, 8, HALF)
        hf = mem(25552, 8, 2, HALF)
        pos_t, w3 = mem(39888, T, p1=POS), mem(40912, 1024, p1=FFN)
        h1, h2 = mem(41936, T, p1=FFN), mem(42960, T, p1=FFN)
        win = mem(43984, 8, HYW)
        xr_in = mem(46032, 3, D)
        hw = mem(49104, 2, 1024)
        fodd = mem(51152, 2, HALF)
        warg, turns = mem(52176, T, p1=FFN), mem(24528, T, p1=FFN)
        win_w = mem(33744, 3, KT, 256)
        u_hy = mem(39888, 6, T)
        g_hy = mem(46032, 3, 4, 2, HYW)
        dc, ds_ = mem(17360, 4, T), mem(21456, 4, T)
        ic, is_ = mem(25552, 8, HALF), mem(29648, 8, HALF)
        pm = mem(39888, 2, 4, HYW)
        zbuf = mem(41936, 4, 2, HYW)
        yf = mem(43984, 2, HALF)
        t1, t2 = mem(45008, HALF), mem(45520, HALF)
        odd = t1[:, 0:HYW]
        skipb = mem(52176, 2, HYW)
        tsk = mem(37840, 4, 2, HYW)
        xr, gelu = mem(976, 2, T), mem(3024, 2, T)
        rb, rb_lru = mem(5072, T), mem(8144, T)
        cos_t, sin_t = mem(6096, T), mem(7120, T)
        hs = mem(17360, 2, T)
        la, lx, lt = mem(19408, 2, T), mem(21456, 2, T), mem(23504, 2, T)
        ld = mem(25552, T)
        lruw = mem(52176, 8, 128)
        wuq = mem(26576, 6, NH * DQ)
        wukv = mem(31184, 2, 1024)
        cq, ckv = mem(39888, 6, T), mem(46032, 2, T)
        kr = mem(48080, T, p1=DQ)
        sq = mem(49104, T)
        yT_hy = mem(50128, 2, T)
        yT_lru = hs
        v_at, o_at = mem(9168, TT, NH * DV), mem(13264, TT, NH * DV)
        qh, kh = mem(33744, 2, T), mem(35792, 2, T)
        rtmp, rtmp2 = mem(37840, T), mem(25552, T)
        p_at, pT = mem(19408, 2, T), mem(21456, 2, T)
        yT_at = mem(23504, 4, T)
        wout = mem(976, KT, D)
        gin, bin_ = mem(9168, D), mem(10192, D)
        gmix, bmix = mem(11216, D), mem(12240, D)
        xres, x1t = mem(19408, 2, D), mem(21456, 2, D)
        x1T = [mem(27600, D), mem(52176, D)]
        rw = mem(16848, KT, NE)
        accb = mem(13264, 2, D)
        affT = mem(15312, T // 2, p1=NE2)

        WC, WS = 12, 3
        wraw = mem(28624, WC, 4 * HALF)
        wsplit = [parts(16336 + 4096 * i, 4, HALF) for i in range(WS)]
        xe, xeT, hidT = mem(976, 2, D), parts(3024, KT, CAP), parts(7120, KT, CAP)
        sil, hid, ye = mem(5072, 2, HALF), mem(6096, D), mem(9168, 2, D)
        best, idxs = mem(10192, 4, CAP, p1=NE2), mem(10704, CAP, p1=NE2).bitcast(U32)
        pick = mem(10832, 3, NE)
        gff, bff = mem(11216, D), mem(12240, D)
        fin = mem(16336, TT, D)


        s_par, s_wint, s_fmat = sem("params_ld"), sem("window_ld"), sem("filter_mats_ld")
        s_x = [sem(f"x_ld{i}") for i in range(3)]
        s_eps, s_parT, s_parc = sem("eps_set"), sem("params_turned"), sem("params_copied")
        s_fmm, s_arg, s_sin, s_f3 = sem("ffn_psum"), sem("sine_arg"), sem("sine_done"), sem("filter_psum")
        s_hw, s_hab = sem("filter_windowed"), sem("filter_folded")
        s_st, s_sd, s_xn, s_xst, s_xp, s_xT = sem("in_stats"), sem("in_root"), sem("in_normed"), sem("xhat_stored"), sem("x_turned"), sem("xT_done")
        s_dft, s_fodd, s_kf = sem("filter_sums_psum"), sem("filter_odd_copied"), sem("spectra_done")
        s_w = [sem(f"w_in_ld{i}") for i in range(3)]
        s_pj, s_pja, s_pjv = sem("proj_psum"), sem("proj_read_act"), sem("proj_read_dve")
        s_ut, s_uta, s_utv = sem("hyena_turned"), sem("hyena_copied_act"), sem("hyena_copied_dve")
        s_dmat = sem("dft_ld")
        s_fold, s_uf, s_yf, s_yfu = sem("folded"), sem("spectrum_psum"), sem("product_done"), sem("product_used")
        s_inv, s_od, s_z = sem("inverse_psum"), sem("odd_copied"), sem("z_done")
        s_hsd, s_hyn, s_hyT, s_hyc = sem("hyena_root"), sem("hyena_normed"), sem("hyena_back_psum"), sem("hyena_out")
        s_zero, s_lw, s_spa, s_spv = sem("zeroed"), sem("lru_w_ld"), sem("softplus_exp"), sem("softplus_done")
        s_gmm, s_gact, s_lact, s_lv, s_hsg = sem("gates_psum"), sem("gates_read"), sem("lru_act"), sem("lru_dve"), sem("lru_gated")
        s_sq, s_ssq, s_rsd, s_rb = sem("squares"), sem("squares_summed"), sem("rms_root"), sem("rms_applied")
        s_mw, s_rope, s_krm, s_kro = sem("mla_w_ld"), sem("rope_ld"), sem("kr_partner_psum"), sem("kr_roped")
        s_vmm, s_va, s_vv = sem("v_psum"), sem("v_copied_act"), sem("v_copied_dve")
        s_hp, s_hpa, s_hpv = sem("head_proj_psum"), sem("head_proj_act"), sem("head_proj_dve")
        s_qk, s_nm, s_exp, s_tr = sem("scores_psum"), sem("neg_max"), sem("exp_done"), sem("probs_turned")
        s_pta, s_ptv, s_pv, s_ov = sem("probsT_act"), sem("probsT_dve"), sem("pv_psum"), sem("o_done")
        s_osd, s_on, s_oT, s_oc = sem("o_root"), sem("o_normed"), sem("o_turned"), sem("yT_at_done")
        s_wo, s_gb, s_rw, s_gff = sem("w_out_ld"), sem("gains_ld"), sem("router_w_ld"), sem("ffn_gains_ld")
        s_xh = [sem(f"xhat_ld{i}") for i in range(2)]
        s_res, s_mix, s_mixu, s_mst, s_msd, s_x1 = sem("residual"), sem("mix_psum"), sem("mix_read"), sem("mix_stats"), sem("mix_root"), sem("x1_done")
        s_x1st, s_acst, s_acc = [sem(f"x1_stored{i}") for i in range(2)], [sem(f"acc_stored{i}") for i in range(2)], sem("acc_scaled")
        s_x1p, s_x1ta, s_x1tv, s_lg = sem("x1_turned"), sem("x1T_act"), sem("x1T_dve"), sem("logits")
        s_rm, s_re, s_aff, s_afT = sem("router_max"), sem("router_exp"), sem("affinity"), sem("affinity_turned")
        s_topk, s_idxp, s_idxc = sem("topk_done"), sem("idx_turned"), sem("idx_ready")
        s_wc, s_wcu = [sem(f"expert_w_ld{c}") for c in range(WC)], sem("expert_w_used")
        s_ie, s_xe = sem("expert_idx"), [sem(f"xe_gathered{i}") for i in range(2)]
        s_xep, s_xea, s_xev = sem("xe_turned"), sem("xeT_act"), sem("xeT_dve")
        s_whi, s_wlo = sem("expert_w_high"), sem("expert_w_split")
        s_sil, s_hid = sem("silu_done"), sem("hidden_done")
        s_ht, s_hta, s_htv = sem("hid_turned"), sem("hidT_act"), sem("hidT_dve")
        s_yea, s_yev, s_sc = sem("ye_act"), sem("ye_dve"), sem("scattered")
        s_fx, s_out = s_wc[0:TT], sem("out_stored")
        s_fst, s_fsd, s_fo = sem("final_stats"), sem("final_root"), sem("final_done")
        s_dve, s_act, s_pool = sem("dve_chain"), sem("act_chain"), sem("pool_chain")

        def links(eng, chain):
            count = [0]

            def link(ins):
                count[0] += 1
                ins.then_inc(chain, 1)
                eng.wait_ge(chain, count[0])
            return link

        def tokens(ap):
            return ap.rearrange("(t p) d -> p t d", p=P)

        def rows(ap):
            return ap.rearrange("(k p) n -> p k n", p=P)

        def flat(ap3):
            return ap3.rearrange("p a b -> p (a b)")

        def reverse(m, a, b):
            return u_hy[:, m, T - 1 - a:T - 1 - b:-1]

        w_in = rows(A["w_in"][0])
        x_tok, xh_tok, x1_tok, acc_tok = tokens(A["x"][0]), tokens(xhat_dram), tokens(x1_dram), tokens(acc_dram)
        out_tok = tokens(out[0])

        LR0, CQ0, KV0, KR0 = 3 * HYW, 3 * HYW + 2 * LRW, 3 * HYW + 2 * LRW + QL, 3 * HYW + 2 * LRW + QL + KVL
        PROJ = ([(P * m, P) for m in range(10)] + [(KV0 + P * m, P) for m in range(2)] + [(KR0, DR)]
                + [(CQ0 + P * m, P) for m in range(6)])
        N_HY, I_LR, I_LG, I_KV, I_KR, I_CQ = 6, 6, 8, 10, 12, 13
        CHUNKS = [(256 * c, 256) for c in range(5)] + [(KV0, 256), (KR0, DR)] + [(CQ0 + 256 * c, 256) for c in range(3)]
        LAST = [1, 3, 5, 7, 9, 11, 12, 14, 16, 18]

        def chunk_of(i):
            return min(c for c in range(len(CHUNKS)) if LAST[c] >= i)

        def proj_bank(i):
            return 2 * (i % 2) if i < N_HY else 6 if i < I_LG else 4 + 2 * (i % 2)

        def proj_before(i):
            return max([j for j in range(i) if proj_bank(j) == proj_bank(i)], default=None)

        def dve_reads(i):
            return sum(j not in (I_LG, I_LG + 1, I_KR) for j in range(i + 1))

        def act_read(i):
            if i in (I_KV, I_KV + 1):
                return s_sq, i - I_KV + 1
            return (s_sq, i - I_CQ + 3) if i >= I_CQ else (s_pja, min(i, I_KV) + 1)

        block = ctx.enter_context(nc.Block())

        @block.sync
        def _(sp):
            sp.dma_start(mem(0, 352), A["c_tab"]).then_inc(s_par, 16)
            for at, src in ((C_HYW, A["hy_conv_w"][0].rearrange("k (m p) -> (k m) p", p=P)),
                            (C_HYB, A["hy_conv_b"][0].rearrange("(m p) -> m p", p=P)),
                            (C_LRW, A["lru_conv_w"][0].rearrange("k (m p) -> (k m) p", p=P)),
                            (C_LRB, A["lru_conv_b"][0].rearrange("(m p) -> m p", p=P)),
                            (C_BA, A["lru_ba"][0].rearrange("k (m p) -> (k m) p", p=P)),
                            (C_BX, A["lru_bx"][0].rearrange("k (m p) -> (k m) p", p=P)),
                            (C_LAM, A["lru_lambda"][0].rearrange("k (m p) -> (k m) p", p=P)),
                            (C_QG, A["mla_q_norm_g"][0].rearrange("(m p) -> m p", p=P)),
                            (C_KVG, A["mla_kv_norm_g"][0].rearrange("(m p) -> m p", p=P)),
                            (C_GN, A["group_norm_g"][0].rearrange("(m p) -> m p", p=P)),
                            (C_LG, A["ln_in_g"].rearrange("(m p) -> m p", p=P)),
                            (C_LB, A["ln_in_b"].rearrange("(m p) -> m p", p=P))):
                sp.dma_start(prow[at:at + src.shape[0], :], src).then_inc(s_par, 16)
            for i, name in enumerate(("hy_ffn_b1", "hy_sin_f1", "hy_ffn_b2", "hy_sin_f2")):
                sp.dma_start(frow[i:i + 1, :], A[name]).then_inc(s_par, 16)
            sp.dma_start(pos_t, A["c_pos"]).then_inc(s_par, 16)
            sp.dma_start(w1, A["hy_ffn_w1"][0]).then_inc(s_par, 16)
            sp.dma_start(w2, A["hy_ffn_w2"][0]).then_inc(s_par, 16)
            sp.dma_start(w3, A["hy_ffn_w3"][0]).then_inc(s_par, 16)
            for i in range(3):
                sp.dma_start(xr_in[:, i, :], x_tok[:, i, :]).then_inc(s_x[i], 16)
            sp.dma_start(win, rows(A["c_win"])).then_inc(s_wint, 16)
            for i in range(TT):
                sp.wait_ge(s_xn, i + 1)
                sp.dma_start(xh_tok[:, i, :], xr_in[:, i % 3, :]).then_inc(s_xst, 16)
                if i + 3 < TT:
                    sp.wait_ge(s_xst, 16 * (i + 1))
                    sp.wait_ge(s_xp, i + 1)
                    sp.dma_start(xr_in[:, i % 3, :], x_tok[:, i + 3, :]).then_inc(s_x[i % 3], 16)
                if i == 1:
                    sp.dma_start(fc, rows(A["c_fc"])).then_inc(s_fmat, 16)
                    sp.dma_start(fs, rows(A["c_fs"])).then_inc(s_fmat, 16)

            def load_w(c):
                c0, w = CHUNKS[c]
                if c >= 3:
                    sp.wait_ge(s_pj, LAST[c - 3] + 1)
                sp.dma_start(win_w[:, c % 3, :, 0:w], w_in[:, :, c0:c0 + w]).then_inc(s_w[c % 3], 16)

            for c in range(3):
                load_w(c)
            sp.wait_ge(s_dft, 4)
            for dst, name in ((dc, "c_dc"), (ds_, "c_ds"), (ic, "c_ic"), (is_, "c_is")):
                sp.dma_start(dst, rows(A[name])).then_inc(s_dmat, 16)
            sp.wait_ge(s_sin, 4)
            sp.dma_start(skipb, A["hy_skip"][0].partition_broadcast(P)).then_inc(s_dmat, 16)
            load_w(3)
            load_w(4)
            sp.wait_ge(s_inv, 8)
            sp.dma_start(wuq, rows(A["mla_w_uq"][0])).then_inc(s_mw, 16)
            sp.dma_start(wukv, rows(A["mla_w_ukv"][0])).then_inc(s_mw, 16)
            sp.wait_ge(s_z, 8)
            sp.dma_start(cos_t[DV:DQ, :], A["c_cos"]).then_inc(s_rope, 16)
            sp.dma_start(sin_t[DV:DQ, :], A["c_sin"]).then_inc(s_rope, 16)
            load_w(5)
            sp.wait_ge(s_zero, 1)
            for d in range(2):
                for g, name in enumerate(("lru_wa", "lru_wx")):
                    for c in range(2):
                        for b in range(2):
                            sp.dma_start(lruw[64 * b:64 * b + 64, 4 * d + 2 * g + c, 64 * b:64 * b + 64],
                                         A[name][0, d, 2 * c + b]).then_inc(s_lw, 16)
            for c in range(6, len(CHUNKS)):
                load_w(c)
            sp.wait_ge(s_hpv, 2 * NH)
            sp.wait_ge(s_hpa, 4 * NH)
            sp.dma_start(wout, rows(A["w_out"][0])).then_inc(s_wo, 16)
            sp.wait_ge(s_pv, NH * TT)
            for dst, src in ((gin, A["ln_in_g"]), (bin_, A["ln_in_b"]), (gmix, A["ln_mix_g"][0]), (bmix, A["ln_mix_b"][0])):
                sp.dma_start(dst, src.partition_broadcast(P)).then_inc(s_gb, 16)
            for i in range(2):
                sp.dma_start(xres[:, i, :], xh_tok[:, i, :]).then_inc(s_xh[i], 16)
            sp.wait_ge(s_oT, TT)
            sp.dma_start(rw, rows(A["router_w"][0])).then_inc(s_rw, 16)

            def load_chunk(e, c):
                if c < 8:
                    half, kind, k = c // 4, ("exp_w_gate", "exp_w_up")[c % 4 // 2], c % 2
                else:
                    half, kind, k = c % 2, "exp_w_down", (c - 8) // 2
                w = A[kind][0]
                w = w[e] if isinstance(e, int) else w[bass.ds(e, 1)].rearrange("a k n -> (a k) n")
                src = w[HALF * k:HALF * k + HALF, HALF * half:HALF * half + HALF]
                sp.dma_start(wraw[:, c].rearrange("p (k n) -> p k n", k=4), rows(src)).then_inc(s_wc[c], 16)

            for c in range(10):
                load_chunk(0, c)
            for i in range(TT):
                sp.wait_ge(s_x1, i + 1)
                sp.dma_start(x1_tok[:, i, :], x1t[:, i % 2, :]).then_inc(s_x1st[i % 2], 16)
                if i + 2 < TT:
                    sp.wait_ge(s_mixu, i + 1)
                    sp.dma_start(xres[:, i % 2, :], xh_tok[:, i + 2, :]).then_inc(s_xh[i % 2], 16)
            sp.wait_ge(s_lg, TT)
            for c in (10, 11):
                load_chunk(0, c)
            for dst, name in ((gff, "ln_ffn_g"), (bff, "ln_ffn_b")):
                sp.dma_start(dst, A[name][0].partition_broadcast(P)).then_inc(s_gff, 16)
            with sp.Fori(1, NE) as e:
                for c in range(WC):
                    sp.wait_ge(s_wlo, WC * e + (c + 1 - WC))
                    load_chunk(e, c)
            sp.wait_ge(s_sc, 16 * NE)
            for i in range(TT):
                sp.dma_start(fin[:, i, :], acc_tok[:, i, :]).then_inc(s_fx[i], 16)
            for i in range(TT):
                sp.wait_ge(s_fo, i + 1)
                sp.dma_start(out_tok[:, i, :], fin[:, i, :]).then_inc(s_out, 16)
            sp.wait_ge(s_out, 16 * TT)

        @block.gpsimd
        def _(pool):
            link = links(pool, s_pool)
            pool.memset(eps, EPS).then_inc(s_eps, 1)
            for nt in range(8):
                pool.wait_ge(s_hw, nt + 1)
                fwd, bwd = hw[:, nt % 2, 0:HALF], hw[:, nt % 2, HALF:]
                if nt == 0:
                    link(pool.memset(bwd[0:1, :], 0.0))
                pool.tensor_tensor(hf[:, nt, 0, :], fwd, bwd, ALU.add)
                pool.tensor_tensor(hf[:, nt, 1, :], fwd, bwd, ALU.subtract).then_inc(s_hab, 1)
            pool.wait_ge(s_z, 8)
            pool.memset(lruw, 0.0).then_inc(s_zero, 1)
            pool.memset(kr[0:DV, :], 0.0).then_inc(s_zero, 1)
            pool.wait_ge(s_gb, 64)
            for i in range(TT):
                res = xres[:, i % 2, :]
                pool.wait_ge(s_xh[i % 2], 16 * (i // 2 + 1))
                link(pool.tensor_tensor(res, res, gin, ALU.mult))
                pool.tensor_tensor(res, res, bin_, ALU.add).then_inc(s_res, 1)

            def gather(e, slot):
                copied, col = 2 * e + 2, slice(e, e + 1) if isinstance(e, int) else bass.ds(e, 1)
                pool.tensor_copy(idx_e[:, slot:slot + 1], idx_t[:, col]).then_inc(s_ie, 1)
                pool.tensor_copy(gate_e[:, slot:slot + 1], gate_t[:, col]).then_inc(s_ie, 1)
                pool.wait_ge(s_ie, copied)
                if not isinstance(e, int):
                    pool.tensor_tensor(idle[:, 0:1], eps, eps, ALU.add)
                pool.indirect_dma_start(xe[:, slot, :], None, x1_dram,
                                        bass.IndirectOffsetOnAxis(ap=idx_e[:, slot:slot + 1], axis=0)).then_inc(s_xe[slot], 16)

            def scatter(e, slot):
                pool.wait_ge(s_yea, e + 1)
                pool.wait_ge(s_yev, e + 1)
                if not isinstance(e, int):
                    pool.tensor_tensor(idle[:, 1:2], eps, eps, ALU.add)
                pool.indirect_dma_start(acc_dram, bass.IndirectOffsetOnAxis(ap=idx_e[:, slot:slot + 1], axis=0),
                                        ye[:, slot, :], None, compute_op=ALU.add).then_inc(s_sc, 16)

            for i in range(2):
                pool.wait_ge(s_x1st[i], 16 * TT // 2)
                pool.wait_ge(s_acst[i], 16 * TT // 2)
            pool.wait_ge(s_idxc, 1)
            gather(0, 0)
            gather(1, 1)
            scatter(0, 0)
            pool.wait_ge(s_sc, 16)
            gather(2, 0)
            scatter(1, 1)
            with pool.Fori(2, NE - 2, 2) as e:
                for n, slot in ((e, 0), (e + 1, 1)):
                    pool.wait_ge(s_sc, 16 * n)
                    pool.wait_ge(s_xep, 2 * n + 2)
                    gather(n + 1, 1 - slot)
                    scatter(n, slot)
            pool.wait_ge(s_sc, 16 * (NE - 2))
            gather(NE - 1, 1)
            scatter(NE - 2, 0)
            pool.wait_ge(s_sc, 16 * (NE - 1))
            scatter(NE - 1, 1)

        @block.scalar
        def _(act):
            link = links(act, s_act)
            a = act.activation

            def sines(layer):
                for j in range(2):
                    act.wait_ge(s_arg, 2 * layer + j + 1)
                    h = slice(HALF * j, HALF * j + HALF)
                    a((h1, h2)[layer][:, h], warg[:, h], ACT.Sin).then_inc(s_sin, 1)

            def in_root(i):
                act.wait_ge(s_st, i + 1)
                a(sd[:, i % 2:i % 2 + 1], mv[:, i % 2, 1:2], ACT.Sqrt, bias=eps).then_inc(s_sd, 1)

            def x_copy(i):
                act.wait_ge(s_xp, i + 1)
                src = bank(4 + 2 * (i % 2), 2)
                for k in range(KT):
                    ins = a(xT[:, k, P * i:P * i + P], src[:, P * k:P * k + P], ACT.Identity,
                            scale=par[:, C_LG + k:C_LG + k + 1], bias=par[:, C_LB + k:C_LB + k + 1])
                ins.then_inc(s_xT, 1)

            act.wait_ge(s_eps, 1)
            act.wait_ge(s_parc, 2)
            sines(0)
            in_root(0)
            sines(1)
            for i in range(TT):
                if i + 1 < TT:
                    in_root(i + 1)
                x_copy(i)

            for jt in range(4):
                act.wait_ge(s_dft, jt + 1)
                if jt:
                    act.wait_ge(s_kf, 4 * jt)
                a(fodd[:, 0, :], bank(4 * (jt % 2) + 1), ACT.Copy).then_inc(s_fodd, 1)
                a(fodd[:, 1, :], bank(4 * (jt % 2) + 3), ACT.Copy).then_inc(s_fodd, 1)

            def hy_copy(m):
                act.wait_ge(s_ut, 2 * m + 1)
                a(g_hy[:, m // 2, :, 0, P * (m % 2):P * (m % 2) + P],
                  bank(4).rearrange("p (i c) -> p i c", i=4), ACT.Copy).then_inc(s_uta, 1)

            act.wait_ge(s_xst, 16 * TT)
            for m in range(N_HY):
                act.wait_ge(s_pj, m + 1)
                y = bank(proj_bank(m), 2)
                for dst, src in ((u_hy[:, m, 0:HALF], y[:, HALF:]), (reverse(m, 0, HALF), y[:, 0:HALF])):
                    ins = a(dst, src, ACT.Identity, scale=par[:, C_HYW + 6 + m:C_HYW + 7 + m], bias=par[:, C_HYB + m:C_HYB + m + 1])
                ins.then_inc(s_pja, 1)
                if m:
                    hy_copy(m - 1)
            hy_copy(N_HY - 1)

            def odd_copies(o):
                for i in range(4):
                    act.wait_ge(s_inv, 4 * o + i + 1)
                    if i or o:
                        act.wait_ge(s_z, 4 * o + i)
                    a(odd, bank(i)[:, HYW:], ACT.Copy).then_inc(s_od, 1)

            def lr_centre(c):
                act.wait_ge(s_pj, I_LR + c + 1)
                a(xr[:, c, :], bank(6, 2), ACT.Identity, scale=par[:, C_LRW + 4 + c:C_LRW + 5 + c],
                  bias=par[:, C_LRB + c:C_LRB + c + 1]).then_inc(s_pja, 1)

            odd_copies(0)
            lr_centre(0)
            odd_copies(1)
            act.wait_ge(s_z, 8)
            for i in range(8):
                link(a(odd, zbuf[:, i // 2, i % 2, :], ACT.Square, accum_out=hss[:, i:i + 1]))
            a(hsd, hss, ACT.Sqrt, scale=1.0 / HYW, bias=eps).then_inc(s_hsd, 1)
            link(a(spt[:, 0, :], par[:, C_LAM:C_LAM + 4], ACT.Abs))
            a(spt[:, 1, :], spt[:, 0, :], ACT.Exp, scale=-1.0).then_inc(s_spa, 1)
            lr_centre(1)
            for c in range(2):
                act.wait_ge(s_pj, I_LG + c + 1)
                a(gelu[:, c, :], bank(proj_bank(I_LG + c), 2), ACT.Gelu_apprx_tanh).then_inc(s_pja, 1)
            for c in range(2):
                act.wait_ge(s_hyT, c + 1)
                gcol = par[:, C_GN + c:C_GN + c + 1]
                a(yT_hy[:, c, HALF:T], bank(2 * c), ACT.Copy, scale=gcol)
                a(yT_hy[:, c, HALF - 1::-1], bank(2 * c + 1), ACT.Copy, scale=gcol).then_inc(s_hyc, 1)

            def gates(q):
                la_, lx_, lt_ = la[:, q % 2, :], lx[:, q % 2, :], lt[:, q % 2, :]
                if q == 0:
                    act.wait_ge(s_spv, 1)
                if q >= 2:
                    act.wait_ge(s_lv, 2 * (q - 1))
                for j in range(2):
                    act.wait_ge(s_gmm, 2 * q + j + 1)
                    h = slice(HALF * j, HALF * j + HALF)
                    a(lx_[:, h], bank(1), ACT.Sigmoid, bias=par[:, C_BX + q:C_BX + q + 1])
                    a(lt_[:, h], bank(0), ACT.Sigmoid, bias=par[:, C_BA + q:C_BA + q + 1]).then_inc(s_gact, 1)
                act.wait_ge(s_gact, 2 * q + 2)
                a(la_, lt_, ACT.Exp, scale=nsp8[:, q:q + 1])
                a(lt_, lt_, ACT.Tanh, scale=sp8[:, q:q + 1]).then_inc(s_lact, 1)
                act.wait_ge(s_lv, 2 * q + 1)
                a(lt_, lt_, ACT.Sqrt, scale=2.0).then_inc(s_lact, 1)

            def squares(i, n):
                act.wait_ge(s_pj, i + 1)
                if n:
                    act.wait_ge(s_ssq, n)
                a(sq, bank(proj_bank(i), 2), ACT.Square).then_inc(s_sq, 1)

            def rms_root(dst, n, k):
                act.wait_ge(s_ssq, n)
                a(dst, bank(2, 2), ACT.Sqrt, scale=1.0 / k, bias=eps).then_inc(s_rsd, 1)

            squares(I_KV, 0)
            gates(0)
            squares(I_KV + 1, 1)
            gates(1)
            rms_root(rb, 2, KVL)
            act.wait_ge(s_pj, I_KR + 1)
            act.wait_ge(s_zero, 2)
            a(kr[DV:DQ, :], bank(proj_bank(I_KR), 2, DV, DQ), ACT.Copy).then_inc(s_pja, 1)
            gates(2)
            squares(I_CQ, 2)
            squares(I_CQ + 1, 3)
            gates(3)
            for c in range(2, 6):
                squares(I_CQ + c, 2 + c)
            act.wait_ge(s_rb, 1)
            rms_root(rb, 8, QL)
            for c in range(2):
                act.wait_ge(s_hsg, c + 1)
                act.wait_ge(s_ssq, 8 + c)
                a(sq, hs[:, c, :], ACT.Square).then_inc(s_sq, 1)
            rms_root(rb_lru, 10, LRW)

            for t in range(0, TT, 2):
                act.wait_ge(s_vmm, t + 1)
                a(v_at[:, t, :], bank(0), ACT.Copy).then_inc(s_va, 1)

            def head_copy(h, s):
                act.wait_ge(s_hp, 6 * h + s + 1)
                if h >= 2 and s == 0:
                    act.wait_ge(s_qk, TT * (h - 1))
                dst, p1 = (qh, DQ) if s < 2 else (kh, DV)
                a(dst[0:p1, h % 2, HALF * (s % 2):HALF * (s % 2) + HALF], bank(6, p1=p1), ACT.Copy).then_inc(s_hpa, 1)

            def probs_copy(n):
                act.wait_ge(s_tr, 2 * n + 1)
                if n >= 2:
                    act.wait_ge(s_pv, n - 1)
                a(pT[:, n % 2, 0:HALF], bank(4), ACT.Copy).then_inc(s_pta, 1)

            for s in (0, 1, 4, 5):
                head_copy(0, s)
            for n in range(NH * TT):
                h, qt = divmod(n, TT)
                act.wait_ge(s_nm, n + 1)
                if n >= 2:
                    act.wait_ge(s_tr, 2 * (n - 1))
                a(p_at[:, n % 2, :], bank(2 * (n % 2), 2), ACT.Exp, scale=SCALE, bias=nm[:, n % 2:n % 2 + 1],
                  accum_out=rsum[:, n % 4:n % 4 + 1]).then_inc(s_exp, 1)
                if n >= 1:
                    probs_copy(n - 1)
                if h + 1 < NH and qt in (1, 2, 5, 6):
                    head_copy(h + 1, qt - 1)
            probs_copy(NH * TT - 1)
            for t in range(TT):
                act.wait_ge(s_ov, NH * TT - TT + t + 1)
                link(a(sq[:, 0:HALF], o_at[:, t, :], ACT.Square, accum_out=ass[:, t:t + 1]))
                a(asd[:, t:t + 1], ass[:, t:t + 1], ACT.Sqrt, scale=1.0 / (NH * DV), bias=eps).then_inc(s_osd, 1)

            def router_exp(i):
                act.wait_ge(s_rm, i + 1)
                a(aff[:, i % 4, 32 * (i // 4):32 * (i // 4) + NE], bank(6)[:, NE * (i % 2):NE * (i % 2) + NE], ACT.Exp, bias=rmx[:, i % 2:i % 2 + 1],
                  accum_out=rsm[:, i % 2:i % 2 + 1]).then_inc(s_re, 1)

            for i in range(TT + 1):
                if i < TT:
                    act.wait_ge(s_mst, i + 1)
                    a(sd[:, i % 2:i % 2 + 1], mv[:, i % 2, 1:2], ACT.Sqrt, bias=eps).then_inc(s_msd, 1)
                    act.wait_ge(s_x1, i + 1)
                    if i >= 2:
                        act.wait_ge(s_acst[i % 2], 16 * (i // 2))
                    else:
                        act.wait_ge(s_oT, TT)
                    a(accb[:, i % 2, :], x1t[:, i % 2, :], ACT.Copy, scale=ALPHA).then_inc(s_acc, 1)
                    act.wait_ge(s_acc, i + 1)
                    act.dma_start(acc_tok[:, i, :], accb[:, i % 2, :]).then_inc(s_acst[i % 2], 16)
                    act.wait_ge(s_x1p, 2 * i + 1)
                    if i >= 2:
                        act.wait_ge(s_lg, i - 1)
                    a(x1T[i % 2][:, 0:HALF], bank(4), ACT.Copy).then_inc(s_x1ta, 1)
                if 1 <= i <= TT:
                    router_exp(i - 1)

            def high(e, c):
                act.wait_ge(s_wc[c], 16 * e + 16)
                if not (isinstance(e, int) and WC * e + c < WS):
                    act.wait_ge(s_wcu, WC * e + (c + 1 - WS))
                a(flat(wsplit[c % WS][0]), wraw[:, c], ACT.Copy).then_inc(s_whi, 1)

            def turned(dst, b, bank_, event, n, done):
                act.wait_ge(event, n)
                a(flat(dst[0])[:, HALF * b:HALF * b + HALF], bank(bank_), ACT.Copy).then_inc(done, 1)

            def expert(e, slot, first, last):
                for c in range(WC):
                    if c + 2 < WC or not last:
                        high(e + (c + 2) // WC, (c + 2) % WC)
                    if c in (1, 5):
                        act.wait_ge(s_wcu, WC * e + (c + 1))
                        a(sil[:, c // 4, :], bank(c // 2), ACT.Silu).then_inc(s_sil, 1)
                    if c in (5, 8):
                        turned(hidT, c // 8, 4, s_ht, 2 * e + c // 8 + 1, s_hta)
                    if c in (7, 9) and not last:
                        turned(xeT, c // 9, 5, s_xep, 2 * e + 2 + c // 9 + 1, s_xea)
                    if c == 10:
                        act.wait_ge(s_wcu, WC * e + 11)
                        if not first:
                            act.wait_ge(s_sc, 16 * e - 16)
                        a(ye[:, slot, 0:HALF], bank(6), ACT.Copy, scale=gate_e[:, slot:slot + 1]).then_inc(s_yea, 1)

            for i in range(2):
                act.wait_ge(s_x1st[i], 16 * TT // 2)
            act.wait_ge(s_lg, TT)
            high(0, 0)
            high(0, 1)
            act.wait_ge(s_idxc, 1)
            for b in range(2):
                turned(xeT, b, 4 + b, s_xep, b + 1, s_xea)
            expert(0, 0, True, False)
            expert(1, 1, True, False)
            with act.Fori(2, NE - 2, 2) as e:
                expert(e, 0, False, False)
                expert(e + 1, 1, False, False)
            expert(NE - 2, 0, False, False)
            expert(NE - 1, 1, False, True)
            for i in range(TT):
                act.wait_ge(s_fst, i + 1)
                a(sd[:, i % 2:i % 2 + 1], mv[:, i % 2, 1:2], ACT.Sqrt, bias=eps).then_inc(s_fsd, 1)

        @block.tensor
        def _(pe):
            mm = pe.matmul
            pe.wait_ge(s_par, 16 * 21)
            pe.transpose(bank(0)[:, 0:N_PAR], prow, ident[0:N_PAR, 0:N_PAR]).then_inc(s_parT, 1)
            pe.transpose(bank(1, p1=FFN)[:, 0:4], frow, ident[0:4, 0:4]).then_inc(s_parT, 1)
            pe.wait_ge(s_parc, 2)
            for j in range(2):
                mm(bank(j, p1=FFN), w1, pos_t[:, HALF * j:HALF * j + HALF], start=True, stop=True).then_inc(s_fmm, 1)
            for j in range(2):
                pe.wait_ge(s_sin, j + 1)
                mm(bank(j, p1=FFN), w2, h1[:, HALF * j:HALF * j + HALF], start=True, stop=True).then_inc(s_fmm, 1)

            def x_turn(i):
                pe.wait_ge(s_xn, i + 1)
                if i >= 2:
                    pe.wait_ge(s_xT, i - 1)
                for k in range(KT):
                    ins = pe.transpose(bank(4 + 2 * (i % 2), 2)[:, P * k:P * k + P], xr_in[:, i % 3, P * k:P * k + P], ident)
                ins.then_inc(s_xp, 1)

            for nt in range(8):
                if nt == 0:
                    pe.wait_ge(s_sin, 4)
                else:
                    pe.wait_ge(s_hw, max(nt - 1, 1))
                for d in range(2):
                    ins = mm(bank(2 * (nt % 2) + d), h2[:, P * nt:P * nt + P], w3[:, HALF * d:HALF * d + HALF], start=True, stop=True)
                ins.then_inc(s_f3, 1)
                x_turn(nt)

            pe.wait_ge(s_fmat, 32)
            pe.wait_ge(s_hab, 8)
            pe.wait_ge(s_hw, 8)
            pe.wait_ge(s_xT, TT)
            for jt in range(4):
                if jt >= 2:
                    pe.wait_ge(s_kf, 4 * (jt - 1))
                for b, (mat, part) in enumerate(((fc, 0), (fc, 0), (fs, 1), (fs, 1))):
                    for n in range(4):
                        nt = 4 * (b % 2) + n
                        ins = mm(bank(4 * (jt % 2) + b), mat[:, nt, P * jt:P * jt + P], hf[:, nt, part, :], start=(n == 0), stop=(n == 3))
                ins.then_inc(s_dft, 1)

            def project(i):
                c = chunk_of(i)
                c0, w = PROJ[i]
                at = c0 - CHUNKS[c][0]
                p0 = DV if i == I_KR else 0
                pe.wait_ge(s_w[c % 3], 16 * (c // 3 + 1))
                before = proj_before(i)
                if before is not None:
                    pe.wait_ge(*act_read(before))
                    pe.wait_ge(s_pjv, dve_reads(before))
                for k in range(KT):
                    for j in range(2):
                        ins = mm(bank(proj_bank(i) + j, 1, p0, p0 + w), win_w[:, c % 3, k, at:at + w], xT[:, k, HALF * j:HALF * j + HALF],
                                 start=(k == 0), stop=(k == KT - 1))
                ins.then_inc(s_pj, 1)

            def hy_turn(m):
                pe.wait_ge(s_pjv, m + 1)
                for half in range(2):
                    if m:
                        pe.wait_ge((s_uta, s_utv)[half], m)
                    for i in range(4):
                        t0 = HALF * half + P * i
                        ins = pe.transpose(bank(4 + half)[:, P * i:P * i + P], u_hy[:, m, t0:t0 + P], ident)
                    ins.then_inc(s_ut, 1)

            pe.wait_ge(s_kf, 16)
            for m in range(N_HY):
                project(m)
                if m:
                    hy_turn(m - 1)
            hy_turn(N_HY - 1)

            def conv(o):
                if o == 0:
                    pe.wait_ge(s_dmat, 80)
                    pe.wait_ge(s_uta, N_HY)
                    pe.wait_ge(s_utv, N_HY)
                pe.wait_ge(s_fold, o + 1)
                for f in range(9):
                    if f < 8:
                        if f >= 2 or o:
                            pe.wait_ge(s_yf, 8 * o + f - 1 if f >= 2 else 8)
                        for part, mat in enumerate((dc, ds_)):
                            for i in range(4):
                                ins = mm(bank(4 + f % 2)[:, HYW * part:HYW * part + HYW], mat[:, i, P * f:P * f + P], pm[:, part, i, :],
                                         start=(i == 0), stop=(i == 3))
                        ins.then_inc(s_uf, 1)
                    if f:
                        g = f - 1
                        if g == 0 and o:
                            pe.wait_ge(s_z, 4)
                        pe.wait_ge(s_yf, 8 * o + g + 1)
                        for i in range(4):
                            mm(bank(i)[:, 0:HYW], ic[:, g, P * i:P * i + P], yf[:, g % 2, 0:HYW], start=(g == 0), stop=(g == 7), skip_group_check=True)
                            ins = mm(bank(i)[:, HYW:], is_[:, g, P * i:P * i + P], yf[:, g % 2, HYW:], start=False, stop=(g == 7), skip_group_check=True)
                            if g == 7:
                                ins.then_inc(s_inv, 1)
                        if g < 7:
                            ins.then_inc(s_yfu, 1)

            pe.wait_ge(s_pja, N_HY)
            conv(0)
            project(I_LR)
            conv(1)
            pe.wait_ge(s_yf, 16)
            for i in range(I_LR + 1, I_KV):
                project(i)
            pe.wait_ge(s_hyn, 1)
            for c in range(2):
                for half in range(2):
                    for i in range(4):
                        ins = pe.transpose(bank(2 * c + half)[:, P * i:P * i + P], zbuf[:, i, half, P * c:P * c + P], ident)
                ins.then_inc(s_hyT, 1)

            def gates(q):
                d, c = divmod(q, 2)
                if q == 0:
                    pe.wait_ge(s_lw, 16 * 16)
                    pe.wait_ge(s_hyc, 2)
                    pe.wait_ge(s_pjv, dve_reads(I_LR + 1))
                for j in range(2):
                    if 2 * q + j:
                        pe.wait_ge(s_gact, 2 * q + j)
                    for g in range(2):
                        ins = mm(bank(g), lruw[:, 4 * d + 2 * g + c, :], xr[:, c, HALF * j:HALF * j + HALF], start=True, stop=True)
                    ins.then_inc(s_gmm, 1)

            def sum_squares(n, first, last):
                if n == 2 or n == 8:
                    pe.wait_ge(s_rsd, 1 if n == 2 else 2)
                pe.wait_ge(s_sq, n + 1)
                for j in range(2):
                    ins = mm(bank(2 + j), ones, sq[:, HALF * j:HALF * j + HALF], start=first, stop=last)
                ins.then_inc(s_ssq, 1)

            project(I_KV)
            gates(0)
            project(I_KV + 1)
            sum_squares(0, True, False)
            gates(1)
            sum_squares(1, False, True)
            project(I_KR)
            gates(2)
            pe.wait_ge(*act_read(I_KR))
            pe.wait_ge(s_gact, 6)
            for j in range(2):
                ins = mm(bank(j, p1=DQ), rot, kr[:, HALF * j:HALF * j + HALF], start=True, stop=True)
            ins.then_inc(s_krm, 1)
            project(I_CQ)
            project(I_CQ + 1)
            sum_squares(2, True, False)
            pe.wait_ge(s_kro, 1)
            gates(3)
            for c in range(2, 6):
                project(I_CQ + c)
                sum_squares(1 + c, False, False)
            sum_squares(7, False, True)
            sum_squares(8, True, False)
            sum_squares(9, False, True)

            pe.wait_ge(s_mw, 32)
            pe.wait_ge(s_rb, 1)
            pe.wait_ge(s_gact, 8)
            wv = wukv.rearrange("p k (h n) -> p k h n", h=NH)
            for t in range(TT):
                if t >= 2:
                    pe.wait_ge((s_va, s_vv)[t % 2], t // 2)
                for k in range(2):
                    ins = mm(bank(t % 2), ckv[:, k, P * t:P * t + P], wv[:, k, :, DV:], start=(k == 0), stop=(k == 1))
                ins.then_inc(s_vmm, 1)

            def head_step(h, s):
                if s == 0:
                    if h:
                        pe.wait_ge(s_hpa, 4 * h)
                    else:
                        pe.wait_ge(s_rb, 2)
                        pe.wait_ge(*act_read(len(PROJ) - 1))
                elif s in (1, 2):
                    pe.wait_ge(s_hpa, 4 * h + s)
                elif s in (3, 4):
                    pe.wait_ge(s_hpv, 2 * h + s - 2)
                else:
                    pe.wait_ge(s_hpa, 4 * h + 3)
                h0 = HALF * (s % 2)
                if s < 2:
                    for k in range(6):
                        ins = mm(bank(6, p1=DQ), wuq[:, k, DQ * h:DQ * h + DQ], cq[:, k, h0:h0 + HALF], start=(k == 0), stop=(k == 5))
                elif s < 4:
                    ins = mm(bank(6, p1=DQ), rot, qh[0:DQ, h % 2, h0:h0 + HALF], start=True, stop=True)
                else:
                    for k in range(2):
                        ins = mm(bank(6, p1=DV), wv[:, k, h, 0:DV], ckv[:, k, h0:h0 + HALF], start=(k == 0), stop=(k == 1))
                ins.then_inc(s_hp, 1)

            def scores(n):
                h, qt = divmod(n, TT)
                if qt == 0:
                    pe.wait_ge(s_hpa, 4 * h + 4)
                    pe.wait_ge(s_hpv, 2 * h + 2)
                if n == 0:
                    pe.wait_ge(s_kro, 2)
                    pe.wait_ge(s_rsd, 3)
                    pe.wait_ge(s_va, TT // 2)
                    pe.wait_ge(s_vv, TT // 2)
                if n >= 2:
                    pe.wait_ge(s_exp, n - 1)
                for j in range(2):
                    ins = mm(bank(2 * (n % 2) + j), qh[0:DQ, h % 2, P * qt:P * qt + P], kh[0:DQ, h % 2, HALF * j:HALF * j + HALF], start=True, stop=True)
                ins.then_inc(s_qk, 1)

            def probs_turn(n):
                pe.wait_ge(s_exp, n + 1)
                for b in range(2):
                    if n:
                        pe.wait_ge((s_pta, s_ptv)[b], n)
                    for k in range(4):
                        ins = pe.transpose(bank(4 + b)[:, P * k:P * k + P], p_at[:, n % 2, HALF * b + P * k:HALF * b + P * k + P], ident)
                    ins.then_inc(s_tr, 1)

            def pv(n):
                h = n // TT
                pe.wait_ge(s_pta, n + 1)
                pe.wait_ge(s_ptv, n + 1)
                if n:
                    pe.wait_ge(s_ov, n)
                for k in range(KT):
                    ins = mm(bank(7)[:, DV * (n % 2):DV * (n % 2) + DV], pT[:, n % 2, P * k:P * k + P], v_at[:, k, DV * h:DV * h + DV],
                             start=(k == 0), stop=(k == KT - 1))
                ins.then_inc(s_pv, 1)

            for s in range(6):
                head_step(0, s)
            scores(0)
            N = NH * TT
            for n in range(N):
                h, qt = divmod(n, TT)
                if n + 1 < N:
                    scores(n + 1)
                probs_turn(n)
                if n:
                    pv(n - 1)
                if h + 1 < NH and qt < 6:
                    head_step(h + 1, qt)
            pv(N - 1)

            for t in range(TT):
                pe.wait_ge(s_on, t + 1)
                if t >= 2:
                    pe.wait_ge(s_oc, t - 1)
                for c in range(4):
                    ins = pe.transpose(bank(t % 2)[:, P * c:P * c + P], o_at[:, t, P * c:P * c + P], ident)
                ins.then_inc(s_oT, 1)

            def x1_turn(i):
                pe.wait_ge(s_x1, i + 1)
                for b in range(2):
                    if i:
                        pe.wait_ge((s_x1ta, s_x1tv)[b], i)
                    for k in range(4):
                        ins = pe.transpose(bank(4 + b)[:, P * k:P * k + P], x1t[:, i % 2, HALF * b + P * k:HALF * b + P * k + P], ident)
                    ins.then_inc(s_x1p, 1)

            def logits(i):
                pe.wait_ge(s_x1ta, i + 1)
                pe.wait_ge(s_x1tv, i + 1)
                if i == 0:
                    pe.wait_ge(s_rw, 16)
                if i:
                    pe.wait_ge(s_re, i)
                for k in range(KT):
                    ins = mm(bank(6)[:, NE * (i % 2):NE * (i % 2) + NE], x1T[i % 2][:, P * k:P * k + P], rw[:, k, :], start=(k == 0), stop=(k == KT - 1))
                ins.then_inc(s_lg, 1)

            pe.wait_ge(s_wo, 16)
            pe.wait_ge(s_oc, TT)
            pe.wait_ge(s_rb, 3)
            yT = [yT_hy[:, 0, :], yT_hy[:, 1, :], yT_lru[:, 0, :], yT_lru[:, 1, :]] + [yT_at[:, c, :] for c in range(4)]
            for i in range(TT + 2):
                if i < TT:
                    if i >= 2:
                        pe.wait_ge(s_mixu, i - 1)
                    for k in range(KT):
                        for j in range(2):
                            ins = mm(bank(2 * (i % 2) + j), yT[k][:, P * i:P * i + P], wout[:, k, HALF * j:HALF * j + HALF], start=(k == 0), stop=(k == KT - 1))
                    ins.then_inc(s_mix, 1)
                if 1 <= i <= TT:
                    x1_turn(i - 1)
                if 2 <= i <= TT + 1:
                    logits(i - 2)
            pe.wait_ge(s_aff, TT)
            for i in range(4):
                ins = pe.transpose(bank(7, p1=NE2)[:, P * i:P * i + P], aff[:, i, :], ident)
            ins.then_inc(s_afT, 1)
            pe.wait_ge(s_topk, 1)
            for i in range(4):
                ins = pe.transpose(bank(4)[:, NE2 * i:NE2 * i + NE2], best[:, i, :], ident[0:NE2, 0:NE2])
            ins.then_inc(s_idxp, 1)

            def xe_turn(e, slot, b, bank_):
                if b == 0:
                    pe.wait_ge(s_xe[slot], 16 if isinstance(e, int) and e < 2 else 8 * e + (16 if slot == 0 else 8))
                for k in range(4):
                    ins = pe.transpose(bank(bank_)[:, P * k:P * k + P], xe[:, slot, HALF * b + P * k:HALF * b + P * k + P], ident)
                ins.then_inc(s_xep, 1)

            def hid_turn(e, b):
                if b:
                    pe.wait_ge(s_htv, 2 * e + 1)
                pe.wait_ge(s_hid, 2 * e + b + 1)
                for k in range(4):
                    ins = pe.transpose(bank(4)[:, P * k:P * k + P], hid[:, HALF * b + P * k:HALF * b + P * k + P], ident)
                ins.then_inc(s_ht, 1)

            def expert(e, slot, last):
                zero = isinstance(e, int) and e == 0
                for c in range(WC):
                    if c < 8:
                        out_bank, src, k0 = c // 2, xeT, 4 * (c % 2)
                    else:
                        out_bank, src, k0 = 6 + c % 2, hidT, 4 * ((c - 8) // 2)
                    if c == 0:
                        pe.wait_ge(s_xev, 2 * e + 2)
                    if c in (0, 2, 4, 6) and not zero:
                        pe.wait_ge(s_hid, 2 * e + c // 4 - 1)
                    if c in (8, 10):
                        pe.wait_ge(s_htv, 2 * e + c // 10 + 1)
                    if c in (8, 9) and not zero:
                        pe.wait_ge((s_yea, s_yev)[c - 8], e)
                    pe.wait_ge(s_wlo, WC * e + (c + 1))
                    whi, wlo = wsplit[c % WS][0:2]
                    first, last_k = k0 == 0, k0 + 3
                    for k in range(k0, k0 + 4):
                        mm(bank(out_bank), src[0][:, k, :], whi[:, k % 4, :], start=(k == 0), stop=False)
                        mm(bank(out_bank), src[0][:, k, :], wlo[:, k % 4, :], start=False, stop=False)
                        ins = mm(bank(out_bank), src[1][:, k, :], whi[:, k % 4, :], start=False, stop=(k == KT - 1))
                    ins.then_inc(s_wcu, 1)
                    if c == 5:
                        hid_turn(e, 0)
                    if c == 8:
                        hid_turn(e, 1)
                    if c == 7 and not last:
                        if zero:
                            pe.wait_ge(s_xev, 2)
                        xe_turn(e + 1, 1 - slot, 0, 5)
                    if c == 9 and not last:
                        pe.wait_ge(s_xev, 2 * e + 3)
                        xe_turn(e + 1, 1 - slot, 1, 5)

            pe.wait_ge(s_idxc, 1)
            xe_turn(0, 0, 0, 4)
            xe_turn(0, 0, 1, 5)
            expert(0, 0, False)
            expert(1, 1, False)
            with pe.Fori(2, NE - 2, 2) as e:
                expert(e, 0, False)
                expert(e + 1, 1, False)
            expert(NE - 2, 0, False)
            expert(NE - 1, 1, True)

        @block.vector
        def _(v):
            link = links(v, s_dve)
            stt, tt, ts = v.scalar_tensor_tensor, v.tensor_tensor, v.tensor_scalar

            v.wait_ge(s_parT, 2)
            v.tensor_copy(par[:, 0:N_PAR], bank(0)[:, 0:N_PAR]).then_inc(s_parc, 1)
            v.tensor_copy(fpar, bank(1, p1=FFN)[:, 0:4]).then_inc(s_parc, 1)
            v.wait_ge(s_parc, 2)

            def sine_args(layer):
                for j in range(2):
                    w, n = warg[:, HALF * j:HALF * j + HALF], turns[:, HALF * j:HALF * j + HALF]
                    v.wait_ge(s_fmm, 2 * layer + j + 1)
                    link(ts(w, bank(j, p1=FFN), fpar[:, 2 * layer:2 * layer + 1], fpar[:, 2 * layer + 1:2 * layer + 2], ALU.add, ALU.mult))
                    link(ts(n, w, 1.0 / (2.0 * np.pi), MAGIC, ALU.mult, ALU.add))
                    link(ts(n, n, MAGIC, None, ALU.subtract))
                    link(stt(w, n, -TWO_PI_HI, w, ALU.mult, ALU.add))
                    link(stt(w, n, -TWO_PI_LO, w, ALU.mult, ALU.add))
                    ts(w, w, PI_IN, -PI_IN, ALU.min, ALU.max).then_inc(s_arg, 1)

            def stats(x, st_, mv_):
                v.bn_stats(st_[:, 0:6], x[:, 0:HALF])
                link(v.bn_stats(st_[:, 6:12], x[:, HALF:D]))
                return v.bn_aggr(mv_, st_)

            def norm_rows(x, root, inv, mv_):
                link(v.reciprocal(inv, root))
                return ts(x, x, mv_[:, 0:1], inv, ALU.subtract, ALU.mult)

            def in_norm(i):
                v.wait_ge(s_x[i % 3], 16 * (i // 3 + 1))
                x, b = xr_in[:, i % 3, :], i % 2
                stats(x, st[:, b, :], mv[:, b, :]).then_inc(s_st, 1)
                v.wait_ge(s_sd, i + 1)
                norm_rows(x, sd[:, b:b + 1], rstd[:, b:b + 1], mv[:, b, :]).then_inc(s_xn, 1)

            sine_args(0)
            in_norm(0)
            sine_args(1)
            v.wait_ge(s_wint, 16)
            for nt in range(8):
                if nt + 1 < TT:
                    in_norm(nt + 1)
                v.wait_ge(s_f3, nt + 1)
                if nt >= 2:
                    v.wait_ge(s_hab, nt - 1)
                tt(hw[:, nt % 2, :].rearrange("p (a c) -> p a c", a=4), bank(2 * (nt % 2), 2).rearrange("p (a c) -> p a c", a=4),
                   win[:, nt, :].unsqueeze(1).to_broadcast([P, 4, HYW]), ALU.mult).then_inc(s_hw, 1)

            def by_order(ap):
                return ap.rearrange("p (o c) -> p o c", o=2)

            for jt in range(4):
                b0 = 4 * (jt % 2)
                v.wait_ge(s_fodd, 2 * jt + 2)
                for part in range(2):
                    even, oddp = by_order(bank(b0 + 2 * part)), by_order(fodd[:, part, :])
                    tt(kf[:, :, jt, part, :], even, oddp, ALU.add).then_inc(s_kf, 1)
                    if part == 0:
                        tt(kf[:, :, 4 + jt, part, :], even, oddp, ALU.subtract).then_inc(s_kf, 1)
                    else:
                        tt(kf[:, :, 4 + jt, part, :], oddp, even, ALU.subtract).then_inc(s_kf, 1)

            def hy_copy(m):
                v.wait_ge(s_ut, 2 * m + 2)
                v.tensor_copy(g_hy[:, m // 2, :, 1, P * (m % 2):P * (m % 2) + P], bank(5).rearrange("p (i c) -> p i c", i=4)).then_inc(s_utv, 1)

            v.wait_ge(s_xst, 16 * TT)
            for m in range(N_HY):
                v.wait_ge(s_pja, m + 1)
                u, y = u_hy[:, m, :], bank(proj_bank(m), 2)
                w0, w2 = par[:, C_HYW + m:C_HYW + m + 1], par[:, C_HYW + 12 + m:C_HYW + 13 + m]
                lo = reverse(m, 1, HALF)
                stt(u[:, 0:HALF], y[:, HALF - 1:T - 1], w0, u[:, 0:HALF], ALU.mult, ALU.add)
                link(stt(lo, y[:, 0:HALF - 1], w0, lo, ALU.mult, ALU.add))
                lo = reverse(m, 0, HALF)
                stt(u[:, 0:HALF - 1], y[:, HALF + 1:], w2, u[:, 0:HALF - 1], ALU.mult, ALU.add)
                stt(lo, y[:, 1:HALF + 1], w2, lo, ALU.mult, ALU.add).then_inc(s_pjv, 1)
                if m:
                    hy_copy(m - 1)
            hy_copy(N_HY - 1)

            def lr_taps(c):
                v.wait_ge(s_pja, I_LR + c + 1)
                x, y = xr[:, c, :], bank(6, 2)
                w = [par[:, C_LRW + 2 * k + c:C_LRW + 2 * k + c + 1] for k in range(4)]
                link(stt(x[:, 2:], y[:, 0:T - 2], w[0], x[:, 2:], ALU.mult, ALU.add))
                link(stt(x[:, 1:], y[:, 0:T - 1], w[1], x[:, 1:], ALU.mult, ALU.add))
                stt(x[:, 0:T - 1], y[:, 1:], w[3], x[:, 0:T - 1], ALU.mult, ALU.add).then_inc(s_pjv, 1)

            def conv(o, z):
                tt(pm[:, 0], z[:, :, 0, :], z[:, :, 1, :], ALU.add)
                tt(pm[:, 1], z[:, :, 0, :], z[:, :, 1, :], ALU.subtract).then_inc(s_fold, 1)
                tt(tsk.rearrange("p i h c -> p (i h) c"), z.rearrange("p i h c -> p (i h) c"),
                   skipb[:, o, :].unsqueeze(1).to_broadcast([P, 8, HYW]), ALU.mult)
                for f in range(8):
                    v.wait_ge(s_uf, 8 * o + f + 1)
                    kc, ks = kf[:, o, f, 0, :], kf[:, o, f, 1, :]
                    u = bank(4 + f % 2)
                    if f or o:
                        v.wait_ge(s_yf, 8 * o + f)
                    tt(by_order(t1), by_order(u), kc.unsqueeze(1).to_broadcast([P, 2, HYW]), ALU.mult)
                    tt(t2[:, 0:HYW], u[:, HYW:], ks, ALU.mult)
                    link(tt(t2[:, HYW:], u[:, 0:HYW], ks, ALU.mult))
                    if f >= 2:
                        v.wait_ge(s_yfu, 7 * o + f - 1)
                    elif o:
                        v.wait_ge(s_inv, 4)
                    y = yf[:, f % 2, :]
                    tt(y[:, 0:HYW], t1[:, 0:HYW], t2[:, 0:HYW], ALU.subtract)
                    tt(y[:, HYW:], t1[:, HYW:], t2[:, HYW:], ALU.add).then_inc(s_yf, 1)
                for i in range(4):
                    s = tsk[:, i]
                    v.wait_ge(s_od, 4 * o + i + 1)
                    link(tt(s, s, bank(i)[:, 0:HYW].unsqueeze(1).to_broadcast([P, 2, HYW]), ALU.add))
                    tt(s[:, 0, :], s[:, 0, :], odd, ALU.add)
                    link(tt(s[:, 1, :], s[:, 1, :], odd, ALU.subtract))
                    tt(zbuf[:, i], s, g_hy[:, o, i], ALU.mult).then_inc(s_z, 1)

            v.wait_ge(s_dmat, 80)
            v.wait_ge(s_pj, N_HY)
            v.wait_ge(s_uta, N_HY)
            v.wait_ge(s_utv, N_HY)
            conv(0, g_hy[:, 2])
            v.wait_ge(s_z, 4)
            conv(1, zbuf)
            lr_taps(0)
            v.wait_ge(s_z, 8)
            v.wait_ge(s_hsd, 1)
            link(v.reciprocal(hrs, hsd))
            for i in range(8):
                zz = zbuf[:, i // 2, i % 2, :]
                ins = ts(zz, zz, hrs[:, i:i + 1], None, ALU.mult)
            ins.then_inc(s_hyn, 1)
            v.wait_ge(s_spa, 1)
            e_, r_, s2, q_ = spt[:, 1, :], spt[:, 2, :], spt[:, 3, :], spt[:, 4, :]
            link(ts(r_, e_, 2.0, None, ALU.add))
            link(v.reciprocal(r_, r_))
            link(tt(r_, r_, e_, ALU.mult))
            link(tt(s2, r_, r_, ALU.mult))
            link(ts(q_, s2, 1.0 / 19, 1.0 / 17, ALU.mult, ALU.add))
            for k in (15, 13, 11, 9, 7, 5, 3, 1):
                link(tt(q_, q_, s2, ALU.mult))
                link(ts(q_, q_, 1.0 / k, None, ALU.add))
            link(tt(q_, q_, r_, ALU.mult))
            link(ts(r_, par[:, C_LAM:C_LAM + 4], -1.0, 0.0, ALU.mult, ALU.max))
            link(stt(q_, q_, 2.0, r_, ALU.mult, ALU.add))
            ts(sp8, q_, LRU_C, None, ALU.mult)
            ts(nsp8, q_, -LRU_C, None, ALU.mult).then_inc(s_spv, 1)
            lr_taps(1)

            def scan(q):
                d, c = divmod(q, 2)
                la_, lx_, lt_ = la[:, q % 2, :], lx[:, q % 2, :], lt[:, q % 2, :]
                v.wait_ge(s_lact, 2 * q + 1)
                link(ts(ld, lt_, 1.0, None, ALU.add))
                link(v.reciprocal(ld, ld))
                tt(lt_, lt_, ld, ALU.mult).then_inc(s_lv, 1)
                link(tt(lx_, lx_, xr[:, c, :], ALU.mult))
                v.wait_ge(s_lact, 2 * q + 2)
                link(tt(lx_, lx_, lt_, ALU.mult))
                if d == 0:
                    v.tensor_tensor_scan(hs[:, c, :], la_, lx_, 0.0, ALU.mult, ALU.add).then_inc(s_lv, 1)
                else:
                    link(v.tensor_tensor_scan(ld[:, ::-1], la_[:, ::-1], lx_[:, ::-1], 0.0, ALU.mult, ALU.add))
                    v.wait_ge(s_lv, 2 * c + 2)
                    tt(hs[:, c, :], hs[:, c, :], ld, ALU.add).then_inc(s_lv, 1)
                    v.wait_ge(s_lv, 2 * q + 2)
                    tt(hs[:, c, :], hs[:, c, :], gelu[:, c, :], ALU.mult).then_inc(s_hsg, 1)

            def latent(i, dst, gcol):
                v.wait_ge(*act_read(i))
                ts(dst, bank(proj_bank(i), 2), gcol, None, ALU.mult).then_inc(s_pjv, 1)

            latent(I_KV, ckv[:, 0, :], par[:, C_KVG:C_KVG + 1])
            scan(0)
            latent(I_KV + 1, ckv[:, 1, :], par[:, C_KVG + 1:C_KVG + 2])
            scan(1)
            v.wait_ge(s_rsd, 1)
            link(v.reciprocal(rb, rb))
            for c in range(2):
                ins = tt(ckv[:, c, :], ckv[:, c, :], rb, ALU.mult)
            ins.then_inc(s_rb, 1)
            v.wait_ge(s_rope, 32)
            v.wait_ge(s_krm, 1)
            tt(rtmp2[DV:DQ, :], bank(0, 2, DV, DQ), sin_t[DV:DQ, :], ALU.mult)
            link(tt(kr[DV:DQ, :], kr[DV:DQ, :], cos_t[DV:DQ, :], ALU.mult))
            tt(kr[DV:DQ, :], kr[DV:DQ, :], rtmp2[DV:DQ, :], ALU.add).then_inc(s_kro, 1)
            v.wait_ge(s_kro, 1)
            scan(2)
            for c in range(6):
                latent(I_CQ + c, cq[:, c, :], par[:, C_QG + c:C_QG + c + 1])
                if c == 1:
                    scan(3)
            v.wait_ge(s_rsd, 2)
            link(v.reciprocal(rb, rb))
            for c in range(6):
                ins = tt(cq[:, c, :], cq[:, c, :], rb, ALU.mult)
            ins.then_inc(s_rb, 1)
            v.wait_ge(s_rsd, 3)
            link(v.reciprocal(rb_lru, rb_lru))
            for c in range(2):
                ins = stt(yT_lru[:, c, :], hs[:, c, :], par[:, C_GN + 2 + c:C_GN + 3 + c], rb_lru, ALU.mult, ALU.mult)
            ins.then_inc(s_rb, 1)
            v.wait_ge(s_pj, len(PROJ))
            v.wait_ge(s_kro, 1)
            for b in range(2):
                ins = v.tensor_copy(kh[DV:DQ, b, :], kr[DV:DQ, :])
            ins.then_inc(s_kro, 1)
            for t in range(1, TT, 2):
                v.wait_ge(s_vmm, t + 1)
                v.tensor_copy(v_at[:, t, :], bank(1)).then_inc(s_vv, 1)

            def rope(h, s):
                hh = slice(HALF * s, HALF * s + HALF)
                q, tmp = qh[DV:DQ, h % 2, hh], rtmp[DV:DQ, hh]
                v.wait_ge(s_hp, 6 * h + 3 + s)
                tt(tmp, bank(6, 1, DV, DQ), sin_t[DV:DQ, hh], ALU.mult)
                link(tt(q, q, cos_t[DV:DQ, hh], ALU.mult))
                tt(q, q, tmp, ALU.add).then_inc(s_hpv, 1)

            def row_max(n):
                v.wait_ge(s_qk, n + 1)
                link(v.tensor_reduce(mx[:, n % 2:n % 2 + 1], bank(2 * (n % 2), 2), AX.X, ALU.max))
                ts(nm[:, n % 2:n % 2 + 1], mx[:, n % 2:n % 2 + 1], -SCALE, None, ALU.mult).then_inc(s_nm, 1)

            def probs_copy(n):
                v.wait_ge(s_tr, 2 * n + 2)
                if n >= 2:
                    v.wait_ge(s_pv, n - 1)
                v.tensor_copy(pT[:, n % 2, HALF:], bank(5)).then_inc(s_ptv, 1)

            def output(n):
                h, qt = divmod(n, TT)
                v.wait_ge(s_pv, n + 1)
                link(v.reciprocal(rinv[:, n % 2:n % 2 + 1], rsum[:, n % 4:n % 4 + 1]))
                ts(o_at[:, qt, DV * h:DV * h + DV], bank(7)[:, DV * (n % 2):DV * (n % 2) + DV], rinv[:, n % 2:n % 2 + 1], None, ALU.mult).then_inc(s_ov, 1)

            rope(0, 0)
            rope(0, 1)
            N = NH * TT
            for n in range(N):
                h, qt = divmod(n, TT)
                row_max(n)
                if n >= 1:
                    probs_copy(n - 1)
                if n >= 2:
                    output(n - 2)
                if h + 1 < NH and qt in (3, 4):
                    rope(h + 1, qt - 3)
            probs_copy(N - 1)
            output(N - 2)
            output(N - 1)
            for t in range(TT):
                v.wait_ge(s_osd, t + 1)
                link(v.reciprocal(ars[:, t:t + 1], asd[:, t:t + 1]))
                ts(o_at[:, t, :], o_at[:, t, :], ars[:, t:t + 1], None, ALU.mult).then_inc(s_on, 1)
                if t:
                    o_copy = t - 1
                    v.wait_ge(s_oT, o_copy + 1)
                    tt(yT_at[:, :, P * o_copy:P * o_copy + P], bank(o_copy % 2).rearrange("p (c t) -> p c t", c=4),
                       par[:, C_GN + 4:C_GN + 8].unsqueeze(2).to_broadcast([P, 4, P]), ALU.mult).then_inc(s_oc, 1)
            v.wait_ge(s_oT, TT)
            tt(yT_at[:, :, T - P:], bank((TT - 1) % 2).rearrange("p (c t) -> p c t", c=4),
               par[:, C_GN + 4:C_GN + 8].unsqueeze(2).to_broadcast([P, 4, P]), ALU.mult).then_inc(s_oc, 1)

            def router(i):
                b, b1 = i % 2, i % 2 + 1
                lgt = bank(6)[:, NE * b:NE * b + NE]
                v.wait_ge(s_lg, i + 1)
                v.tensor_reduce(rmx[:, b:b1], lgt, AX.X, ALU.max, negate=True).then_inc(s_rm, 1)
                v.wait_ge(s_re, i + 1)
                link(v.reciprocal(rri[:, b:b1], rsm[:, b:b1]))
                e_ = aff[:, i % 4, 32 * (i // 4):32 * (i // 4) + NE]
                ts(e_, e_, rri[:, b:b1], None, ALU.mult).then_inc(s_aff, 1)

            link(v.memset(aff, 0.0))
            for i in range(TT + 1):
                if i < TT:
                    b = i % 2
                    x = x1t[:, b, :]
                    v.wait_ge(s_mix, i + 1)
                    v.wait_ge(s_res, i + 1)
                    if i >= 2:
                        v.wait_ge(s_x1st[b], 16 * (i // 2))
                        v.wait_ge(s_acc, i - 1)
                        v.wait_ge(s_x1p, 2 * (i - 1))
                    stt(x, xres[:, b, :], ALPHA, bank(2 * b, 2), ALU.mult, ALU.add).then_inc(s_mixu, 1)
                    v.wait_ge(s_mixu, i + 1)
                    stats(x, st[:, b, :], mv[:, b, :]).then_inc(s_mst, 1)
                    v.wait_ge(s_msd, i + 1)
                    link(v.reciprocal(rstd[:, b:b + 1], sd[:, b:b + 1]))
                    link(stt(x, x, mv[:, b, 0:1], gmix, ALU.subtract, ALU.mult))
                    stt(x, x, rstd[:, b:b + 1], bmix, ALU.mult, ALU.add).then_inc(s_x1, 1)
                    v.wait_ge(s_x1p, 2 * i + 2)
                    if i >= 2:
                        v.wait_ge(s_lg, i - 1)
                    v.tensor_copy(x1T[b][:, HALF:], bank(5)).then_inc(s_x1tv, 1)
                if i >= 1:
                    router(i - 1)

            v.wait_ge(s_afT, 1)
            v.wait_ge(s_acst[0], 16 * TT // 2)
            v.wait_ge(s_acst[1], 16 * TT // 2)
            link(v.tensor_copy(affT, bank(7, p1=NE2)))
            for r in range(CAP // 8):
                top = best[:, 0, 8 * r:8 * r + 8]
                link(v.max(top, affT))
                link(v.max_index(idxs[:, 8 * r:8 * r + 8], top, affT))
                if r + 1 < CAP // 8:
                    link(v.match_replace(affT, top, affT, -1.0))
            link(v.tensor_copy(best[:, 1, :], idxs))
            for i in range(2):
                ins = v.tensor_copy(best[:, 2 + i, ::-1], best[:, i, :])
            ins.then_inc(s_topk, 1)
            v.wait_ge(s_idxp, 1)
            b4 = bank(4)[:, 0:4 * NE2].rearrange("p (i e) -> p i e", i=4)
            lo_a, lo_i = b4[:, 0, 0:NE], b4[:, 1, 0:NE]
            link(v.tensor_copy(pick[:, 0:2, :], b4[:, 2:4, 32:32 + NE]))
            hi_a, hi_i, first = pick[:, 0, :], pick[:, 1, :], pick[:, 2, :]
            link(ts(hi_i, hi_i, float(T // 2), None, ALU.add))
            tt(first, lo_a, hi_a, ALU.is_ge)
            link(tt(gate_t, lo_a, hi_a, ALU.max))
            link(tt(hi_a, lo_i, hi_i, ALU.subtract))
            link(tt(hi_a, hi_a, first, ALU.mult))
            tt(idx_t, hi_a, hi_i, ALU.add).then_inc(s_idxc, 1)

            def low(e, c):
                v.wait_ge(s_whi, WC * e + (c + 1))
                _, lo, hi = wsplit[c % WS]
                tt(flat(lo), wraw[:, c], flat(hi), ALU.subtract).then_inc(s_wlo, 1)

            def turned(dst, b, bank_, high_done, n, done):
                v.wait_ge(high_done, n)
                h = slice(HALF * b, HALF * b + HALF)
                tt(flat(dst[1])[:, h], bank(bank_), flat(dst[2])[:, h], ALU.subtract).then_inc(done, 1)

            def expert(e, slot, first, last):
                for c in range(WC):
                    if c + 2 < WC or not last:
                        low(e + (c + 2) // WC, (c + 2) % WC)
                    if c in (3, 7):
                        f = c // 4
                        v.wait_ge(s_sil, 2 * e + f + 1)
                        v.wait_ge(s_wcu, WC * e + (c + 1))
                        tt(hid[:, HALF * f:HALF * f + HALF], sil[:, f, :], bank(c // 2), ALU.mult).then_inc(s_hid, 1)
                    if c in (5, 8):
                        turned(hidT, c // 8, 4, s_hta, 2 * e + c // 8 + 1, s_htv)
                    if c in (7, 9) and not last:
                        turned(xeT, c // 9, 5, s_xea, 2 * e + 2 + c // 9 + 1, s_xev)
                    if c == 11:
                        v.wait_ge(s_wcu, WC * e + WC)
                        if not first:
                            v.wait_ge(s_sc, 16 * e - 16)
                        ts(ye[:, slot, HALF:], bank(7), gate_e[:, slot:slot + 1], None, ALU.mult).then_inc(s_yev, 1)

            low(0, 0)
            low(0, 1)
            for b in range(2):
                turned(xeT, b, 4 + b, s_xea, b + 1, s_xev)
            expert(0, 0, True, False)
            expert(1, 1, True, False)
            with v.Fori(2, NE - 2, 2) as e:
                expert(e, 0, False, False)
                expert(e + 1, 1, False, False)
            expert(NE - 2, 0, False, False)
            expert(NE - 1, 1, False, True)

            v.wait_ge(s_gff, 32)
            for i in range(TT):
                x, b = fin[:, i, :], i % 2
                v.wait_ge(s_fx[i], 16 * NE + 16)
                stats(x, st[:, b, :], mv[:, b, :]).then_inc(s_fst, 1)
                v.wait_ge(s_fsd, i + 1)
                link(v.reciprocal(rstd[:, b:b + 1], sd[:, b:b + 1]))
                link(stt(x, x, mv[:, b, 0:1], gff, ALU.subtract, ALU.mult))
                stt(x, x, rstd[:, b:b + 1], bff, ALU.mult, ALU.add).then_inc(s_fo, 1)


_INS = ["x", "ln_in_g", "ln_in_b", "w_in", "hy_conv_w", "hy_conv_b", "hy_ffn_w1", "hy_ffn_b1", "hy_sin_f1",
        "hy_ffn_w2", "hy_ffn_b2", "hy_sin_f2", "hy_ffn_w3", "hy_skip", "lru_conv_w", "lru_conv_b", "lru_wa", "lru_ba",
        "lru_wx", "lru_bx", "lru_lambda", "mla_q_norm_g", "mla_w_uq", "mla_kv_norm_g", "mla_w_ukv", "group_norm_g",
        "w_out", "ln_mix_g", "ln_mix_b", "router_w", "exp_w_gate", "exp_w_up", "exp_w_down", "ln_ffn_g", "ln_ffn_b"]


def kernel(**inputs):
    import numpy as _np
    import concourse.bacc as _bacc
    from concourse import mybir as _mybir
    from concourse.bass_utils import run_bass_kernel_spmd as _run

    nc = _bacc.Bacc("TRN2", target_bir_lowering=False, num_devices=1)
    given = {name: _np.ascontiguousarray(inputs[name]) for name in _INS}
    given.update(shape_constants())
    arrays = {f"in_{name}": a for name, a in given.items()}
    aps = {name: nc.dram_tensor(f"in_{name}", a.shape, _mybir.dt.from_np(a.dtype), kind="ExternalInput").ap()
           for name, a in given.items()}
    out = nc.dram_tensor("out_0", (1, T, D), F32, kind="ExternalOutput").ap()
    encoder(nc, aps, out)
    r = _run(nc, [arrays], core_ids=[0])
    return r.results[0]["out_0"]
```

```python
import numpy as np
import concourse.bass as bass
from concourse import mybir
from contextlib import ExitStack

F32 = mybir.dt.float32
F32R = mybir.dt.float32r
U32 = mybir.dt.uint32
ALU = mybir.AluOpType
ACT = mybir.ActivationFunctionType
AX = mybir.AxisListType

P = 128
D = 1024
T = 1024
KT = D // P
TT = T // P
HALF = 512
HYW = D // 4
LRW = D // 4
NH, DV, DR = 8, 64, 32
DQ = DV + DR
QL, KVL = 12 * DV, 4 * DV
FFN, POS = 64, 33
NE, CAP = 16, 2 * T // 16
NE2 = 32 + NE
NIN = 3 * HYW + 2 * LRW + QL + KVL + DR
EPS = 1e-5
ALPHA = 2.0 ** 0.25
SCALE = float(DQ) ** -0.5
LRU_C = 8.0
MAGIC = 1.5 * 2.0 ** 23
TWO_PI_HI = 6.28125
TWO_PI_LO = 2.0 * np.pi - 6.28125
PI_IN = 3.1415925

C_HYW, C_HYB, C_LRW, C_LRB = 0, 18, 24, 32
C_BA, C_BX, C_LAM, C_QG, C_KVG = 34, 38, 42, 46, 52
C_GN, C_LG, C_LB, N_PAR = 54, 62, 70, 78


def shape_constants():
    f32 = np.float32
    tab = np.concatenate([np.eye(P), np.ones((P, P))], axis=1)
    partner = np.arange(P) // DR * DR + (np.arange(P) + DR // 2) % DR
    rot = np.eye(P)[partner]
    order = np.concatenate([np.arange(0, T, 2), np.arange(1, T, 2)])
    t = np.linspace(0.0, 1.0, T, dtype=f32)[:, None]
    bands = (POS - 1) // 2
    freqs = np.linspace(1e-4, bands - 1, bands, dtype=f32)[None, :]
    ang = (f32(2.0 * np.pi) * np.arange(T, dtype=f32)[:, None] * freqs / f32(T)).astype(f32)
    a64 = ang.astype(np.float64)
    z = np.concatenate([t, np.cos(a64), -np.sin(a64)], axis=-1).astype(f32)
    lo, hi = np.log(1e-2) / 1.5, np.log(1e-2) / 0.3
    deltas = np.abs(np.linspace(lo, hi, HYW, dtype=f32))
    window = np.exp((-t * deltas[None, :]).astype(np.float64)).astype(f32)
    j = np.arange(HALF)
    w = np.pi * (2 * j + 1) / (2.0 * T)
    fall = np.concatenate([w, np.pi - w])
    n = order[:, None]
    tau = (np.arange(HALF) + 0.5)[:, None]
    inv = 1.0 / T
    rope = 10000.0 ** (-np.arange(0, DR, 2, dtype=f32) / f32(DR))
    rang = (np.arange(T, dtype=f32)[:, None] * rope.astype(f32)[None, :]).astype(np.float64).T
    out = {
        "c_tab": tab, "c_pos": z[order].T, "c_win": window[order],
        "c_fc": np.cos(n * w), "c_fs": np.sin(n * w),
        "c_dc": np.cos(tau * fall), "c_ds": np.sin(tau * fall),
        "c_ic": (np.cos(tau * fall) * inv).T, "c_is": (np.sin(tau * fall) * inv).T,
        "c_rot": rot,
        "c_cos": np.concatenate([np.cos(rang), np.cos(rang)] * (P // DR)),
        "c_sin": np.concatenate([-np.sin(rang), np.sin(rang)] * (P // DR)),
    }
    return {k: np.ascontiguousarray(v, dtype=f32) for k, v in out.items()}


def encoder(nc, A, out):
    ctx = ExitStack()
    with ctx:
        def sem(name):
            return ctx.enter_context(nc.semaphore(name))

        WORDS, ARENA_AT = 53200, 16512
        arena = nc.alloc_sbuf_tensor_at("arena", [P, WORDS], F32, offset=ARENA_AT)
        psum = ctx.enter_context(nc.psum_tensor("psum", [P, 8 * HALF], F32))

        def mem(at, *dims, p0=0, p1=P):
            n = int(np.prod(dims))
            assert at + n <= WORDS
            return shaped(arena[p0:p1, at:at + n], dims)

        def shaped(v, dims):
            if len(dims) == 2:
                v = v.rearrange("p (a b) -> p a b", a=dims[0])
            elif len(dims) == 3:
                v = v.rearrange("p (a b c) -> p a b c", a=dims[0], b=dims[1])
            elif len(dims) == 4:
                v = v.rearrange("p (a b c d) -> p a b c d", a=dims[0], b=dims[1], c=dims[2])
            return v

        def parts(at, *dims, p1=P):
            n = int(np.prod(dims))
            both = nc.alloc_sbuf_tensor_at(f"split_at_{at}_{dims[-1]}", [P, 2 * n], F32R, offset=ARENA_AT + 4 * at)
            return shaped(both[0:p1, 0:n], dims), shaped(both[0:p1, n:2 * n], dims), shaped(both[0:p1, 0:n].bitcast(F32), dims)

        def bank(b, n=1, p0=0, p1=P):
            return psum[p0:p1, HALF * b:HALF * (b + n)]

        def dram(name, shape):
            return nc.dram_tensor(name, shape, F32, kind="Internal").ap()

        xhat_dram = dram("xhat_scratch", [T, D])
        x1_dram = dram("x1_scratch", [T, D])
        acc_dram = dram("acc_scratch", [T, D])

        ident, ones = mem(0, 128), mem(128, 128)
        par = mem(352, 80)
        w1, w2 = mem(432, FFN, p1=POS), mem(496, FFN, p1=FFN)
        fpar = mem(560, 4, p1=FFN)
        eps, idle = mem(564, 1), mem(596, 2)
        sp8 = mem(566, 4)
        nsp8 = mem(570, 4)
        spt = mem(574, 5, 4)
        st = mem(600, 2, 12)
        mv = mem(624, 2, 2)
        sd = mem(628, 2)
        rstd = mem(630, 2)
        hss = mem(632, 8)
        hsd = mem(640, 8)
        hrs = mem(648, 8)
        mx, nm, rsum, rinv = mem(656, 2), mem(658, 2), mem(660, 4), mem(664, 2)
        ass, asd, ars = mem(666, 8), mem(674, 8), mem(682, 8)
        rmx, rsm, rri = mem(690, 2), mem(692, 2), mem(694, 2)
        aff = mem(784, 4, NE2)
        gate_t = mem(744, NE)
        idx_t = mem(760, NE).bitcast(U32)
        idx_e = mem(704, 4).bitcast(U32)
        gate_e = mem(778, 2)
        prow = mem(784, 128, p1=N_PAR)
        frow = mem(912, FFN, p1=4)

        kf = mem(976, 2, 8, 2, HYW)
        xT = mem(9168, KT, T)
        fc, fs = mem(17360, 8, HALF), mem(21456, 8, HALF)
        hf = mem(25552, 8, 2, HALF)
        pos_t, w3 = mem(39888, T, p1=POS), mem(40912, 1024, p1=FFN)
        h1, h2 = mem(41936, T, p1=FFN), mem(42960, T, p1=FFN)
        win = mem(43984, 8, HYW)
        xr_in = mem(46032, 3, D)
        hw = mem(49104, 2, 1024)
        fodd = mem(51152, 2, HALF)
        warg, turns = mem(52176, T, p1=FFN), mem(24528, T, p1=FFN)
        win_w = mem(33744, 3, KT, 256)
        u_hy = mem(39888, 6, T)
        g_hy = mem(46032, 3, 4, 2, HYW)
        dc, ds_ = mem(17360, 4, T), mem(21456, 4, T)
        ic, is_ = mem(25552, 8, HALF), mem(29648, 8, HALF)
        pm = mem(39888, 2, 4, HYW)
        zbuf = mem(41936, 4, 2, HYW)
        yf = mem(43984, 2, HALF)
        t1, t2 = mem(45008, HALF), mem(45520, HALF)
        odd = t1[:, 0:HYW]
        skipb = mem(52176, 2, HYW)
        tsk = mem(37840, 4, 2, HYW)
        xr, gelu = mem(976, 2, T), mem(3024, 2, T)
        rb, rb_lru = mem(5072, T), mem(8144, T)
        cos_t, sin_t = mem(6096, T), mem(7120, T)
        hs = mem(17360, 2, T)
        la, lx, lt = mem(19408, 2, T), mem(21456, 2, T), mem(23504, 2, T)
        ld = mem(25552, T)
        lruw = mem(52176, 8, 128)
        wq = mem(26576, 6, NH * DV)
        wqr = mem(29648, 6, NH * DR)
        wk, wv = mem(31184, 2, NH * DV), mem(32208, 2, NH * DV)
        cq, ckv = mem(39888, 6, T), mem(46032, 2, T)
        kr = mem(48080, T)
        sq = mem(49104, T)
        yT_hy = mem(50128, 2, T)
        v_at, o_at = mem(9168, TT, NH * DV), mem(27600, TT, NH * DV)
        rot = mem(784, 128)
        qrope, rtmp, rtmp_k = mem(25552, T), mem(52176, T), mem(25552, T)
        q_at = [mem(13264, NH // 2, T, p1=DQ), mem(976, NH // 2, T, p1=DQ)]
        k_at = [mem(19408, NH // 2, T, p1=DV), mem(33744, NH // 2, T, p1=DV)]
        qs = [parts(23504, T, p1=DQ), parts(39888, T, p1=DQ)]
        ks = [parts(37840, T, p1=DQ), parts(41936, T, p1=DQ)]
        pT, p_at = mem(43984, 2, T), mem(46032, 2, T)
        wout_in = mem(48080, 2, D)
        wout = [parts(at, D) for at in (5072, 7120, 13264, 15312, 19408, 21456, 25552, 31696)]
        y_hy, y_lru = parts(33744, 2, T), parts(976, 2, T)
        y_at = [parts(37840, 2, T), parts(41936, 2, T)]
        gin, bin_ = mem(9168, D), mem(10192, D)
        gmix, bmix = mem(11216, D), mem(12240, D)
        o_sq = mem(52176, HALF)
        xres, x1t = mem(46032, 2, D), mem(48080, 2, D)
        x1T = [mem(27600, D), mem(52176, D)]
        rw = mem(24528, KT, NE)
        accb = mem(50128, 2, D)
        affT = mem(9168, T // 2, p1=NE2)

        WC, WS = 12, 4
        wraw = mem(28624, WC, 4 * HALF)
        wsplit = [parts(12240 + 4096 * i, 4, HALF) for i in range(WS)]
        xe, xeT, hidT = mem(976, 2, D), parts(3024, KT, CAP), parts(7120, KT, CAP)
        sil, hid, ye = mem(5072, 2, HALF), mem(6096, D), mem(9168, 2, D)
        best, idxs = mem(10192, 4, CAP, p1=NE2), mem(10704, CAP, p1=NE2).bitcast(U32)
        pick = mem(10832, 3, NE)
        gff, bff = mem(28624, D), mem(29648, D)
        fin = mem(16336, TT, D)
        fin_rstd = mem(696, TT)

        s_tab, s_par, s_wint, s_fmat = sem("tables_ld"), sem("params_ld"), sem("window_ld"), sem("filter_mats_ld")
        s_x = [sem(f"x_ld{i}") for i in range(3)]
        s_eps, s_parT, s_parc = sem("eps_set"), sem("params_turned"), sem("params_copied")
        s_fmm, s_arg, s_sin, s_f3 = sem("ffn_psum"), sem("sine_arg"), sem("sine_done"), sem("filter_psum")
        s_hw, s_hab = sem("filter_windowed"), sem("filter_folded")
        s_st, s_sd, s_xn, s_xst, s_xp, s_xT = sem("in_stats"), sem("in_root"), sem("in_normed"), sem("xhat_stored"), sem("x_turned"), sem("xT_done")
        s_dft, s_fodd, s_kf = sem("filter_sums_psum"), sem("filter_odd_copied"), sem("spectra_done")
        s_w = [sem(f"w_in_ld{i}") for i in range(3)]
        s_pj, s_pja, s_pjv = sem("proj_psum"), sem("proj_read_act"), sem("proj_read_dve")
        s_ut, s_uta, s_utv = sem("hyena_turned"), sem("hyena_copied_act"), sem("hyena_copied_dve")
        s_dmat = sem("dft_ld")
        s_fold, s_uf, s_yf, s_yfu = sem("folded"), sem("spectrum_psum"), sem("product_done"), sem("product_used")
        s_inv, s_od, s_z = sem("inverse_psum"), sem("odd_copied"), sem("z_done")
        s_hsd, s_hyn, s_hyT, s_hyc = sem("hyena_root"), sem("hyena_normed"), sem("hyena_back_psum"), sem("hyena_out")
        s_zero, s_lw, s_spa, s_spv = sem("zeroed"), sem("lru_w_ld"), sem("softplus_exp"), sem("softplus_done")
        s_gmm, s_gact, s_lact, s_lv, s_hsg = sem("gates_psum"), sem("gates_read"), sem("lru_act"), sem("lru_dve"), sem("lru_gated")
        s_sq, s_ssq, s_rsd, s_rb = sem("squares"), sem("squares_summed"), sem("rms_root"), sem("rms_applied")
        s_mw, s_rope, s_krm, s_kro = sem("mla_w_ld"), sem("rope_ld"), sem("rotary_partners_psum"), sem("kr_roped")
        s_vmm, s_va = sem("v_psum"), sem("v_copied")
        s_hp, s_hpa, s_hpv = sem("heads_psum"), sem("heads_copied_act"), sem("heads_copied_dve")
        s_qro, s_qkh, s_qkl = sem("queries_roped"), sem("head_high"), sem("head_split")
        s_qk, s_nm, s_exp, s_tr = sem("scores_psum"), sem("neg_max"), sem("exp_done"), sem("probs_turned")
        s_pta, s_ptv, s_pv, s_ov = sem("probsT_act"), sem("probsT_dve"), sem("pv_psum"), sem("o_done")
        s_osd, s_on, s_oT = sem("o_root"), sem("o_normed"), sem("o_turned")
        s_yh, s_yl = sem("mixer_high"), sem("mixer_split")
        s_wo, s_woh, s_wol = [sem(f"w_out_ld{i}") for i in range(2)], sem("w_out_high"), sem("w_out_split")
        s_gb, s_rw, s_gff = sem("gains_ld"), sem("router_w_ld"), sem("ffn_gains_ld")
        s_xh = [sem(f"xhat_ld{i}") for i in range(2)]
        s_res, s_mix, s_mixu, s_mst, s_msd, s_x1 = sem("residual"), sem("mix_psum"), sem("mix_read"), sem("mix_stats"), sem("mix_root"), sem("x1_done")
        s_x1st, s_acst, s_acc = [sem(f"x1_stored{i}") for i in range(2)], [sem(f"acc_stored{i}") for i in range(2)], sem("acc_scaled")
        s_x1p, s_x1ta, s_x1tv, s_lg = sem("x1_turned"), sem("x1T_act"), sem("x1T_dve"), sem("logits")
        s_rm, s_re, s_aff, s_afT = sem("router_max"), sem("router_exp"), sem("affinity"), sem("affinity_turned")
        s_topk, s_idxp, s_idxc = sem("topk_done"), sem("idx_turned"), sem("idx_ready")
        s_wc, s_wcu = [sem(f"expert_w_ld{c}") for c in range(WC)], sem("expert_w_used")
        s_ie, s_xe = sem("expert_idx"), [sem(f"xe_gathered{i}") for i in range(2)]
        s_xep, s_xea, s_xev = sem("xe_turned"), sem("xeT_act"), sem("xeT_dve")
        s_whi, s_wlo = sem("expert_w_high"), sem("expert_w_split")
        s_sil, s_hid = sem("silu_done"), sem("hidden_done")
        s_ht, s_hta, s_htv = sem("hid_turned"), sem("hidT_act"), sem("hidT_dve")
        s_yea, s_yev, s_sc = sem("ye_act"), sem("ye_dve"), sem("scattered")
        s_fx, s_out = s_wc[0:TT], sem("out_stored")
        s_fst, s_fsd, s_fg, s_fi, s_fn, s_fo = sem("final_stats"), sem("final_root"), sem("final_gained"), sem("final_inverse"), sem("final_normed"), sem("final_done")
        s_dve, s_act, s_pool = sem("dve_chain"), sem("act_chain"), sem("pool_chain")

        def links(eng, chain):
            count = [0]

            def link(ins):
                count[0] += 1
                ins.then_inc(chain, 1)
                eng.wait_ge(chain, count[0])
            return link

        def tokens(ap):
            return ap.rearrange("(t p) d -> p t d", p=P)

        def rows(ap):
            return ap.rearrange("(k p) n -> p k n", p=P)

        def flat(ap3):
            return ap3.rearrange("p a b -> p (a b)")

        def reverse(m, a, b):
            return u_hy[:, m, T - 1 - a:T - 1 - b:-1]

        w_in = rows(A["w_in"][0])
        x_tok, xh_tok, x1_tok, acc_tok = tokens(A["x"][0]), tokens(xhat_dram), tokens(x1_dram), tokens(acc_dram)
        out_tok = tokens(out[0])

        LR0, CQ0, KV0, KR0 = 3 * HYW, 3 * HYW + 2 * LRW, 3 * HYW + 2 * LRW + QL, 3 * HYW + 2 * LRW + QL + KVL
        PROJ = ([(P * m, P) for m in range(10)] + [(KV0 + P * m, P) for m in range(2)] + [(KR0, DR)]
                + [(CQ0 + P * m, P) for m in range(6)])
        N_HY, I_LR, I_LG, I_KV, I_KR, I_CQ = 6, 6, 8, 10, 12, 13
        CHUNKS = [(256 * c, 256) for c in range(5)] + [(KV0, 256), (KR0, DR)] + [(CQ0 + 256 * c, 256) for c in range(3)]
        LAST = [1, 3, 5, 7, 9, 11, 12, 14, 16, 18]

        def chunk_of(i):
            return min(c for c in range(len(CHUNKS)) if LAST[c] >= i)

        def proj_bank(i):
            return 2 * (i % 2) if i < N_HY else 6 if i < I_LG else 4 + 2 * (i % 2)

        def proj_before(i):
            return max([j for j in range(i) if proj_bank(j) == proj_bank(i)], default=None)

        def dve_reads(i):
            return sum(j not in (I_LG, I_LG + 1, I_KR) for j in range(i + 1))

        def act_read(i):
            if i in (I_KV, I_KV + 1):
                return s_sq, i - I_KV + 1
            return (s_sq, i - I_CQ + 3) if i >= I_CQ else (s_pja, min(i, I_KV) + 1)

        HEADS = [("key", i) for i in range(4)] + [("rope", 0), ("query", 0), ("rope", 1), ("query", 1), ("query", 2), ("query", 3)]
        U_HEAD0 = HEADS.index(("query", 0))

        N_UNIT = NH * TT
        WOUT_AT = [TT * h + qt for h in range(3, 7) for qt in (5, 7)]

        GROUPS_AT = [N_UNIT - 7, N_UNIT - 5, N_UNIT - 3, N_UNIT - 2]

        def heads_bank(u):
            return 4 + 2 * (u % 2)

        def dve_heads(u):
            return sum(kind != "rope" for kind, _ in HEADS[:u + 1])

        block = ctx.enter_context(nc.Block())

        @block.sync
        def _(sp):
            sp.dma_start(mem(0, 256), A["c_tab"]).then_inc(s_tab, 16)
            for i in range(3):
                sp.dma_start(xr_in[:, i, :], x_tok[:, i, :]).then_inc(s_x[i], 16)
            for at, src in ((C_HYW, A["hy_conv_w"][0].rearrange("k (m p) -> (k m) p", p=P)),
                            (C_HYB, A["hy_conv_b"][0].rearrange("(m p) -> m p", p=P)),
                            (C_LRW, A["lru_conv_w"][0].rearrange("k (m p) -> (k m) p", p=P)),
                            (C_LRB, A["lru_conv_b"][0].rearrange("(m p) -> m p", p=P)),
                            (C_BA, A["lru_ba"][0].rearrange("k (m p) -> (k m) p", p=P)),
                            (C_BX, A["lru_bx"][0].rearrange("k (m p) -> (k m) p", p=P)),
                            (C_LAM, A["lru_lambda"][0].rearrange("k (m p) -> (k m) p", p=P)),
                            (C_QG, A["mla_q_norm_g"][0].rearrange("(m p) -> m p", p=P)),
                            (C_KVG, A["mla_kv_norm_g"][0].rearrange("(m p) -> m p", p=P)),
                            (C_GN, A["group_norm_g"][0].rearrange("(m p) -> m p", p=P)),
                            (C_LG, A["ln_in_g"].rearrange("(m p) -> m p", p=P)),
                            (C_LB, A["ln_in_b"].rearrange("(m p) -> m p", p=P))):
                sp.dma_start(prow[at:at + src.shape[0], :], src).then_inc(s_par, 16)
            for i, name in enumerate(("hy_ffn_b1", "hy_sin_f1", "hy_ffn_b2", "hy_sin_f2")):
                sp.dma_start(frow[i:i + 1, :], A[name]).then_inc(s_par, 16)
            sp.dma_start(pos_t, A["c_pos"]).then_inc(s_par, 16)
            sp.dma_start(w1, A["hy_ffn_w1"][0]).then_inc(s_par, 16)
            sp.dma_start(w2, A["hy_ffn_w2"][0]).then_inc(s_par, 16)
            sp.dma_start(w3, A["hy_ffn_w3"][0]).then_inc(s_par, 16)
            sp.dma_start(win, rows(A["c_win"])).then_inc(s_wint, 16)
            for i in range(TT):
                sp.wait_ge(s_xn, i + 1)
                sp.dma_start(xh_tok[:, i, :], xr_in[:, i % 3, :]).then_inc(s_xst, 16)
                if i + 3 < TT:
                    sp.wait_ge(s_xst, 16 * (i + 1))
                    sp.wait_ge(s_xp, i + 1)
                    sp.dma_start(xr_in[:, i % 3, :], x_tok[:, i + 3, :]).then_inc(s_x[i % 3], 16)
                if i == TT - 4:
                    sp.dma_start(fc, rows(A["c_fc"])).then_inc(s_fmat, 16)
                    sp.dma_start(fs, rows(A["c_fs"])).then_inc(s_fmat, 16)

            def load_w(c):
                c0, w = CHUNKS[c]
                if c >= 3:
                    sp.wait_ge(s_pj, LAST[c - 3] + 1)
                sp.dma_start(win_w[:, c % 3, :, 0:w], w_in[:, :, c0:c0 + w]).then_inc(s_w[c % 3], 16)

            sp.wait_ge(s_fmat, 32)
            for c in range(3):
                load_w(c)
            sp.wait_ge(s_dft, 4)
            for dst, name in ((dc, "c_dc"), (ds_, "c_ds"), (ic, "c_ic"), (is_, "c_is")):
                sp.dma_start(dst, rows(A[name])).then_inc(s_dmat, 16)
            sp.wait_ge(s_sin, 4)
            sp.dma_start(skipb, A["hy_skip"][0].partition_broadcast(P)).then_inc(s_dmat, 16)
            load_w(3)
            load_w(4)
            sp.wait_ge(s_inv, 8)
            for dst, name, n_k, d0 in ((wq, "mla_w_uq", 6, 0), (wqr, "mla_w_uq", 6, DV), (wk, "mla_w_ukv", 2, 0), (wv, "mla_w_ukv", 2, DV)):
                w = dst.shape[2] // NH
                for k in range(n_k):
                    src = A[name][0, P * k:P * k + P, :].rearrange("p (h n) -> p h n", h=NH)[:, :, d0:d0 + w]
                    sp.dma_start(dst[:, k, :].rearrange("p (h n) -> p h n", h=NH), src).then_inc(s_mw, 16)
            sp.wait_ge(s_z, 8)
            for dst, name in ((rot, "c_rot"), (cos_t, "c_cos"), (sin_t, "c_sin")):
                sp.dma_start(dst, A[name]).then_inc(s_rope, 16)
            load_w(5)
            sp.wait_ge(s_zero, 1)
            for d in range(2):
                for g, name in enumerate(("lru_wa", "lru_wx")):
                    for c in range(2):
                        for b in range(2):
                            sp.dma_start(lruw[64 * b:64 * b + 64, 4 * d + 2 * g + c, 64 * b:64 * b + 64],
                                         A[name][0, d, 2 * c + b]).then_inc(s_lw, 16)
            for c in range(6, len(CHUNKS)):
                load_w(c)
            sp.wait_ge(s_qkl, 4)
            for k in range(KT):
                if k >= 2:
                    sp.wait_ge(s_wol, k - 1)
                sp.dma_start(wout_in[:, k % 2, :], A["w_out"][0, P * k:P * k + P, :]).then_inc(s_wo[k % 2], 16)
            sp.wait_ge(s_pv, NH * TT)
            for dst, src in ((gin, A["ln_in_g"]), (bin_, A["ln_in_b"]), (gmix, A["ln_mix_g"][0]), (bmix, A["ln_mix_b"][0])):
                sp.dma_start(dst, src.partition_broadcast(P)).then_inc(s_gb, 16)
            for i in range(2):
                sp.dma_start(xres[:, i, :], xh_tok[:, i, :]).then_inc(s_xh[i], 16)
            sp.wait_ge(s_oT, TT)
            sp.dma_start(rw, rows(A["router_w"][0])).then_inc(s_rw, 16)

            def load_chunk(e, c):
                if c < 8:
                    half, kind, k = c // 4, ("exp_w_gate", "exp_w_up")[c % 4 // 2], c % 2
                else:
                    half, kind, k = c % 2, "exp_w_down", (c - 8) // 2
                w = A[kind][0]
                w = w[e] if isinstance(e, int) else w[bass.ds(e, 1)].rearrange("a k n -> (a k) n")
                src = w[HALF * k:HALF * k + HALF, HALF * half:HALF * half + HALF]
                sp.dma_start(wraw[:, c].rearrange("p (k n) -> p k n", k=4), rows(src)).then_inc(s_wc[c], 16)

            load_chunk(0, 0)
            for i in range(TT):
                sp.wait_ge(s_x1, i + 1)
                sp.dma_start(x1_tok[:, i, :], x1t[:, i % 2, :]).then_inc(s_x1st[i % 2], 16)
                if i + 2 < TT:
                    sp.wait_ge(s_mixu, i + 1)
                    sp.dma_start(xres[:, i % 2, :], xh_tok[:, i + 2, :]).then_inc(s_xh[i % 2], 16)
            sp.wait_ge(s_mix, TT)
            for c in range(1, 8):
                load_chunk(0, c)
            sp.wait_ge(s_lg, TT)
            for i in range(2):
                sp.wait_ge(s_acst[i], 16 * TT // 2)
            for c in range(8, WC):
                load_chunk(0, c)
            with sp.Fori(1, NE) as e:
                for c in range(WC):
                    sp.wait_ge(s_wlo, WC * e + (c + 1 - WC))
                    load_chunk(e, c)
            sp.wait_ge(s_wlo, WC * (NE - 1) + 1)
            for dst, name in ((gff, "ln_ffn_g"), (bff, "ln_ffn_b")):
                sp.dma_start(dst, A[name][0].partition_broadcast(P)).then_inc(s_gff, 16)
            sp.wait_ge(s_sc, 16 * NE)
            for i in range(TT):
                sp.dma_start(fin[:, i, :], acc_tok[:, i, :]).then_inc(s_fx[i], 16)
            for i in range(TT):
                sp.wait_ge(s_fo, i + 1)
                sp.dma_start(out_tok[:, i, :], fin[:, i, :]).then_inc(s_out, 16)
            sp.wait_ge(s_out, 16 * TT)

        @block.gpsimd
        def _(pool):
            link = links(pool, s_pool)
            pool.memset(eps, EPS).then_inc(s_eps, 1)
            for nt in range(8):
                pool.wait_ge(s_hw, nt + 1)
                fwd, bwd = hw[:, nt % 2, 0:HALF], hw[:, nt % 2, HALF:]
                if nt == 0:
                    link(pool.memset(bwd[0:1, :], 0.0))
                pool.tensor_tensor(hf[:, nt, 0, :], fwd, bwd, ALU.add)
                pool.tensor_tensor(hf[:, nt, 1, :], fwd, bwd, ALU.subtract).then_inc(s_hab, 1)
            pool.wait_ge(s_z, 8)
            pool.memset(lruw, 0.0).then_inc(s_zero, 1)
            pool.memset(kr, 0.0).then_inc(s_zero, 1)
            pool.wait_ge(s_gb, 64)
            for i in range(TT):
                res = xres[:, i % 2, :]
                pool.wait_ge(s_xh[i % 2], 16 * (i // 2 + 1))
                link(pool.tensor_tensor(res, res, gin, ALU.mult))
                pool.tensor_tensor(res, res, bin_, ALU.add).then_inc(s_res, 1)

            def gather(e, n):
                copied, col = 2 * e + 2, slice(e, e + 1) if isinstance(e, int) else bass.ds(e, 1)
                pool.tensor_copy(idx_e[:, n:n + 1], idx_t[:, col]).then_inc(s_ie, 1)
                pool.tensor_copy(gate_e[:, n % 2:n % 2 + 1], gate_t[:, col]).then_inc(s_ie, 1)
                pool.wait_ge(s_ie, copied)
                if not isinstance(e, int):
                    pool.tensor_tensor(idle[:, 0:1], eps, eps, ALU.add)
                pool.indirect_dma_start(xe[:, n % 2, :], None, x1_dram,
                                        bass.IndirectOffsetOnAxis(ap=idx_e[:, n:n + 1], axis=0)).then_inc(s_xe[n % 2], 16)

            def finish(e, n, more):
                pool.wait_ge(s_yea, e + 1)
                pool.wait_ge(s_yev, e + 1)
                if more:
                    gather(e + 2, (n + 2) % 4)
                if not (isinstance(e, int) and e == 0):
                    pool.wait_ge(s_sc, 16 * e)
                if not isinstance(e, int):
                    pool.tensor_tensor(idle[:, 1:2], eps, eps, ALU.add)
                pool.indirect_dma_start(acc_dram, bass.IndirectOffsetOnAxis(ap=idx_e[:, n:n + 1], axis=0),
                                        ye[:, n % 2, :], None, compute_op=ALU.add).then_inc(s_sc, 16)

            for c in range(WS):
                _, lo, hi = wsplit[c]
                pool.wait_ge(s_whi, c + 1)
                pool.tensor_tensor(flat(lo), wraw[:, c], flat(hi), ALU.subtract).then_inc(s_wlo, 1)
            for i in range(2):
                pool.wait_ge(s_x1st[i], 16 * TT // 2)
                pool.wait_ge(s_acst[i], 16 * TT // 2)
            pool.wait_ge(s_idxc, 1)
            gather(0, 0)
            gather(1, 1)
            finish(0, 0, True)
            finish(1, 1, True)
            with pool.Fori(0, (NE - 4) // 4) as group:
                for i in range(2, 6):
                    finish(4 * group + i, i % 4, True)
            finish(NE - 2, (NE - 2) % 4, False)
            finish(NE - 1, (NE - 1) % 4, False)
            pool.wait_ge(s_gff, 32)
            for i in range(TT):
                pool.wait_ge(s_fn, i + 1)
                pool.tensor_tensor(fin[:, i, :], fin[:, i, :], bff, ALU.add).then_inc(s_fo, 1)

        @block.scalar
        def _(act):
            link = links(act, s_act)
            a = act.activation

            def sines(layer):
                for j in range(2):
                    act.wait_ge(s_arg, 2 * layer + j + 1)
                    h = slice(HALF * j, HALF * j + HALF)
                    a((h1, h2)[layer][:, h], warg[:, h], ACT.Sin).then_inc(s_sin, 1)

            def in_root(i):
                act.wait_ge(s_st, i + 1)
                a(sd[:, i % 2:i % 2 + 1], mv[:, i % 2, 1:2], ACT.Sqrt, bias=eps).then_inc(s_sd, 1)

            def x_copy(i):
                act.wait_ge(s_xp, i + 1)
                src = bank(4 + 2 * (i % 2), 2)
                for k in range(KT):
                    ins = a(xT[:, k, P * i:P * i + P], src[:, P * k:P * k + P], ACT.Identity,
                            scale=par[:, C_LG + k:C_LG + k + 1], bias=par[:, C_LB + k:C_LB + k + 1])
                ins.then_inc(s_xT, 1)

            act.wait_ge(s_eps, 1)
            for i in range(3):
                in_root(i)
            act.wait_ge(s_parc, 2)
            x_copy(0)
            x_copy(1)
            sines(0)
            in_root(3)
            x_copy(2)
            sines(1)
            in_root(4)
            x_copy(3)
            for i in range(4, TT):
                if i + 1 < TT:
                    in_root(i + 1)
                x_copy(i)

            for jt in range(4):
                act.wait_ge(s_dft, jt + 1)
                if jt:
                    act.wait_ge(s_kf, 4 * jt)
                a(fodd[:, 0, :], bank(4 * (jt % 2) + 1), ACT.Copy).then_inc(s_fodd, 1)
                a(fodd[:, 1, :], bank(4 * (jt % 2) + 3), ACT.Copy).then_inc(s_fodd, 1)

            def hy_copy(m):
                act.wait_ge(s_ut, 2 * m + 1)
                a(g_hy[:, m // 2, :, 0, P * (m % 2):P * (m % 2) + P],
                  bank(4).rearrange("p (i c) -> p i c", i=4), ACT.Copy).then_inc(s_uta, 1)

            act.wait_ge(s_xst, 16 * TT)
            for m in range(N_HY):
                act.wait_ge(s_pj, m + 1)
                y = bank(proj_bank(m), 2)
                for dst, src in ((u_hy[:, m, 0:HALF], y[:, HALF:]), (reverse(m, 0, HALF), y[:, 0:HALF])):
                    ins = a(dst, src, ACT.Identity, scale=par[:, C_HYW + 6 + m:C_HYW + 7 + m], bias=par[:, C_HYB + m:C_HYB + m + 1])
                ins.then_inc(s_pja, 1)
                if m:
                    hy_copy(m - 1)
            hy_copy(N_HY - 1)

            def odd_copies(o):
                for i in range(4):
                    act.wait_ge(s_inv, 4 * o + i + 1)
                    if i or o:
                        act.wait_ge(s_z, 4 * o + i)
                    a(odd, bank(i)[:, HYW:], ACT.Copy).then_inc(s_od, 1)

            def lr_centre(c):
                act.wait_ge(s_pj, I_LR + c + 1)
                a(xr[:, c, :], bank(6, 2), ACT.Identity, scale=par[:, C_LRW + 4 + c:C_LRW + 5 + c],
                  bias=par[:, C_LRB + c:C_LRB + c + 1]).then_inc(s_pja, 1)

            odd_copies(0)
            lr_centre(0)
            odd_copies(1)
            act.wait_ge(s_z, 8)
            for i in range(8):
                link(a(odd, zbuf[:, i // 2, i % 2, :], ACT.Square, accum_out=hss[:, i:i + 1]))
            a(hsd, hss, ACT.Sqrt, scale=1.0 / HYW, bias=eps).then_inc(s_hsd, 1)
            link(a(spt[:, 0, :], par[:, C_LAM:C_LAM + 4], ACT.Abs))
            a(spt[:, 1, :], spt[:, 0, :], ACT.Exp, scale=-1.0).then_inc(s_spa, 1)
            lr_centre(1)
            for c in range(2):
                act.wait_ge(s_pj, I_LG + c + 1)
                a(gelu[:, c, :], bank(proj_bank(I_LG + c), 2), ACT.Gelu_apprx_tanh).then_inc(s_pja, 1)
            for c in range(2):
                act.wait_ge(s_hyT, c + 1)
                a(yT_hy[:, c, HALF:T], bank(2 * c), ACT.Copy)
                a(yT_hy[:, c, HALF - 1::-1], bank(2 * c + 1), ACT.Copy).then_inc(s_hyc, 1)

            def gates(q):
                la_, lx_, lt_ = la[:, q % 2, :], lx[:, q % 2, :], lt[:, q % 2, :]
                if q == 0:
                    act.wait_ge(s_spv, 1)
                if q >= 2:
                    act.wait_ge(s_lv, 2 * (q - 1))
                for j in range(2):
                    act.wait_ge(s_gmm, 2 * q + j + 1)
                    h = slice(HALF * j, HALF * j + HALF)
                    a(lx_[:, h], bank(1), ACT.Sigmoid, bias=par[:, C_BX + q:C_BX + q + 1])
                    a(lt_[:, h], bank(0), ACT.Sigmoid, bias=par[:, C_BA + q:C_BA + q + 1]).then_inc(s_gact, 1)
                act.wait_ge(s_gact, 2 * q + 2)
                a(la_, lt_, ACT.Exp, scale=nsp8[:, q:q + 1])
                a(lt_, lt_, ACT.Tanh, scale=sp8[:, q:q + 1]).then_inc(s_lact, 1)
                act.wait_ge(s_lv, 2 * q + 1)
                a(lt_, lt_, ACT.Sqrt).then_inc(s_lact, 1)

            def squares(i, n):
                act.wait_ge(s_pj, i + 1)
                if n:
                    act.wait_ge(s_ssq, n)
                a(sq, bank(proj_bank(i), 2), ACT.Square).then_inc(s_sq, 1)

            def rms_root(dst, n, k):
                act.wait_ge(s_ssq, n)
                a(dst, bank(2, 2), ACT.Sqrt, scale=1.0 / k, bias=eps).then_inc(s_rsd, 1)

            squares(I_KV, 0)
            gates(0)
            squares(I_KV + 1, 1)
            gates(1)
            rms_root(rb, 2, KVL)
            act.wait_ge(s_pj, I_KR + 1)
            act.wait_ge(s_zero, 2)
            a(kr[DV:DQ, :], bank(proj_bank(I_KR), 2, DV, DQ), ACT.Copy).then_inc(s_pja, 1)
            gates(2)
            squares(I_CQ, 2)
            squares(I_CQ + 1, 3)
            gates(3)
            for c in range(2, 6):
                squares(I_CQ + c, 2 + c)
            act.wait_ge(s_rb, 1)
            rms_root(rb, 8, QL)
            for t in range(TT):
                act.wait_ge(s_vmm, t + 1)
                a(v_at[:, t, :], bank(t % 2), ACT.Copy).then_inc(s_va, 1)
            for c in range(2):
                act.wait_ge(s_hsg, c + 1)
                act.wait_ge(s_ssq, 8 + c)
                a(sq, hs[:, c, :], ACT.Square).then_inc(s_sq, 1)
            rms_root(rb_lru, 10, LRW)

            def heads_copy(u):
                act.wait_ge(s_hp, u + 1)
                kind, i = HEADS[u]
                if kind == "rope":
                    if i:
                        act.wait_ge(s_qro, 1)
                    dst, src = qrope, bank(heads_bank(u), 2)
                else:
                    at = (k_at if kind == "key" else q_at)[i // 2]
                    dst, src = at[0:DV, 2 * i % 4, :], bank(heads_bank(u), 2, 0, DV)
                a(dst, src, ACT.Copy).then_inc(s_hpa, 1)

            def head_high(h, part):
                if h >= 2:
                    act.wait_ge(s_qk, TT * (h - 1))
                if part == 0:
                    a(qs[h % 2][0][0:DQ, :], q_at[h // 4][:, h % 4, :], ACT.Copy).then_inc(s_qkh, 1)
                else:
                    a(ks[h % 2][0][0:DV, :], k_at[h // 4][:, h % 4, :], ACT.Copy).then_inc(s_qkh, 1)

            def rotary_high(slot):
                a(ks[slot][0][DV:DQ, :], kr[DV:DQ, :], ACT.Copy).then_inc(s_qkh, 1)

            def probs_copy(n):
                act.wait_ge(s_tr, 2 * n + 1)
                if n >= 2:
                    act.wait_ge(s_pv, n - 1)
                a(pT[:, n % 2, 0:HALF], bank(4), ACT.Copy).then_inc(s_pta, 1)

            for u in range(len(HEADS)):
                heads_copy(u)
                if u == U_HEAD0:
                    act.wait_ge(s_hpa, U_HEAD0 + 1)
                    act.wait_ge(s_hpv, dve_heads(U_HEAD0))
                    act.wait_ge(s_pj, len(PROJ))
                    act.wait_ge(s_qro, 1)
                    head_high(0, 0)
                    head_high(0, 1)
                    rotary_high(0)
            act.wait_ge(s_hp, len(HEADS))
            act.wait_ge(s_hpa, len(HEADS))
            act.wait_ge(s_hpv, dve_heads(len(HEADS) - 1))
            act.wait_ge(s_qro, 2)
            for n in range(NH * TT):
                h, qt = divmod(n, TT)
                act.wait_ge(s_nm, n + 1)
                if n >= 2:
                    act.wait_ge(s_tr, 2 * (n - 1))
                a(p_at[:, n % 2, :], bank(2 * (n % 2), 2), ACT.Exp, scale=SCALE, bias=nm[:, n % 2:n % 2 + 1],
                  accum_out=rsum[:, n % 4:n % 4 + 1]).then_inc(s_exp, 1)
                if n >= 1:
                    probs_copy(n - 1)
                if n == 0:
                    rotary_high(1)
                if h + 1 < NH and qt in (1, 3):
                    head_high(h + 1, qt // 2)
                if n in WOUT_AT:
                    k = WOUT_AT.index(n)
                    act.wait_ge(s_wo[k % 2], 16 * (k // 2 + 1))
                    a(wout[k][0], wout_in[:, k % 2, :], ACT.Copy, scale=par[:, C_GN + k:C_GN + k + 1]).then_inc(s_woh, 1)
                if n in GROUPS_AT:
                    g, c = divmod(GROUPS_AT.index(n), 2)
                    act.wait_ge(s_qkl, 2 * NH + 2)
                    act.wait_ge(s_rb, 3)
                    a((y_hy, y_lru)[g][0][:, c, :], (yT_hy, hs)[g][:, c, :], ACT.Copy).then_inc(s_yh, 1)
            probs_copy(NH * TT - 1)

            def y_copy(t):
                act.wait_ge(s_oT, t + 1)
                o4 = bank(6 + t % 2).rearrange("p (c t) -> p c t", c=4)
                a(y_at[0][0][:, :, P * t:P * t + P], o4[:, 0:2, :], ACT.Copy)
                a(y_at[1][0][:, :, P * t:P * t + P], o4[:, 2:4, :], ACT.Copy).then_inc(s_yh, 1)

            for t in range(TT + 1):
                if t < TT:
                    act.wait_ge(s_ov, NH * TT - TT + t + 1)
                    link(a(o_sq, o_at[:, t, :], ACT.Square, accum_out=ass[:, t:t + 1]))
                    a(asd[:, t:t + 1], ass[:, t:t + 1], ACT.Sqrt, scale=1.0 / (NH * DV), bias=eps).then_inc(s_osd, 1)
                if t:
                    y_copy(t - 1)

            def router_exp(i):
                act.wait_ge(s_rm, i + 1)
                a(aff[:, i % 4, 32 * (i // 4):32 * (i // 4) + NE], bank(6)[:, NE * (i % 2):NE * (i % 2) + NE], ACT.Exp, bias=rmx[:, i % 2:i % 2 + 1],
                  accum_out=rsm[:, i % 2:i % 2 + 1]).then_inc(s_re, 1)

            for i in range(TT + 2):
                if i < TT:
                    act.wait_ge(s_mst, i + 1)
                    a(sd[:, i % 2:i % 2 + 1], mv[:, i % 2, 1:2], ACT.Sqrt, bias=eps).then_inc(s_msd, 1)
                    act.wait_ge(s_x1, i + 1)
                    if i >= 2:
                        act.wait_ge(s_acst[i % 2], 16 * (i // 2))
                    else:
                        act.wait_ge(s_yl, 2)
                    a(accb[:, i % 2, :], x1t[:, i % 2, :], ACT.Copy, scale=ALPHA).then_inc(s_acc, 1)
                    act.wait_ge(s_acc, i + 1)
                    act.dma_start(acc_tok[:, i, :], accb[:, i % 2, :]).then_inc(s_acst[i % 2], 16)
                if 1 <= i <= TT:
                    act.wait_ge(s_x1p, 2 * i - 1)
                    if i >= 3:
                        act.wait_ge(s_lg, i - 2)
                    a(x1T[(i - 1) % 2][:, 0:HALF], bank(4), ACT.Copy).then_inc(s_x1ta, 1)
                if i >= 2:
                    router_exp(i - 2)

            def high(e, c):
                act.wait_ge(s_wc[c], 16 * e + 16)
                if not (isinstance(e, int) and WC * e + c < WS):
                    act.wait_ge(s_wcu, WC * e + (c + 1 - WS))
                a(flat(wsplit[c % WS][0]), wraw[:, c], ACT.Copy).then_inc(s_whi, 1)

            def turned(dst, b, bank_, event, n, done):
                act.wait_ge(event, n)
                a(flat(dst[0])[:, HALF * b:HALF * b + HALF], bank(bank_), ACT.Copy).then_inc(done, 1)

            def expert(e, slot, first, last):
                for c in range(WC):
                    ahead = c + WS - 1
                    if (ahead < WC or not last) and not (first and slot == 0 and ahead < WS):
                        high(e + ahead // WC, ahead % WC)
                    if c in (1, 5):
                        act.wait_ge(s_wcu, WC * e + (c + 1))
                        a(sil[:, c // 4, :], bank(c // 2), ACT.Silu).then_inc(s_sil, 1)
                    if c in (5, 8):
                        turned(hidT, c // 8, 4, s_ht, 2 * e + c // 8 + 1, s_hta)
                    if c in (7, 9) and not last:
                        turned(xeT, c // 9, 5, s_xep, 2 * e + 2 + c // 9 + 1, s_xea)
                    if c == 10:
                        act.wait_ge(s_wcu, WC * e + 11)
                        if not first:
                            act.wait_ge(s_sc, 16 * e - 16)
                        a(ye[:, slot, 0:HALF], bank(6), ACT.Copy, scale=gate_e[:, slot:slot + 1]).then_inc(s_yea, 1)

            for i in range(2):
                act.wait_ge(s_x1st[i], 16 * TT // 2)
            act.wait_ge(s_lg, TT)
            act.wait_ge(s_mixu, TT)
            act.wait_ge(s_x1, TT)
            for c in range(WS):
                high(0, c)
            act.wait_ge(s_idxc, 1)
            for b in range(2):
                turned(xeT, b, 4 + b, s_xep, b + 1, s_xea)
            expert(0, 0, True, False)
            expert(1, 1, True, False)
            with act.Fori(2, NE - 2, 2) as e:
                expert(e, 0, False, False)
                expert(e + 1, 1, False, False)
            expert(NE - 2, 0, False, False)
            expert(NE - 1, 1, False, True)
            for i in range(TT):
                act.wait_ge(s_fst, i + 1)
                a(sd[:, i % 2:i % 2 + 1], mv[:, i % 2, 1:2], ACT.Sqrt, bias=eps).then_inc(s_fsd, 1)
                act.wait_ge(s_fi, i + 1)
                act.wait_ge(s_fg, i + 1)
                a(fin[:, i, :], fin[:, i, :], ACT.Copy, scale=fin_rstd[:, i:i + 1]).then_inc(s_fn, 1)

        @block.tensor
        def _(pe):
            mm = pe.matmul
            def x_turn(i):
                pe.wait_ge(s_xn, i + 1)
                if i >= 2:
                    pe.wait_ge(s_xT, i - 1)
                for k in range(KT):
                    ins = pe.transpose(bank(4 + 2 * (i % 2), 2)[:, P * k:P * k + P], xr_in[:, i % 3, P * k:P * k + P], ident)
                ins.then_inc(s_xp, 1)

            pe.wait_ge(s_tab, 16)
            x_turn(0)
            x_turn(1)
            pe.wait_ge(s_par, 16 * 20)
            pe.transpose(bank(0)[:, 0:N_PAR], prow, ident[0:N_PAR, 0:N_PAR]).then_inc(s_parT, 1)
            pe.transpose(bank(1, p1=FFN)[:, 0:4], frow, ident[0:4, 0:4]).then_inc(s_parT, 1)
            pe.wait_ge(s_parc, 2)
            for j in range(2):
                mm(bank(j, p1=FFN), w1, pos_t[:, HALF * j:HALF * j + HALF], start=True, stop=True).then_inc(s_fmm, 1)
            x_turn(2)
            for j in range(2):
                pe.wait_ge(s_sin, j + 1)
                mm(bank(j, p1=FFN), w2, h1[:, HALF * j:HALF * j + HALF], start=True, stop=True).then_inc(s_fmm, 1)

            x_turn(3)

            for nt in range(8):
                if nt == 0:
                    pe.wait_ge(s_sin, 4)
                else:
                    pe.wait_ge(s_hw, max(nt - 1, 1))
                for d in range(2):
                    ins = mm(bank(2 * (nt % 2) + d), h2[:, P * nt:P * nt + P], w3[:, HALF * d:HALF * d + HALF], start=True, stop=True)
                ins.then_inc(s_f3, 1)
                if nt + 4 < TT:
                    x_turn(nt + 4)

            pe.wait_ge(s_fmat, 32)
            pe.wait_ge(s_hw, 8)
            pe.wait_ge(s_xT, TT)
            for jt in range(4):
                if jt >= 2:
                    pe.wait_ge(s_kf, 4 * (jt - 1))
                for b, mat, part in ((0, fc, 0), (2, fs, 1), (1, fc, 0), (3, fs, 1)):
                    pe.wait_ge(s_hab, 4 + 4 * (b % 2))
                    for n in range(4):
                        nt = 4 * (b % 2) + n
                        ins = mm(bank(4 * (jt % 2) + b), mat[:, nt, P * jt:P * jt + P], hf[:, nt, part, :], start=(n == 0), stop=(n == 3))
                ins.then_inc(s_dft, 1)

            def project(i):
                c = chunk_of(i)
                c0, w = PROJ[i]
                at = c0 - CHUNKS[c][0]
                p0 = DV if i == I_KR else 0
                pe.wait_ge(s_w[c % 3], 16 * (c // 3 + 1))
                before = proj_before(i)
                if before is not None:
                    pe.wait_ge(*act_read(before))
                    pe.wait_ge(s_pjv, dve_reads(before))
                for k in range(KT):
                    for j in range(2):
                        ins = mm(bank(proj_bank(i) + j, 1, p0, p0 + w), win_w[:, c % 3, k, at:at + w], xT[:, k, HALF * j:HALF * j + HALF],
                                 start=(k == 0), stop=(k == KT - 1))
                ins.then_inc(s_pj, 1)

            def hy_turn(m):
                pe.wait_ge(s_pjv, m + 1)
                for half in range(2):
                    if m:
                        pe.wait_ge((s_uta, s_utv)[half], m)
                    for i in range(4):
                        t0 = HALF * half + P * i
                        ins = pe.transpose(bank(4 + half)[:, P * i:P * i + P], u_hy[:, m, t0:t0 + P], ident)
                    ins.then_inc(s_ut, 1)

            pe.wait_ge(s_kf, 16)
            for m in range(N_HY):
                project(m)
                if m:
                    hy_turn(m - 1)
            hy_turn(N_HY - 1)

            def conv(o):
                if o == 0:
                    pe.wait_ge(s_dmat, 80)
                    pe.wait_ge(s_uta, N_HY)
                    pe.wait_ge(s_utv, N_HY)
                pe.wait_ge(s_fold, o + 1)
                for f in range(9):
                    if f < 8:
                        if f >= 2 or o:
                            pe.wait_ge(s_yf, 8 * o + f - 1 if f >= 2 else 8)
                        for part, mat in enumerate((dc, ds_)):
                            for i in range(4):
                                ins = mm(bank(4 + f % 2)[:, HYW * part:HYW * part + HYW], mat[:, i, P * f:P * f + P], pm[:, part, i, :],
                                         start=(i == 0), stop=(i == 3))
                        ins.then_inc(s_uf, 1)
                    if f:
                        g = f - 1
                        if g == 0 and o:
                            pe.wait_ge(s_z, 4)
                        pe.wait_ge(s_yf, 8 * o + g + 1)
                        for i in range(4):
                            mm(bank(i)[:, 0:HYW], ic[:, g, P * i:P * i + P], yf[:, g % 2, 0:HYW], start=(g == 0), stop=(g == 7), skip_group_check=True)
                            ins = mm(bank(i)[:, HYW:], is_[:, g, P * i:P * i + P], yf[:, g % 2, HYW:], start=False, stop=(g == 7), skip_group_check=True)
                            if g == 7:
                                ins.then_inc(s_inv, 1)
                        if g < 7:
                            ins.then_inc(s_yfu, 1)

            pe.wait_ge(s_pja, N_HY)
            conv(0)
            project(I_LR)
            conv(1)
            pe.wait_ge(s_yf, 16)
            for i in range(I_LR + 1, I_KV):
                project(i)
            pe.wait_ge(s_hyn, 1)
            for c in range(2):
                for half in range(2):
                    for i in range(4):
                        ins = pe.transpose(bank(2 * c + half)[:, P * i:P * i + P], zbuf[:, i, half, P * c:P * c + P], ident)
                ins.then_inc(s_hyT, 1)

            def gates(q):
                d, c = divmod(q, 2)
                if q == 0:
                    pe.wait_ge(s_lw, 16 * 16)
                    pe.wait_ge(s_hyc, 2)
                    pe.wait_ge(s_pjv, dve_reads(I_LR + 1))
                for j in range(2):
                    if 2 * q + j:
                        pe.wait_ge(s_gact, 2 * q + j)
                    for g in range(2):
                        ins = mm(bank(g), lruw[:, 4 * d + 2 * g + c, :], xr[:, c, HALF * j:HALF * j + HALF], start=True, stop=True)
                    ins.then_inc(s_gmm, 1)

            def sum_squares(n, first, last):
                if n == 2 or n == 8:
                    pe.wait_ge(s_rsd, 1 if n == 2 else 2)
                pe.wait_ge(s_sq, n + 1)
                for j in range(2):
                    ins = mm(bank(2 + j), ones, sq[:, HALF * j:HALF * j + HALF], start=first, stop=last)
                ins.then_inc(s_ssq, 1)

            project(I_KV)
            gates(0)
            project(I_KV + 1)
            sum_squares(0, True, False)
            gates(1)
            sum_squares(1, False, True)
            project(I_KR)
            project(I_CQ)
            gates(2)
            pe.wait_ge(s_rope, 48)
            pe.wait_ge(*act_read(I_KR))
            pe.wait_ge(s_gact, 6)
            for j in range(2):
                ins = mm(bank(j), rot, kr[:, HALF * j:HALF * j + HALF], start=True, stop=True)
            ins.then_inc(s_krm, 1)
            project(I_CQ + 1)
            sum_squares(2, True, False)
            pe.wait_ge(s_kro, 1)
            gates(3)
            for c in range(2, 6):
                project(I_CQ + c)
                sum_squares(1 + c, False, False)
            sum_squares(7, False, True)

            pe.wait_ge(s_mw, 16 * 16)
            pe.wait_ge(s_rb, 1)
            pe.wait_ge(s_gact, 8)
            for t in range(TT):
                if t >= 2:
                    pe.wait_ge(s_va, t - 1)
                for k in range(2):
                    ins = mm(bank(t % 2), ckv[:, k, P * t:P * t + P], wv[:, k, :], start=(k == 0), stop=(k == 1))
                ins.then_inc(s_vmm, 1)

            sum_squares(8, True, False)
            sum_squares(9, False, True)

            for u, (kind, i) in enumerate(HEADS):
                if u == 0:
                    pe.wait_ge(*act_read(len(PROJ) - 1))
                    pe.wait_ge(s_pjv, dve_reads(len(PROJ) - 1))
                if u >= 2:
                    pe.wait_ge(s_hpa, u - 1)
                    pe.wait_ge(s_hpv, dve_heads(u - 2))
                if kind == "rope" and i == 0:
                    pe.wait_ge(s_rb, 2)
                w, src, n_k = {"key": (wk, ckv, 2), "query": (wq, cq, 6), "rope": (wqr, cq, 6)}[kind]
                for k in range(n_k):
                    for j in range(2):
                        ins = mm(bank(heads_bank(u) + j), w[:, k, P * i:P * i + P], src[:, k, HALF * j:HALF * j + HALF], start=(k == 0), stop=(k == n_k - 1))
                ins.then_inc(s_hp, 1)
                if u and HEADS[u - 1][0] == "rope":
                    r = HEADS[u - 1][1]
                    pe.wait_ge(s_hpa, u)
                    if r:
                        pe.wait_ge(s_qro, r)
                    else:
                        pe.wait_ge(s_rsd, 3)
                    for j in range(2):
                        ins = mm(bank(2 + j), rot, qrope[:, HALF * j:HALF * j + HALF], start=True, stop=True)
                    ins.then_inc(s_krm, 1)

            def scores(n):
                h, qt = divmod(n, TT)
                if n == 0:
                    pe.wait_ge(s_qro, 2)
                    pe.wait_ge(s_va, TT)
                if qt == 0:
                    pe.wait_ge(s_qkl, 3 if h == 0 else 2 * h + 4)
                if n >= 2:
                    pe.wait_ge(s_exp, n - 1)
                q, k = qs[h % 2], ks[h % 2]
                for j in range(2):
                    out_, qc, kc = bank(2 * (n % 2) + j), slice(P * qt, P * qt + P), slice(HALF * j, HALF * j + HALF)
                    mm(out_, q[0][0:DQ, qc], k[0][0:DQ, kc], start=True, stop=False)
                    mm(out_, q[0][0:DQ, qc], k[1][0:DQ, kc], start=False, stop=False)
                    ins = mm(out_, q[1][0:DQ, qc], k[0][0:DQ, kc], start=False, stop=True)
                ins.then_inc(s_qk, 1)

            def probs_turn(n):
                pe.wait_ge(s_exp, n + 1)
                if n == 0:
                    pe.wait_ge(s_hpa, len(HEADS))
                    pe.wait_ge(s_hpv, dve_heads(len(HEADS) - 1))
                for b in range(2):
                    if n:
                        pe.wait_ge((s_pta, s_ptv)[b], n)
                    for k in range(4):
                        ins = pe.transpose(bank(4 + b)[:, P * k:P * k + P], p_at[:, n % 2, HALF * b + P * k:HALF * b + P * k + P], ident)
                    ins.then_inc(s_tr, 1)

            def pv(n):
                h = n // TT
                pe.wait_ge(s_pta, n + 1)
                pe.wait_ge(s_ptv, n + 1)
                if n:
                    pe.wait_ge(s_ov, n)
                for k in range(KT):
                    ins = mm(bank(7)[:, DV * (n % 2):DV * (n % 2) + DV], pT[:, n % 2, P * k:P * k + P], v_at[:, k, DV * h:DV * h + DV],
                             start=(k == 0), stop=(k == KT - 1))
                ins.then_inc(s_pv, 1)

            scores(0)
            N = NH * TT
            for n in range(N):
                h, qt = divmod(n, TT)
                if n + 1 < N:
                    scores(n + 1)
                probs_turn(n)
                if n:
                    pv(n - 1)
            pv(N - 1)

            def y_turn(t):
                pe.wait_ge(s_on, t + 1)
                if t >= 2:
                    pe.wait_ge(s_yl, 4 + t - 1)
                for c in range(4):
                    ins = pe.transpose(bank(6 + t % 2)[:, P * c:P * c + P], o_at[:, t, P * c:P * c + P], ident)
                ins.then_inc(s_oT, 1)

            def x1_turn(i):
                pe.wait_ge(s_x1, i + 1)
                for b in range(2):
                    if i:
                        pe.wait_ge((s_x1ta, s_x1tv)[b], i)
                    for k in range(4):
                        ins = pe.transpose(bank(4 + b)[:, P * k:P * k + P], x1t[:, i % 2, HALF * b + P * k:HALF * b + P * k + P], ident)
                    ins.then_inc(s_x1p, 1)

            def logits(i):
                pe.wait_ge(s_x1ta, i + 1)
                pe.wait_ge(s_x1tv, i + 1)
                if i == 0:
                    pe.wait_ge(s_rw, 16)
                if i:
                    pe.wait_ge(s_re, i)
                for k in range(KT):
                    ins = mm(bank(6)[:, NE * (i % 2):NE * (i % 2) + NE], x1T[i % 2][:, P * k:P * k + P], rw[:, k, :], start=(k == 0), stop=(k == KT - 1))
                ins.then_inc(s_lg, 1)

            pe.wait_ge(s_wol, KT)
            y = [(group[0][:, c, :], group[1][:, c, :]) for group in (y_hy, y_lru, *y_at) for c in range(2)]
            for i in range(TT + 2):
                if i < 2:
                    for t in range(4 * i, 4 * i + 4):
                        y_turn(t)
                if i < TT:
                    pe.wait_ge(s_yl, 4 + i + 1)
                    if i >= 2:
                        pe.wait_ge(s_mixu, i - 1)
                    for k in range(KT):
                        high, low = y[k][0][:, P * i:P * i + P], y[k][1][:, P * i:P * i + P]
                        for j in range(2):
                            out_, cols = bank(2 * (i % 2) + j), slice(HALF * j, HALF * j + HALF)
                            mm(out_, high, wout[k][0][:, cols], start=(k == 0), stop=False)
                            mm(out_, high, wout[k][1][:, cols], start=False, stop=False)
                            ins = mm(out_, low, wout[k][0][:, cols], start=False, stop=(k == KT - 1))
                    ins.then_inc(s_mix, 1)
                if 1 <= i <= TT:
                    x1_turn(i - 1)
                if 2 <= i <= TT + 1:
                    logits(i - 2)
            pe.wait_ge(s_aff, TT)
            for i in range(4):
                ins = pe.transpose(bank(7, p1=NE2)[:, P * i:P * i + P], aff[:, i, :], ident)
            ins.then_inc(s_afT, 1)
            pe.wait_ge(s_topk, 1)
            for i in range(4):
                ins = pe.transpose(bank(4)[:, NE2 * i:NE2 * i + NE2], best[:, i, :], ident[0:NE2, 0:NE2])
            ins.then_inc(s_idxp, 1)

            def xe_turn(e, slot, b, bank_):
                if b == 0:
                    pe.wait_ge(s_xe[slot], 16 if isinstance(e, int) and e < 2 else 8 * e + (16 if slot == 0 else 8))
                for k in range(4):
                    ins = pe.transpose(bank(bank_)[:, P * k:P * k + P], xe[:, slot, HALF * b + P * k:HALF * b + P * k + P], ident)
                ins.then_inc(s_xep, 1)

            def hid_turn(e, b):
                if b:
                    pe.wait_ge(s_htv, 2 * e + 1)
                pe.wait_ge(s_hid, 2 * e + b + 1)
                for k in range(4):
                    ins = pe.transpose(bank(4)[:, P * k:P * k + P], hid[:, HALF * b + P * k:HALF * b + P * k + P], ident)
                ins.then_inc(s_ht, 1)

            def expert(e, slot, last):
                zero = isinstance(e, int) and e == 0
                for c in range(WC):
                    if c < 8:
                        out_bank, src, k0 = c // 2, xeT, 4 * (c % 2)
                    else:
                        out_bank, src, k0 = 6 + c % 2, hidT, 4 * ((c - 8) // 2)
                    if c == 0:
                        pe.wait_ge(s_xev, 2 * e + 2)
                    if c in (0, 2, 4, 6) and not zero:
                        pe.wait_ge(s_hid, 2 * e + c // 4 - 1)
                    if c in (8, 10):
                        pe.wait_ge(s_htv, 2 * e + c // 10 + 1)
                    if c in (8, 9) and not zero:
                        pe.wait_ge((s_yea, s_yev)[c - 8], e)
                    pe.wait_ge(s_wlo, WC * e + (c + 1))
                    whi, wlo = wsplit[c % WS][0:2]
                    first, last_k = k0 == 0, k0 + 3
                    for k in range(k0, k0 + 4):
                        mm(bank(out_bank), src[0][:, k, :], whi[:, k % 4, :], start=(k == 0), stop=False)
                        mm(bank(out_bank), src[0][:, k, :], wlo[:, k % 4, :], start=False, stop=False)
                        ins = mm(bank(out_bank), src[1][:, k, :], whi[:, k % 4, :], start=False, stop=(k == KT - 1))
                    ins.then_inc(s_wcu, 1)
                    if c == 5:
                        hid_turn(e, 0)
                    if c == 8:
                        hid_turn(e, 1)
                    if c == 7 and not last:
                        if zero:
                            pe.wait_ge(s_xev, 2)
                        xe_turn(e + 1, 1 - slot, 0, 5)
                    if c == 9 and not last:
                        pe.wait_ge(s_xev, 2 * e + 3)
                        xe_turn(e + 1, 1 - slot, 1, 5)

            pe.wait_ge(s_idxc, 1)
            xe_turn(0, 0, 0, 4)
            xe_turn(0, 0, 1, 5)
            expert(0, 0, False)
            expert(1, 1, False)
            with pe.Fori(2, NE - 2, 2) as e:
                expert(e, 0, False)
                expert(e + 1, 1, False)
            expert(NE - 2, 0, False)
            expert(NE - 1, 1, True)

        @block.vector
        def _(v):
            link = links(v, s_dve)
            stt, tt, ts = v.scalar_tensor_tensor, v.tensor_tensor, v.tensor_scalar

            def sine_args(layer):
                for j in range(2):
                    w, n = warg[:, HALF * j:HALF * j + HALF], turns[:, HALF * j:HALF * j + HALF]
                    v.wait_ge(s_fmm, 2 * layer + j + 1)
                    link(ts(w, bank(j, p1=FFN), fpar[:, 2 * layer:2 * layer + 1], fpar[:, 2 * layer + 1:2 * layer + 2], ALU.add, ALU.mult))
                    link(ts(n, w, 1.0 / (2.0 * np.pi), MAGIC, ALU.mult, ALU.add))
                    link(ts(n, n, MAGIC, None, ALU.subtract))
                    link(stt(w, n, -TWO_PI_HI, w, ALU.mult, ALU.add))
                    link(stt(w, n, -TWO_PI_LO, w, ALU.mult, ALU.add))
                    ts(w, w, PI_IN, -PI_IN, ALU.min, ALU.max).then_inc(s_arg, 1)

            def stats(x, st_, mv_):
                v.bn_stats(st_[:, 0:6], x[:, 0:HALF])
                link(v.bn_stats(st_[:, 6:12], x[:, HALF:D]))
                return v.bn_aggr(mv_, st_)

            def norm_rows(x, root, inv, mv_):
                link(v.reciprocal(inv, root))
                return ts(x, x, mv_[:, 0:1], inv, ALU.subtract, ALU.mult)

            def in_norm(i):
                v.wait_ge(s_x[i % 3], 16 * (i // 3 + 1))
                x, b = xr_in[:, i % 3, :], i % 2
                stats(x, st[:, b, :], mv[:, b, :]).then_inc(s_st, 1)
                v.wait_ge(s_sd, i + 1)
                norm_rows(x, sd[:, b:b + 1], rstd[:, b:b + 1], mv[:, b, :]).then_inc(s_xn, 1)

            for i in range(3):
                in_norm(i)
            v.wait_ge(s_parT, 2)
            v.tensor_copy(par[:, 0:N_PAR], bank(0)[:, 0:N_PAR]).then_inc(s_parc, 1)
            v.tensor_copy(fpar, bank(1, p1=FFN)[:, 0:4]).then_inc(s_parc, 1)
            v.wait_ge(s_parc, 2)
            sine_args(0)
            in_norm(3)
            sine_args(1)
            in_norm(4)
            v.wait_ge(s_wint, 16)
            for nt in range(8):
                if nt + 5 < TT:
                    in_norm(nt + 5)
                v.wait_ge(s_f3, nt + 1)
                if nt >= 2:
                    v.wait_ge(s_hab, nt - 1)
                tt(hw[:, nt % 2, :].rearrange("p (a c) -> p a c", a=4), bank(2 * (nt % 2), 2).rearrange("p (a c) -> p a c", a=4),
                   win[:, nt, :].unsqueeze(1).to_broadcast([P, 4, HYW]), ALU.mult).then_inc(s_hw, 1)

            def by_order(ap):
                return ap.rearrange("p (o c) -> p o c", o=2)

            for jt in range(4):
                b0 = 4 * (jt % 2)
                v.wait_ge(s_fodd, 2 * jt + 2)
                for part in range(2):
                    even, oddp = by_order(bank(b0 + 2 * part)), by_order(fodd[:, part, :])
                    tt(kf[:, :, jt, part, :], even, oddp, ALU.add).then_inc(s_kf, 1)
                    if part == 0:
                        tt(kf[:, :, 4 + jt, part, :], even, oddp, ALU.subtract).then_inc(s_kf, 1)
                    else:
                        tt(kf[:, :, 4 + jt, part, :], oddp, even, ALU.subtract).then_inc(s_kf, 1)

            def hy_copy(m):
                v.wait_ge(s_ut, 2 * m + 2)
                v.tensor_copy(g_hy[:, m // 2, :, 1, P * (m % 2):P * (m % 2) + P], bank(5).rearrange("p (i c) -> p i c", i=4)).then_inc(s_utv, 1)

            v.wait_ge(s_xst, 16 * TT)
            for m in range(N_HY):
                v.wait_ge(s_pja, m + 1)
                u, y = u_hy[:, m, :], bank(proj_bank(m), 2)
                w0, w2 = par[:, C_HYW + m:C_HYW + m + 1], par[:, C_HYW + 12 + m:C_HYW + 13 + m]
                lo = reverse(m, 1, HALF)
                stt(u[:, 0:HALF], y[:, HALF - 1:T - 1], w0, u[:, 0:HALF], ALU.mult, ALU.add)
                link(stt(lo, y[:, 0:HALF - 1], w0, lo, ALU.mult, ALU.add))
                lo = reverse(m, 0, HALF)
                stt(u[:, 0:HALF - 1], y[:, HALF + 1:], w2, u[:, 0:HALF - 1], ALU.mult, ALU.add)
                stt(lo, y[:, 1:HALF + 1], w2, lo, ALU.mult, ALU.add).then_inc(s_pjv, 1)
                if m:
                    hy_copy(m - 1)
            hy_copy(N_HY - 1)

            def lr_taps(c):
                v.wait_ge(s_pja, I_LR + c + 1)
                x, y = xr[:, c, :], bank(6, 2)
                w = [par[:, C_LRW + 2 * k + c:C_LRW + 2 * k + c + 1] for k in range(4)]
                link(stt(x[:, 2:], y[:, 0:T - 2], w[0], x[:, 2:], ALU.mult, ALU.add))
                link(stt(x[:, 1:], y[:, 0:T - 1], w[1], x[:, 1:], ALU.mult, ALU.add))
                stt(x[:, 0:T - 1], y[:, 1:], w[3], x[:, 0:T - 1], ALU.mult, ALU.add).then_inc(s_pjv, 1)

            def conv(o, z):
                tt(pm[:, 0], z[:, :, 0, :], z[:, :, 1, :], ALU.add)
                tt(pm[:, 1], z[:, :, 0, :], z[:, :, 1, :], ALU.subtract).then_inc(s_fold, 1)
                tt(tsk.rearrange("p i h c -> p (i h) c"), z.rearrange("p i h c -> p (i h) c"),
                   skipb[:, o, :].unsqueeze(1).to_broadcast([P, 8, HYW]), ALU.mult)
                for f in range(8):
                    v.wait_ge(s_uf, 8 * o + f + 1)
                    kc, ks = kf[:, o, f, 0, :], kf[:, o, f, 1, :]
                    u = bank(4 + f % 2)
                    if f or o:
                        v.wait_ge(s_yf, 8 * o + f)
                    tt(by_order(t1), by_order(u), kc.unsqueeze(1).to_broadcast([P, 2, HYW]), ALU.mult)
                    tt(t2[:, 0:HYW], u[:, HYW:], ks, ALU.mult)
                    link(tt(t2[:, HYW:], u[:, 0:HYW], ks, ALU.mult))
                    if f >= 2:
                        v.wait_ge(s_yfu, 7 * o + f - 1)
                    elif o:
                        v.wait_ge(s_inv, 4)
                    y = yf[:, f % 2, :]
                    tt(y[:, 0:HYW], t1[:, 0:HYW], t2[:, 0:HYW], ALU.subtract)
                    tt(y[:, HYW:], t1[:, HYW:], t2[:, HYW:], ALU.add).then_inc(s_yf, 1)
                    if o and f == 2:
                        lr_taps(0)
                for i in range(4):
                    s = tsk[:, i]
                    v.wait_ge(s_od, 4 * o + i + 1)
                    link(tt(s, s, bank(i)[:, 0:HYW].unsqueeze(1).to_broadcast([P, 2, HYW]), ALU.add))
                    tt(s[:, 0, :], s[:, 0, :], odd, ALU.add)
                    link(tt(s[:, 1, :], s[:, 1, :], odd, ALU.subtract))
                    tt(zbuf[:, i], s, g_hy[:, o, i], ALU.mult).then_inc(s_z, 1)

            v.wait_ge(s_dmat, 80)
            v.wait_ge(s_pj, N_HY)
            v.wait_ge(s_uta, N_HY)
            v.wait_ge(s_utv, N_HY)
            conv(0, g_hy[:, 2])
            v.wait_ge(s_z, 4)
            conv(1, zbuf)
            v.wait_ge(s_z, 8)
            v.wait_ge(s_hsd, 1)
            link(v.reciprocal(hrs, hsd))
            for i in range(8):
                zz = zbuf[:, i // 2, i % 2, :]
                ins = ts(zz, zz, hrs[:, i:i + 1], None, ALU.mult)
            ins.then_inc(s_hyn, 1)
            v.wait_ge(s_spa, 1)
            e_, r_, s2, q_ = spt[:, 1, :], spt[:, 2, :], spt[:, 3, :], spt[:, 4, :]
            link(ts(r_, e_, 2.0, None, ALU.add))
            link(v.reciprocal(r_, r_))
            link(tt(r_, r_, e_, ALU.mult))
            link(tt(s2, r_, r_, ALU.mult))
            link(ts(q_, s2, 1.0 / 19, 1.0 / 17, ALU.mult, ALU.add))
            for k in (15, 13, 11, 9, 7, 5, 3, 1):
                link(tt(q_, q_, s2, ALU.mult))
                link(ts(q_, q_, 1.0 / k, None, ALU.add))
            link(tt(q_, q_, r_, ALU.mult))
            link(ts(r_, par[:, C_LAM:C_LAM + 4], -1.0, 0.0, ALU.mult, ALU.max))
            link(stt(q_, q_, 2.0, r_, ALU.mult, ALU.add))
            ts(sp8, q_, LRU_C, None, ALU.mult)
            ts(nsp8, q_, -LRU_C, None, ALU.mult).then_inc(s_spv, 1)
            lr_taps(1)

            def scan(q):
                d, c = divmod(q, 2)
                la_, lx_, lt_ = la[:, q % 2, :], lx[:, q % 2, :], lt[:, q % 2, :]
                v.wait_ge(s_lact, 2 * q + 1)
                link(tt(ld, la_, la_, ALU.mult))
                stt(lt_, ld, 1.0, lt_, ALU.add, ALU.mult).then_inc(s_lv, 1)
                link(tt(lx_, lx_, xr[:, c, :], ALU.mult))
                v.wait_ge(s_lact, 2 * q + 2)
                link(tt(lx_, lx_, lt_, ALU.mult))
                if d == 0:
                    v.tensor_tensor_scan(hs[:, c, :], la_, lx_, 0.0, ALU.mult, ALU.add).then_inc(s_lv, 1)
                else:
                    link(v.tensor_tensor_scan(ld[:, ::-1], la_[:, ::-1], lx_[:, ::-1], 0.0, ALU.mult, ALU.add))
                    v.wait_ge(s_lv, 2 * c + 2)
                    tt(hs[:, c, :], hs[:, c, :], ld, ALU.add).then_inc(s_lv, 1)
                    v.wait_ge(s_lv, 2 * q + 2)
                    tt(hs[:, c, :], hs[:, c, :], gelu[:, c, :], ALU.mult).then_inc(s_hsg, 1)

            def latent(i, dst, gcol):
                v.wait_ge(*act_read(i))
                ts(dst, bank(proj_bank(i), 2), gcol, None, ALU.mult).then_inc(s_pjv, 1)

            latent(I_KV, ckv[:, 0, :], par[:, C_KVG:C_KVG + 1])
            scan(0)
            latent(I_KV + 1, ckv[:, 1, :], par[:, C_KVG + 1:C_KVG + 2])
            scan(1)
            v.wait_ge(s_rsd, 1)
            link(v.reciprocal(rb, rb))
            for c in range(2):
                ins = tt(ckv[:, c, :], ckv[:, c, :], rb, ALU.mult)
            ins.then_inc(s_rb, 1)
            v.wait_ge(s_rope, 48)
            v.wait_ge(s_krm, 1)
            tt(rtmp_k[DV:DQ, :], bank(0, 2, DV, DQ), sin_t[DV:DQ, :], ALU.mult)
            link(tt(kr[DV:DQ, :], kr[DV:DQ, :], cos_t[DV:DQ, :], ALU.mult))
            tt(kr[DV:DQ, :], kr[DV:DQ, :], rtmp_k[DV:DQ, :], ALU.add).then_inc(s_kro, 1)
            v.wait_ge(s_kro, 1)
            scan(2)
            for c in range(6):
                latent(I_CQ + c, cq[:, c, :], par[:, C_QG + c:C_QG + c + 1])
                if c == 1:
                    scan(3)
            v.wait_ge(s_rsd, 2)
            link(v.reciprocal(rb, rb))
            for c in range(6):
                ins = tt(cq[:, c, :], cq[:, c, :], rb, ALU.mult)
            ins.then_inc(s_rb, 1)

            def heads_copy(u):
                kind, i = HEADS[u]
                at = (k_at if kind == "key" else q_at)[i // 2]
                v.wait_ge(s_hp, u + 1)
                v.tensor_copy(at[0:DV, (2 * i + 1) % 4, :], bank(heads_bank(u), 2, DV, P)).then_inc(s_hpv, 1)

            def rope(i):
                v.wait_ge(s_krm, 2 + i)
                tt(rtmp, bank(2, 2), sin_t, ALU.mult)
                link(tt(qrope, qrope, cos_t, ALU.mult))
                for h in range(4):
                    rows_ = slice(DR * h, DR * h + DR)
                    ins = tt(q_at[i][DV:DQ, h, :], qrope[rows_, :], rtmp[rows_, :], ALU.add)
                ins.then_inc(s_qro, 1)

            def head_low(h, part):
                v.wait_ge(s_qkh, (1 if h == 0 else 2 * h + 3) + part)
                if part == 0:
                    _, lo, hi = qs[h % 2]
                    tt(lo[0:DQ, :], q_at[h // 4][:, h % 4, :], hi[0:DQ, :], ALU.subtract).then_inc(s_qkl, 1)
                else:
                    _, lo, hi = ks[h % 2]
                    tt(lo[0:DV, :], k_at[h // 4][:, h % 4, :], hi[0:DV, :], ALU.subtract).then_inc(s_qkl, 1)

            def rotary_low(slot):
                v.wait_ge(s_qkh, 3 + slot)
                _, lo, hi = ks[slot]
                tt(lo[DV:DQ, :], kr[DV:DQ, :], hi[DV:DQ, :], ALU.subtract).then_inc(s_qkl, 1)

            for u, (kind, i) in enumerate(HEADS):
                if kind != "rope":
                    heads_copy(u)
                if u and HEADS[u - 1][0] == "rope":
                    rope(HEADS[u - 1][1])
                if u == len(HEADS) - 2:
                    v.wait_ge(s_rsd, 3)
                    link(v.reciprocal(rb_lru, rb_lru))
                    for c in range(2):
                        ins = tt(hs[:, c, :], hs[:, c, :], rb_lru, ALU.mult)
                    ins.then_inc(s_rb, 1)
                if u == U_HEAD0 + 1:
                    head_low(0, 0)
                    head_low(0, 1)
                    rotary_low(0)

            def row_max(n):
                v.wait_ge(s_qk, n + 1)
                link(v.tensor_reduce(mx[:, n % 2:n % 2 + 1], bank(2 * (n % 2), 2), AX.X, ALU.max))
                ts(nm[:, n % 2:n % 2 + 1], mx[:, n % 2:n % 2 + 1], -SCALE, None, ALU.mult).then_inc(s_nm, 1)

            def probs_copy(n):
                v.wait_ge(s_tr, 2 * n + 2)
                if n >= 2:
                    v.wait_ge(s_pv, n - 1)
                v.tensor_copy(pT[:, n % 2, HALF:], bank(5)).then_inc(s_ptv, 1)

            def output(n):
                h, qt = divmod(n, TT)
                v.wait_ge(s_pv, n + 1)
                link(v.reciprocal(rinv[:, n % 2:n % 2 + 1], rsum[:, n % 4:n % 4 + 1]))
                ts(o_at[:, qt, DV * h:DV * h + DV], bank(7)[:, DV * (n % 2):DV * (n % 2) + DV], rinv[:, n % 2:n % 2 + 1], None, ALU.mult).then_inc(s_ov, 1)

            N = NH * TT
            for n in range(N):
                h, qt = divmod(n, TT)
                row_max(n)
                if n >= 1:
                    probs_copy(n - 1)
                if n >= 2:
                    output(n - 2)
                if n == 0:
                    rotary_low(1)
                if h + 1 < NH and qt in (2, 4):
                    head_low(h + 1, qt // 2 - 1)
                if n in WOUT_AT:
                    k = WOUT_AT.index(n)
                    _, lo, hi = wout[k]
                    v.wait_ge(s_woh, k + 1)
                    stt(lo, wout_in[:, k % 2, :], par[:, C_GN + k:C_GN + k + 1], hi, ALU.mult, ALU.subtract).then_inc(s_wol, 1)
                if n in GROUPS_AT:
                    g, c = divmod(GROUPS_AT.index(n), 2)
                    _, lo, hi = (y_hy, y_lru)[g]
                    v.wait_ge(s_yh, 2 * g + c + 1)
                    tt(lo[:, c, :], (yT_hy, hs)[g][:, c, :], hi[:, c, :], ALU.subtract).then_inc(s_yl, 1)
            probs_copy(N - 1)
            output(N - 2)
            output(N - 1)
            def y_copy(t):
                v.wait_ge(s_yh, 4 + t + 1)
                o4 = bank(6 + t % 2).rearrange("p (c t) -> p c t", c=4)
                for half, (_, lo, hi) in enumerate(y_at):
                    ins = tt(lo[:, :, P * t:P * t + P], o4[:, 2 * half:2 * half + 2, :], hi[:, :, P * t:P * t + P], ALU.subtract)
                ins.then_inc(s_yl, 1)

            for t in range(TT + 1):
                if t < TT:
                    v.wait_ge(s_osd, t + 1)
                    link(v.reciprocal(ars[:, t:t + 1], asd[:, t:t + 1]))
                    ts(o_at[:, t, :], o_at[:, t, :], ars[:, t:t + 1], None, ALU.mult).then_inc(s_on, 1)
                if t:
                    y_copy(t - 1)

            def router(i):
                b, b1 = i % 2, i % 2 + 1
                lgt = bank(6)[:, NE * b:NE * b + NE]
                v.wait_ge(s_lg, i + 1)
                v.tensor_reduce(rmx[:, b:b1], lgt, AX.X, ALU.max, negate=True).then_inc(s_rm, 1)
                v.wait_ge(s_re, i + 1)
                link(v.reciprocal(rri[:, b:b1], rsm[:, b:b1]))
                e_ = aff[:, i % 4, 32 * (i // 4):32 * (i // 4) + NE]
                ts(e_, e_, rri[:, b:b1], None, ALU.mult).then_inc(s_aff, 1)

            link(v.memset(aff, 0.0))
            for i in range(TT + 2):
                if i < TT:
                    b = i % 2
                    x = x1t[:, b, :]
                    v.wait_ge(s_mix, i + 1)
                    v.wait_ge(s_res, i + 1)
                    if i >= 2:
                        v.wait_ge(s_x1st[b], 16 * (i // 2))
                        v.wait_ge(s_acc, i - 1)
                        v.wait_ge(s_x1p, 2 * (i - 1))
                    stt(x, xres[:, b, :], ALPHA, bank(2 * b, 2), ALU.mult, ALU.add).then_inc(s_mixu, 1)
                    v.wait_ge(s_mixu, i + 1)
                    stats(x, st[:, b, :], mv[:, b, :]).then_inc(s_mst, 1)
                    v.wait_ge(s_msd, i + 1)
                    link(v.reciprocal(rstd[:, b:b + 1], sd[:, b:b + 1]))
                    link(stt(x, x, mv[:, b, 0:1], gmix, ALU.subtract, ALU.mult))
                    stt(x, x, rstd[:, b:b + 1], bmix, ALU.mult, ALU.add).then_inc(s_x1, 1)
                if 1 <= i <= TT:
                    v.wait_ge(s_x1p, 2 * i)
                    if i >= 3:
                        v.wait_ge(s_lg, i - 2)
                    v.tensor_copy(x1T[(i - 1) % 2][:, HALF:], bank(5)).then_inc(s_x1tv, 1)
                if i >= 2:
                    router(i - 2)

            v.wait_ge(s_afT, 1)
            v.wait_ge(s_acst[0], 16 * TT // 2)
            v.wait_ge(s_acst[1], 16 * TT // 2)
            link(v.tensor_copy(affT, bank(7, p1=NE2)))
            for r in range(CAP // 8):
                top = best[:, 0, 8 * r:8 * r + 8]
                link(v.max(top, affT))
                link(v.max_index(idxs[:, 8 * r:8 * r + 8], top, affT))
                if r + 1 < CAP // 8:
                    link(v.match_replace(affT, top, affT, -1.0))
            link(v.tensor_copy(best[:, 1, :], idxs))
            for i in range(2):
                ins = v.tensor_copy(best[:, 2 + i, ::-1], best[:, i, :])
            ins.then_inc(s_topk, 1)
            v.wait_ge(s_idxp, 1)
            b4 = bank(4)[:, 0:4 * NE2].rearrange("p (i e) -> p i e", i=4)
            lo_a, lo_i = b4[:, 0, 0:NE], b4[:, 1, 0:NE]
            link(v.tensor_copy(pick[:, 0:2, :], b4[:, 2:4, 32:32 + NE]))
            hi_a, hi_i, first = pick[:, 0, :], pick[:, 1, :], pick[:, 2, :]
            link(ts(hi_i, hi_i, float(T // 2), None, ALU.add))
            tt(first, lo_a, hi_a, ALU.is_ge)
            link(tt(gate_t, lo_a, hi_a, ALU.max))
            link(tt(hi_a, lo_i, hi_i, ALU.subtract))
            link(tt(hi_a, hi_a, first, ALU.mult))
            tt(idx_t, hi_a, hi_i, ALU.add).then_inc(s_idxc, 1)

            def low(e, c):
                v.wait_ge(s_whi, WC * e + (c + 1))
                _, lo, hi = wsplit[c % WS]
                tt(flat(lo), wraw[:, c], flat(hi), ALU.subtract).then_inc(s_wlo, 1)

            def turned(dst, b, bank_, high_done, n, done):
                v.wait_ge(high_done, n)
                h = slice(HALF * b, HALF * b + HALF)
                tt(flat(dst[1])[:, h], bank(bank_), flat(dst[2])[:, h], ALU.subtract).then_inc(done, 1)

            def expert(e, slot, first, last):
                for c in range(WC):
                    ahead = c + WS - 1
                    if (ahead < WC or not last) and not (first and slot == 0 and ahead < WS):
                        low(e + ahead // WC, ahead % WC)
                    if c in (3, 7):
                        f = c // 4
                        v.wait_ge(s_sil, 2 * e + f + 1)
                        v.wait_ge(s_wcu, WC * e + (c + 1))
                        tt(hid[:, HALF * f:HALF * f + HALF], sil[:, f, :], bank(c // 2), ALU.mult).then_inc(s_hid, 1)
                    if c in (5, 8):
                        turned(hidT, c // 8, 4, s_hta, 2 * e + c // 8 + 1, s_htv)
                    if c in (7, 9) and not last:
                        turned(xeT, c // 9, 5, s_xea, 2 * e + 2 + c // 9 + 1, s_xev)
                    if c == 11:
                        v.wait_ge(s_wcu, WC * e + WC)
                        if not first:
                            v.wait_ge(s_sc, 16 * e - 16)
                        ts(ye[:, slot, HALF:], bank(7), gate_e[:, slot:slot + 1], None, ALU.mult).then_inc(s_yev, 1)

            v.wait_ge(s_wlo, WS)
            for b in range(2):
                turned(xeT, b, 4 + b, s_xea, b + 1, s_xev)
            expert(0, 0, True, False)
            expert(1, 1, True, False)
            with v.Fori(2, NE - 2, 2) as e:
                expert(e, 0, False, False)
                expert(e + 1, 1, False, False)
            expert(NE - 2, 0, False, False)
            expert(NE - 1, 1, False, True)

            v.wait_ge(s_gff, 32)
            for i in range(TT):
                x, b = fin[:, i, :], i % 2
                v.wait_ge(s_fx[i], 16 * NE + 16)
                stats(x, st[:, b, :], mv[:, b, :]).then_inc(s_fst, 1)
                v.wait_ge(s_fst, i + 1)
                stt(x, x, mv[:, b, 0:1], gff, ALU.subtract, ALU.mult).then_inc(s_fg, 1)
                v.wait_ge(s_fsd, i + 1)
                v.reciprocal(fin_rstd[:, i:i + 1], sd[:, b:b + 1]).then_inc(s_fi, 1)


_INS = ["x", "ln_in_g", "ln_in_b", "w_in", "hy_conv_w", "hy_conv_b", "hy_ffn_w1", "hy_ffn_b1", "hy_sin_f1",
        "hy_ffn_w2", "hy_ffn_b2", "hy_sin_f2", "hy_ffn_w3", "hy_skip", "lru_conv_w", "lru_conv_b", "lru_wa", "lru_ba",
        "lru_wx", "lru_bx", "lru_lambda", "mla_q_norm_g", "mla_w_uq", "mla_kv_norm_g", "mla_w_ukv", "group_norm_g",
        "w_out", "ln_mix_g", "ln_mix_b", "router_w", "exp_w_gate", "exp_w_up", "exp_w_down", "ln_ffn_g", "ln_ffn_b"]


def kernel(**inputs):
    import numpy as _np
    import concourse.bacc as _bacc
    from concourse import mybir as _mybir
    from concourse.bass_utils import run_bass_kernel_spmd as _run

    nc = _bacc.Bacc("TRN2", target_bir_lowering=False, num_devices=1)
    given = {name: _np.ascontiguousarray(inputs[name]) for name in _INS}
    given.update(shape_constants())
    arrays = {f"in_{name}": a for name, a in given.items()}
    aps = {name: nc.dram_tensor(f"in_{name}", a.shape, _mybir.dt.from_np(a.dtype), kind="ExternalInput").ap()
           for name, a in given.items()}
    out = nc.dram_tensor("out_0", (1, T, D), F32, kind="ExternalOutput").ap()
    encoder(nc, aps, out)
    r = _run(nc, [arrays], core_ids=[0])
    return r.results[0]["out_0"]
```
